# Optimizing a Trainium2 kernel written in Bass

```python
import jax, jax.numpy as jnp
from jax import lax
import numpy as np

D_MODEL = 1024
BATCH = 1
SEQ = 512
DEPTH = 1

HG_HEADS = 4
HG_KDIM = 128
HG_VDIM = 128
HG_WIDTH = HG_HEADS * HG_KDIM
HG_CHUNK = 64
ATT_GROUPS = ((128, 1), (512, 4), (2048, 16))
ATT_HEADS_PER_GROUP = 4
ATT_HEAD_DIM = 128
N_ATT_HEADS = ATT_HEADS_PER_GROUP * len(ATT_GROUPS)
ATT_QKV_WIDTH = N_ATT_HEADS * ATT_HEAD_DIM
ATT_WIDTH = ATT_HEADS_PER_GROUP * ATT_HEAD_DIM
ATT_BLOCK = 128
ALIBI_MAX = 8.0
COL_WIDTHS = (HG_WIDTH, HG_WIDTH, HG_HEADS * HG_VDIM, HG_HEADS * HG_VDIM,
              ATT_QKV_WIDTH, ATT_QKV_WIDTH, ATT_QKV_WIDTH, D_MODEL, D_MODEL)
IN_COLS = sum(COL_WIDTHS)
D_FF = 2816
CONV_W = 3
N_MOD = 6
EPS = 1e-6

kernel_name = "hybrid_hgrn2_dilated_attn_convffn_adaln"

def rms_norm(x, gain):
    xf = x.astype(jnp.float32)
    y = xf * lax.rsqrt(jnp.mean(xf * xf, axis=-1, keepdims=True) + EPS)
    return (y * gain.astype(jnp.float32)).astype(x.dtype)

def alibi_slopes():
    h = jnp.arange(1, N_ATT_HEADS + 1, dtype=jnp.float32)
    return jnp.exp2(-ALIBI_MAX * h / N_ATT_HEADS)

def hgrn2_mix(q_raw, f_raw, i_raw, g_raw, lb, norm_gain):
    B, S, _ = q_raw.shape
    f32 = jnp.float32
    n = S // HG_CHUNK
    q = jax.nn.silu(q_raw.astype(f32))
    fgt = lb + (1.0 - lb) * jax.nn.sigmoid(f_raw.astype(f32))
    k = 1.0 - fgt
    logf = jnp.log(fgt)
    v = i_raw.astype(f32)

    def chunks(t, dim):
        return t.reshape(B, n, HG_CHUNK, HG_HEADS, dim).transpose(1, 0, 3, 2, 4)

    qc, kc, vc = chunks(q, HG_KDIM), chunks(k, HG_KDIM), chunks(v, HG_VDIM)
    gc = jnp.cumsum(chunks(logf, HG_KDIM), axis=3)
    causal = jnp.tril(jnp.ones((HG_CHUNK, HG_CHUNK), dtype=bool))

    def step(state, xs):
        q_, k_, v_, g_ = xs
        diff = g_[:, :, :, None, :] - g_[:, :, None, :, :]
        decay = jnp.exp(jnp.where(causal[:, :, None], diff, -jnp.inf))
        scores = jnp.einsum('bhtk,bhsk,bhtsk->bhts', q_, k_, decay)
        o = (jnp.einsum('bhts,bhsv->bhtv', scores, v_)
             + jnp.einsum('bhtk,bhkv->bhtv', q_ * jnp.exp(g_), state))
        g_last = g_[:, :, -1, :]
        k_dec = k_ * jnp.exp(g_last[:, :, None, :] - g_)
        state = jnp.exp(g_last)[..., None] * state + jnp.einsum('bhsk,bhsv->bhkv', k_dec, v_)
        return state, o

    state0 = jnp.zeros((B, HG_HEADS, HG_KDIM, HG_VDIM), f32)
    _, o = lax.scan(step, state0, (qc, kc, vc, gc))
    o = o.transpose(1, 0, 3, 2, 4).reshape(B, S, HG_HEADS, HG_VDIM)
    o = rms_norm(o, norm_gain).reshape(B, S, HG_HEADS * HG_VDIM)
    return (o * jax.nn.silu(g_raw.astype(f32))).astype(q_raw.dtype)

def dilated_group(q, k, v, slopes, window, dilation):
    B, S, H, E = q.shape
    band = window // dilation
    L = S // dilation
    nb = -(-L // ATT_BLOCK)
    Lp = nb * ATT_BLOCK

    def to_sub(t):
        t = t.reshape(B, L, dilation, H, E).transpose(0, 2, 1, 3, 4)
        t = jnp.pad(t, ((0, 0), (0, 0), (0, Lp - L), (0, 0), (0, 0)))
        return t.reshape(B, dilation, nb, ATT_BLOCK, H, E)

    def with_prev(t):
        prev = jnp.pad(t, ((0, 0), (0, 0), (1, 0), (0, 0), (0, 0), (0, 0)))[:, :, :-1]
        return jnp.concatenate([prev, t], axis=3)

    qb = to_sub(q)
    kw = with_prev(to_sub(k))
    vw = with_prev(to_sub(v))

    qi = jnp.arange(ATT_BLOCK)[:, None] + ATT_BLOCK
    ki = jnp.arange(2 * ATT_BLOCK)[None, :]
    dist = qi - ki
    blk = jnp.arange(nb)[:, None, None]
    valid = (dist >= 0)[None] & (dist <= band)[None] & (blk * ATT_BLOCK + ki[None] - ATT_BLOCK >= 0)
    bias = -slopes[:, None, None] * (dist.astype(jnp.float32) * dilation)[None]

    scores = jnp.einsum('bdnqhe,bdnkhe->bdnhqk', qb, kw).astype(jnp.float32) * (E ** -0.5)
    scores = jnp.where(valid[None, None, :, None], scores + bias[None, None, None], -jnp.inf)
    m = jnp.max(scores, axis=-1, keepdims=True)
    p = jnp.exp(scores - m)
    s = jnp.sum(p, axis=-1, keepdims=True)
    o = jnp.einsum('bdnhqk,bdnkhe->bdnqhe', p / s, vw.astype(jnp.float32))
    lse = (m + jnp.log(s))[..., 0]

    o = o.reshape(B, dilation, Lp, H, E)[:, :, :L].transpose(0, 2, 1, 3, 4).reshape(B, S, H, E)
    lse = lse.transpose(0, 1, 2, 4, 3).reshape(B, dilation, Lp, H)[:, :, :L]
    lse = lse.transpose(0, 2, 1, 3).reshape(B, S, H)
    return o, lse

def dilated_mixture(q_flat, k_flat, v_flat):
    B, S, _ = q_flat.shape
    shp = (B, S, N_ATT_HEADS, ATT_HEAD_DIM)
    q, k, v = q_flat.reshape(shp), k_flat.reshape(shp), v_flat.reshape(shp)
    slopes = alibi_slopes()
    outs, lses = [], []
    for g, (window, dilation) in enumerate(ATT_GROUPS):
        sl = slice(g * ATT_HEADS_PER_GROUP, (g + 1) * ATT_HEADS_PER_GROUP)
        o, lse = dilated_group(q[:, :, sl], k[:, :, sl], v[:, :, sl], slopes[sl], window, dilation)
        outs.append(o)
        lses.append(lse)
    w = jax.nn.softmax(jnp.stack(lses, axis=0), axis=0)
    o = jnp.sum(w[..., None] * jnp.stack(outs, axis=0), axis=0)
    return o.reshape(B, S, ATT_WIDTH).astype(q_flat.dtype)

def causal_dwconv(u, w, b):
    S = u.shape[1]
    up = jnp.pad(u, ((0, 0), (CONV_W - 1, 0), (0, 0)))
    y = b
    for j in range(CONV_W):
        y = y + up[:, j:j + S] * w[j]
    return y

def setup_inputs(seed: int = 0) -> dict:
    key = jax.random.key(seed)
    ks = jax.random.split(key, 18)
    nrm = jax.random.normal
    f32 = jnp.float32
    D = D_MODEL
    return {
        "x": nrm(ks[0], (BATCH, SEQ, D), f32),
        "c": nrm(ks[1], (BATCH, D), f32),
        "w_ada": nrm(ks[2], (DEPTH, D, N_MOD * D), f32) * (0.5 * D ** -0.5),
        "b_ada": nrm(ks[3], (DEPTH, N_MOD * D), f32) * 0.01,
        "g_norm_mix": 1.0 + 0.02 * nrm(ks[4], (DEPTH, D), f32),
        "w_in": nrm(ks[5], (DEPTH, D, IN_COLS), f32) * D ** -0.5,
        "lb_logits": 0.1 * nrm(ks[6], (DEPTH + 1, HG_WIDTH), f32),
        "g_hg_norm": 1.0 + 0.02 * nrm(ks[7], (DEPTH, HG_HEADS, HG_VDIM), f32),
        "w_branch_a": nrm(ks[8], (DEPTH, HG_HEADS * HG_VDIM, D), f32) * (HG_HEADS * HG_VDIM) ** -0.5,
        "w_branch_b": nrm(ks[9], (DEPTH, ATT_WIDTH, D), f32) * ATT_WIDTH ** -0.5,
        "w_out": nrm(ks[10], (DEPTH, D, D), f32) * D ** -0.5,
        "g_norm_ffn": 1.0 + 0.02 * nrm(ks[11], (DEPTH, D), f32),
        "w_up": nrm(ks[12], (DEPTH, D, 2 * D_FF), f32) * D ** -0.5,
        "conv_w": nrm(ks[13], (DEPTH, CONV_W, D_FF), f32) * CONV_W ** -0.5,
        "conv_b": 0.01 * nrm(ks[14], (DEPTH, D_FF), f32),
        "w_down": nrm(ks[15], (DEPTH, D_FF, D), f32) * D_FF ** -0.5,
        "g_final": 1.0 + 0.02 * nrm(ks[16], (D,), f32),
    }

def reference(x, c, w_ada, b_ada, g_norm_mix, w_in, lb_logits, g_hg_norm, w_branch_a, w_branch_b,
              w_out, g_norm_ffn, w_up, conv_w, conv_b, w_down, g_final):
    split_idx = [int(v) for v in np.cumsum(COL_WIDTHS)[:-1]]
    lower_bounds = jnp.cumsum(jax.nn.softmax(lb_logits.astype(jnp.float32), axis=0), axis=0)
    for l in range(DEPTH):
        mod = jax.nn.silu(c) @ w_ada[l] + b_ada[l]
        sh1, sc1, gt1, sh2, sc2, gt2 = [m[:, None, :] for m in jnp.split(mod, N_MOD, axis=-1)]

        h = rms_norm(x, g_norm_mix[l]) * (1.0 + sc1) + sh1
        proj = h @ w_in[l]
        hq, hf, hi, hg, aq, ak, av, ga, gb = jnp.split(proj, split_idx, axis=-1)
        y_a = hgrn2_mix(hq, hf, hi, hg, lower_bounds[l], g_hg_norm[l])
        y_b = dilated_mixture(aq, ak, av)
        merged = jax.nn.sigmoid(ga) * (y_a @ w_branch_a[l]) + jax.nn.sigmoid(gb) * (y_b @ w_branch_b[l])
        x = x + (1.0 + gt1) * (merged @ w_out[l])

        h2 = rms_norm(x, g_norm_ffn[l]) * (1.0 + sc2) + sh2
        u_gate, u_val = jnp.split(h2 @ w_up[l], 2, axis=-1)
        u_gate = causal_dwconv(u_gate, conv_w[l], conv_b[l])
        x = x + (1.0 + gt2) * ((jax.nn.gelu(u_gate) * u_val) @ w_down[l])
    return rms_norm(x, g_final)


_drawn_inputs = setup_inputs


def setup_inputs(seed=0):
    import zlib

    import numpy as np

    out = dict(_drawn_inputs(seed))
    spreads = {}
    factors = {'b_ada': 3.143,
     'g_norm_mix': 4.412,
     'lb_logits': 8.0,
     'g_hg_norm': 7.074,
     'g_norm_ffn': 13.767,
     'conv_b': 39.059,
     'g_final': 8.287}
    for name, (base, spread) in spreads.items():
        noise = np.random.default_rng([zlib.crc32(name.encode()), seed]).standard_normal(out[name].shape)
        drawn = base * np.exp(spread * noise) if base else spread * noise
        out[name] = __import__('jax').numpy.asarray(drawn.astype(out[name].dtype))
    for name, factor in factors.items():
        out[name] = (out[name] * factor).astype(out[name].dtype)
    return out
```

```python
from contextlib import ExitStack

import numpy as np

import concourse.bass as bass
from concourse import mybir

F32 = mybir.dt.float32
F32R = mybir.dt.float32r
I8 = mybir.dt.int8
ALU = mybir.AluOpType
ACT = mybir.ActivationFunctionType
AX_X = mybir.AxisListType.X

P = 128
D = 1024
S = 512
KT = D // P
TT = S // P
HEADS = 4
E_DIM = 128
CHUNK = 64
NCHUNK = S // CHUNK
HW = HEADS * 128
GROUPS = ((128, 1), (512, 4), (2048, 16))
NG = len(GROUPS)
ORDER = tuple(min(d, 4) for _, d in GROUPS)
D_FF = 2816
FT = D_FF // P
EPS = 1e-6
SCALE = float(E_DIM) ** -0.5
FAR = 1e36
KB = 1024

PAIRS = 2 * NG
U_HQ, U_HF, U_HI = 0, 2, 4
U_PAIR = 6
U_HG = U_PAIR + 3 * PAIRS
U_GA = U_HG + 2
U_GB = U_GA + 4
U_A = U_GB + 4
U_B = U_A + 2
U_OUT = U_B + 2
U_UP = U_OUT + 4
U_DOWN = U_UP + FT
N_UNITS = U_DOWN + FT // 2
C_HG, C_AQ = 3 * HW, 4 * HW
C_AK, C_AV = C_AQ + NG * HW, C_AQ + 2 * NG * HW
C_GATES = C_AQ + 3 * NG * HW

LEVELS = 6
SLOT_DIAG = 4
SLOT_LEVEL = 6
SLOT_KDT, SLOT_UPD, SLOT_O, SLOT_SS = 12, 13, 15, 16
SLOT_STAT = U_PAIR + 3 * PAIRS + 2
SLOT_BC = SLOT_STAT + 3
SLOT_ROW = U_A
MOD_SLOTS = 8


def pair(p):
    g = p // 2
    return g, 2 * (p % 2), ORDER[g]


def score_banks(p):
    return 2 if p // 2 == 0 else 1


def plan_banks():
    uses, table, turn = [0] * 8, {}, {"gemm": 0, "small": 0}

    def use(name, pool):
        banks = (0, 1, 2) if pool == "gemm" else (3, 4, 5, 6, 7)
        b = banks[turn[pool] % len(banks)]
        turn[pool] += 1
        table[name] = (b, uses[b])
        uses[b] += 1

    use("vec", "small")
    use("mod1", "small")
    for k in range(KT):
        use(("xT", 0, k), "small")
    for u in range(U_UP):
        for t in range(tiles_of(u)):
            use(("g", u, t), "gemm")
        for name in small_products(u):
            use(name, "small")
    for k in range(KT):
        use(("xT", 1, k), "small")
    base = list(uses)
    for i, name in enumerate(("gate0", "gate1", "val0", "val1")):
        table[name] = (i, base[i])
        uses[i] += FT // 2
    for b in range(8):
        table[("y", b // 2, b % 2)] = (b, uses[b])
    return table


def tiles_of(u):
    if U_HI <= u < U_PAIR or (U_PAIR <= u < U_HG and (u - U_PAIR) % 3 == 2) or U_A <= u < U_UP:
        return 4
    return 2


def small_products(u):
    names = []
    if u < MOD_SLOTS:
        names.append(("mod2", u))
    if u == SLOT_DIAG:
        names += [("diag", h) for h in range(HEADS)]
    if SLOT_LEVEL <= u < SLOT_LEVEL + LEVELS:
        names += [("lev", u - SLOT_LEVEL, i) for i in range(2)]
    if u == SLOT_KDT:
        names += [("kdT", t) for t in range(TT)]
    if u == SLOT_UPD:
        names += [("upd", c) for c in range(4)]
    if u == SLOT_UPD + 1:
        names += [("upd", c) for c in range(4, NCHUNK - 1)]
    if u == SLOT_O:
        names += [("o", h) for h in range(HEADS)]
    if u == SLOT_SS:
        names += [("ss", h) for h in range(HEADS)]
    for p in range(PAIRS):
        s = U_PAIR + 3 * p + 2
        if u == s:
            names += [("S", p, hh, j) for hh in range(2) for j in range(score_banks(p))]
        if u == s + 1:
            names += [("T", p, hh, j) for hh in range(2) for j in range(score_banks(p))]
        if u == s + 2:
            names += [("O", p, hh) for hh in range(2)]
    if u == SLOT_STAT:
        names += [("mT", g) for g in range(NG)]
    if u == SLOT_STAT + 1:
        names += [("sT", g) for g in range(NG)]
    if SLOT_BC <= u < SLOT_BC + HEADS:
        names += [("bc", u - SLOT_BC, g) for g in range(NG)]
    if u in (SLOT_ROW, SLOT_ROW + 1):
        names += [("row", u - SLOT_ROW, i) for i in range(2)]
    return names


BANKS = plan_banks()

BLOCKS0 = [(0, 0), (1, 0), (1, 1), (2, 1), (2, 2), (3, 2), (3, 3)]
BLOCKS1 = [(i, i) for i in range(TT)]


def blocks_of(p):
    return BLOCKS0 if p // 2 == 0 else BLOCKS1


def block_bank(p, n):
    if p // 2 == 0:
        return (0, n * P) if n < 3 else (1, (n - 3) * P)
    return 0, n * P


def layer_kernel(nc, x, c, w_ada, b_ada, g_norm_mix, w_in, lb_logits, g_hg_norm, w_branch_a, w_branch_b, w_out,
                 g_norm_ffn, w_up, conv_w, conv_b, w_down, g_final, out):
    with ExitStack() as ctx:
        BASE = 16512

        def at(name, kb, shape, dt=F32):
            return nc.alloc_sbuf_tensor_at(name, shape, dt, offset=BASE + int(kb * KB))

        raw = [at(f"w_raw{i}", 120 + 8 * i, [P, 2048]) for i in range(2)]
        whi = [at(f"w_hi{i}", 136 + 8 * i, [P, 2048], F32R) for i in range(2)]
        wlo = [at(f"w_lo{i}", 152 + 8 * i, [P, 2048], F32R) for i in range(2)]
        h_hi = at("h_hi", 168, [P, KT, S], F32R)
        h_lo = at("h_lo", 184, [P, KT, S], F32R)

        x_in = at("x_in", 0, [P, TT, D])
        xn_in = at("xn_in", 16, [P, TT, D])
        ada = [at(f"ada{i}", (90, 98, 106, 32, 40, 48, 56, 64)[i], [P, KT, 256]) for i in range(8)]
        h_tmp = at("h_tmp", 72, [P, 2, S])
        hq = at("hq", 0, [P, HEADS, S])
        hk = at("hk", 8, [P, HEADS, S])
        hp = at("hp", 16, [P, HEADS, S])
        hv = at("hv", 24, [P, TT, HW])
        dec = at("dec", 32, [P, HEADS, S])
        zz = [at("z0", 40, [P, HEADS, S]), at("z1", 48, [P, HEADS, S])]
        scT = at("scT", 56, [P, HEADS, S])
        kd = at("kd", 8, [P, TT, HW])
        st_a = at("st_a", 16, [P, 4, HW])
        st_b = at("st_b", 32, [P, 3, HW])
        o_sb = at("o_sb", 8, [P, HEADS, S])
        o_sq = at("o_sq", 48, [P, HEADS, S])
        o_rs = at("o_rs", 0, [P, HEADS, S])
        yh = at("yh", 32, [P, HEADS, S])
        sgt = at("sgt", 56, [P, 2, S])
        ya_hi = at("ya_hi", 40, [P, HEADS, S], F32R)
        ya_lo = at("ya_lo", 48, [P, HEADS, S], F32R)
        qa = at("qa", 64, [P, 2, S])
        ka = at("ka", 68, [P, 2, S])
        va = at("va", 72, [P, TT, 256])
        prob = at("prob", 76, [P, 2, 7 * P])
        probT = at("probT", 83, [P, 2, 7 * P])
        og = at("og", 90, [P, NG, HEADS, S])
        m_row = at("m_row", 32, [HEADS, NG, S])
        s_row = at("s_row", 56, [HEADS, NG, S])
        yb_hi = at("yb_hi", 64, [P, HEADS, S], F32R)
        yb_lo = at("yb_lo", 76, [P, HEADS, S], F32R)
        sga = at("sga", 0, [P, KT, S])
        sgb = at("sgb", 16, [P, KT, S])
        m_hi = at("m_hi", 90, [P, KT, S], F32R)
        m_lo = at("m_lo", 32, [P, KT, S], F32R)
        x1 = at("x1", 48, [P, TT, D])
        g1_row = at("g1_row", 72, [P, D])
        g2_row = at("g2_row", 112, [P, D])
        gf_row = at("gf_row", 108, [P, D])
        xn_ffn = at("xn_ffn", 0, [P, TT, D])
        h_tmp2 = at("h_tmp2", 116, [P, 2, S])
        act_hi = at("act_hi", 0, [P, FT, S], F32R)
        act_lo = at("act_lo", 64, [P, FT, S], F32R)
        conv = at("conv", 44, [P, 2, S])
        gelu = at("gelu", 116, [P, 2, S])
        squares = at("squares", 184, [P, TT, D])
        masks = at("masks", 116, [P, LEVELS + 1, S], I8)
        off = 200.0

        def small(name, cols, rows=P, dt=F32):
            nonlocal off
            t = at(name, off, [rows, cols], dt)
            off += -(-cols * 4 // 32) * 32 / KB
            return t

        ident = small("ident", P)
        ones = small("ones", P)
        dist0 = small("dist0", 2 * P)
        dist1 = small("dist1", P)
        dist2 = small("dist2", P)
        dint = at("dint", 72, [P, P], mybir.dt.int32)
        vec_rows = small("vec_rows", P, 84)
        conv_rows = small("conv_rows", P, 88)
        vec = small("vec", 84)
        convc = small("convc", 88)
        mod = small("mod", 48)
        csig = small("csig", 8)
        csilu = small("csilu", 8)
        lbd = small("lbd", 4)
        lb = small("lb", 4)
        oml = small("oml", 4)
        a1 = small("a1", 8)
        a2 = small("a2", 8)
        gp = small("gp", 16)
        ssq = small("ssq", 12)
        rstd = small("rstd", 12)
        nmax = small("nmax", 48)
        ssum = small("ssum", 48)
        mx = small("mx", 8)
        eglast = small("eglast", 32)
        epsc = small("epsc", 1)
        mhalf = small("mhalf", 4)
        inv = at("inv", 62, [HEADS, S])
        assert BASE + off * KB <= nc.sbuf_usable_end, off
        B_ADA, G_MIX, G_FFN, G_HG, LB, C_ = 0, 48, 56, 64, 68, 76

        bank = [ctx.enter_context(nc.psum_tensor(f"bank{i}", [P, 512], F32)) for i in range(8)]

        def sem(name):
            return ctx.enter_context(nc.semaphore(name))

        full = [sem(f"bank_full{b}") for b in range(8)]
        free = [sem(f"bank_free{b}") for b in range(8)]
        raw_in = [sem(f"raw_in{i}") for i in range(2)]
        hi_done = sem("hi_done")
        lo_done = sem("lo_done")
        down_used = sem("down_used")
        x_in_s = [sem(f"x_landed{t}") for t in range(TT)]
        x_again = sem("x_again")
        vec_in = sem("vec_in")
        ada_in = [sem(f"ada_in{i}") for i in range(8)]
        gf_in = sem("gf_in")
        consts = sem("consts")
        dchain = sem("dve_chain")
        glast_done = sem("glast_done")
        pchain = sem("pool_chain")
        csig_done, csilu_done, lbd_done = sem("csig_done"), sem("csilu_done"), sem("lbd_done")
        lb_done = sem("lb_done")
        sq_done = sem("sq_done")
        rstd_done = sem("rstd_done")
        xn_done = sem("xn_done")
        h_hi_done, h_lo_done = sem("h_hi_done"), sem("h_lo_done")
        sig_done = sem("sig_done")
        f_done, logf_done = sem("f_done"), sem("logf_done")
        d1_done, e_done, z_done, p_done = sem("d1_done"), sem("e_done"), sem("z_done"), sem("p_done")
        eg_done, kdif_done, ke_done, kdec_done = sem("eg_done"), sem("kdif_done"), sem("ke_done"), sem("kdec_done")
        osq_done, rs_done, yfull_done, yahi_done, yalo_done = (
            sem("osq_done"), sem("rs_done"), sem("yfull_done"), sem("yahi_done"), sem("yalo_done"))
        nmax_done, prob_done = sem("nmax_done"), sem("prob_done")
        mdiff_done, wexp_done, crow_done = sem("mdiff_done"), sem("wexp_done"), sem("crow_done")
        ybfull_done, ybhi_done, yblo_done = sem("ybfull_done"), sem("ybhi_done"), sem("yblo_done")
        mfull_done, mhi_done, mlo_done = sem("mfull_done"), sem("mhi_done"), sem("mlo_done")
        gp_done, x1_done = sem("gp_done"), sem("x1_done")
        conv0_done, tap_done, gelu_done, ahi_done, alo_done = (
            sem("conv0_done"), sem("tap_done"), sem("gelu_done"), sem("ahi_done"), sem("alo_done"))
        x2_done, y_done, out_done = sem("x2_done"), sem("y_done"), sem("out_done")

        def claim(eng, name):
            b, n = BANKS[name]
            if n:
                eng.wait_ge(free[b], n)
            return bank[b]

        def filled(ins, name):
            ins.then_inc(full[BANKS[name][0]], 1)

        def ready(eng, name):
            b, n = BANKS[name]
            eng.wait_ge(full[b], n + 1)
            return bank[b]

        def release(ins, name):
            ins.then_inc(free[BANKS[name][0]], 1)

        def evacuated(eng, name):
            b, n = BANKS[name]
            eng.wait_ge(free[b], n + 1)

        def cols_of(w, c0):
            return w[0][:, bass.ds(c0, 256)].rearrange("(k p) c -> p k c", p=P)

        def unit_source(u):
            if u < U_PAIR:
                return cols_of(w_in, 256 * u)
            if u < U_HG:
                p, what = divmod(u - U_PAIR, 3)
                return cols_of(w_in, (C_AQ, C_AK, C_AV)[what] + 256 * p)
            if u < U_GA:
                return cols_of(w_in, C_HG + 256 * (u - U_HG))
            if u < U_A:
                return cols_of(w_in, C_GATES + 256 * (u - U_GA))
            if u < U_OUT:
                w, j = (w_branch_a, u - U_A) if u < U_B else (w_branch_b, u - U_B)
                return w[0][:, 512 * j:512 * j + 512].rearrange("(k p) c -> p k c", p=P)
            return cols_of(w_out, 256 * (u - U_OUT))

        x_tok = x[0].rearrange("(t p) d -> p t d", p=P)
        out_tok = out[0].rearrange("(t p) d -> p t d", p=P)

        block = ctx.enter_context(nc.Block())

        @block.sync
        def _(sp):
            def rows(dst, r0, src, n):
                sp.dma_start(dst[r0:r0 + n, :], src).then_inc(vec_in, 16)

            rows(vec_rows, C_, c.rearrange("b (k p) -> (b k) p", p=P), 8)
            rows(vec_rows, B_ADA, b_ada.rearrange("l (k p) -> (l k) p", p=P), 48)
            rows(vec_rows, G_MIX, g_norm_mix.rearrange("l (k p) -> (l k) p", p=P), 8)
            rows(vec_rows, G_FFN, g_norm_ffn.rearrange("l (k p) -> (l k) p", p=P), 8)
            rows(vec_rows, G_HG, g_hg_norm.rearrange("l h p -> (l h) p"), 4)
            rows(vec_rows, LB, lb_logits.rearrange("l (k p) -> (l k) p", p=P), 8)
            rows(conv_rows, 0, conv_w.rearrange("l j (k p) -> (l j k) p", p=P), 66)
            rows(conv_rows, 66, conv_b.rearrange("l (k p) -> (l k) p", p=P), 22)
            for t in range(TT):
                sp.dma_start(x_in[:, t, :], x_tok[:, t, :]).then_inc(x_in_s[t], 16)

            def load_ada(n):
                slot = n if n < 8 else (n - 8) % 3
                if n >= 8:
                    ready(sp, "mod1" if n < 11 else ("mod2", (n - 11) // 2))
                sp.dma_start(ada[slot][:, :, :], cols_of(w_ada, 256 * n)).then_inc(ada_in[slot], 16)

            def load_unit(u, src, slot):
                if not isinstance(u, int) or u >= 2:
                    sp.wait_ge(hi_done, u - 1)
                    sp.wait_ge(lo_done, u - 1)
                width = src.shape[2]
                sp.dma_start(raw[slot][:, :].rearrange("p (k c) -> p k c", c=width), src).then_inc(raw_in[slot], 16)

            for n in range(8):
                load_ada(n)
            for u in range(U_UP):
                if u == U_B + 2:
                    ready(sp, ("g", U_B - 1, 3))
                    sp.wait_ge(yblo_done, HEADS)
                    sp.dma_start(x1[:, :, :], x_tok).then_inc(x_again, 16)
                    sp.dma_start(gf_row[:, :], g_final.rearrange("(a d) -> a d", a=1).broadcast_to([P, D])).then_inc(gf_in, 16)
                load_unit(u, unit_source(u), u % 2)
                if 0 <= u - 1 < MOD_SLOTS:
                    load_ada(8 + 2 * (u - 1))
                    load_ada(9 + 2 * (u - 1))
            with sp.Fori(0, FT // 2) as i:
                load_unit(2 * i + U_UP, cols_of(w_up, i * 256), 0)
                load_unit(2 * i + U_UP + 1, cols_of(w_up, i * 256 + D_FF), 1)

            def down_rows(i):
                return w_down[0][bass.ds(i * 256, 256), :].rearrange("(k p) c -> p k c", p=P)

            with sp.Fori(0, FT // 4) as i:
                load_unit(2 * i + U_DOWN, down_rows(2 * i), 0)
                load_unit(2 * i + U_DOWN + 1, down_rows(2 * i + 1), 1)
            load_unit(N_UNITS - 1, down_rows(FT // 2 - 1), 0)

            for t in range(TT):
                sp.wait_ge(y_done, t + 1)
                sp.dma_start(out_tok[:, t, :], x1[:, t, :]).then_inc(out_done, 16)
            sp.wait_ge(out_done, 16 * TT)

        @block.gpsimd
        def _(pool):
            n_chain = [0]

            def link(ins):
                n_chain[0] += 1
                ins.then_inc(pchain, 1)
                pool.wait_ge(pchain, n_chain[0])

            def select(t, pattern, base, mult, op=ALU.is_ge, fill=0.0):
                link(pool.affine_select(out=t, in_=t, compare_op=op, fill=fill, base=base, pattern=pattern,
                                        channel_multiplier=mult))

            link(pool.memset(ident[:, :], 0.0))
            select(ident[:, :], [[-1, P]], 0, 1, ALU.not_equal, 1.0)
            link(pool.memset(ones[:, :], 1.0))
            link(pool.memset(mhalf[:, :], -0.5))
            pool.memset(epsc[:, :], EPS).then_inc(consts, 1)

            def inverse_root(first, n):
                cols = slice(first, first + n)
                link(pool.tensor_scalar(rstd[:, cols], ssq[:, cols], 1.0 / D, EPS, ALU.mult, ALU.add))
                pool.tensor_tensor(rstd[:, cols], rstd[:, cols], mhalf[:, 0:n], ALU.pow).then_inc(rstd_done, 1)

            pool.wait_ge(sq_done, TT)
            inverse_root(0, TT)

            link(pool.memset(masks[:, :, :], 1.0))
            for j in range(LEVELS):
                half = 1 << j
                nb = P // (2 * half)
                m = masks[:, j, :].rearrange("p (rep blk tok) -> p rep blk tok", rep=8, blk=nb)
                select(m, [[0, 8], [-2 * half, nb], [0, half]], 0, 1)
                select(m, [[0, 8], [2 * half, nb], [0, half]], half - 1, -1)
            select(masks[:, LEVELS, :].rearrange("p (a t) -> p a t", a=4), [[0, 4], [1, P]], 0, -1, ALU.is_equal)
            for dist, n in ((dist0, 2), (dist1, 1)):
                link(pool.iota(dist[:, :], [[-1, n * P]], base=(n - 1) * P, channel_multiplier=1,
                               allow_small_or_imprecise_dtypes=True))
                select(dist[:, :], [[-1, n * P]], (n - 1) * P, 1, fill=FAR)
                if n == 2:
                    select(dist[:, :], [[1, n * P]], 0, -1, fill=FAR)
            pool.wait_ge(h_lo_done, KT)
            pool.iota(dint[:, :], [[-1, P]], base=P, channel_multiplier=1).then_inc(consts, 1)

            def low_part(u, slot):
                pool.wait_ge(hi_done, u + 1)
                pool.tensor_tensor(wlo[slot][:, :], raw[slot][:, :], whi[slot][:, :].bitcast(F32),
                                   ALU.subtract).then_inc(lo_done, 1)

            with pool.Fori(0, U_UP // 2) as i:
                low_part(2 * i, 0)
                low_part(2 * i + 1, 1)
            for t in range(TT):
                pool.wait_ge(sq_done, TT + 1 + t)
                inverse_root(TT + t, 1)
            with pool.Fori(0, (N_UNITS - U_UP) // 2) as i:
                low_part(2 * i + U_UP, 0)
                low_part(2 * i + U_UP + 1, 1)
            low_part(N_UNITS - 1, 0)
            for t in range(TT):
                pool.wait_ge(sq_done, 2 * TT + 1 + t)
                inverse_root(2 * TT + t, 1)

        @block.scalar
        def _(act):
            def high_part(slot, landed):
                act.wait_ge(raw_in[slot], landed)
                act.activation(whi[slot][:, :], raw[slot][:, :], ACT.Copy).then_inc(hi_done, 1)

            def unit_high(u):
                if u > U_DOWN + 1:
                    act.wait_ge(down_used, u - 1 - U_DOWN)
                elif u == U_DOWN + 1:
                    b, n = BANKS["val1"]
                    act.wait_ge(full[b], n + FT // 2)
                elif u >= 2:
                    ready(act, ("g", u - 2, tiles_of(u - 2) - 1))
                high_part(u % 2, 16 * (u // 2 + 1))

            evacuated(act, "vec")
            act.activation(csig[:, :], vec[:, C_:C_ + 8], ACT.Sigmoid).then_inc(csig_done, 1)
            act.wait_ge(lbd_done, 1)
            act.activation(lb[:, :], lbd[:, :], ACT.Sigmoid).then_inc(lb_done, 1)
            for t in range(TT):
                act.wait_ge(x_in_s[t], 16)
                act.activation(xn_in[:, t, :], x_in[:, t, :], ACT.Square,
                               accum_out=ssq[:, t:t + 1]).then_inc(sq_done, 1)

            def round_h(which):
                for k in range(KT):
                    evacuated(act, ("xT", which, k))
                    tmp = h_tmp if which == 0 else h_tmp2
                    act.activation(h_hi[:, k, :], tmp[:, k % 2, :], ACT.Copy).then_inc(h_hi_done, 1)

            round_h(0)
            unit_high(0)

            def small_results(u):
                if u == SLOT_DIAG:
                    act.wait_ge(f_done, HEADS)
                    act.activation(hp[:, :, :], hp[:, :, :], ACT.Ln).then_inc(logf_done, 1)
                if SLOT_LEVEL <= u < SLOT_LEVEL + LEVELS:
                    level_exp(u - SLOT_LEVEL)
                if u == SLOT_KDT:
                    act.wait_ge(p_done, LEVELS)
                    act.activation(dec[:, :, :], hp[:, :, :], ACT.Exp).then_inc(eg_done, 1)
                    g_last = hp[:, :, :].rearrange("p h (c t) -> p (h c) t", t=CHUNK)[:, :, CHUNK - 1]
                    act.activation(eglast[:, :], g_last, ACT.Exp).then_inc(glast_done, 1)
                    act.wait_ge(kdif_done, 1)
                    act.activation(dec[:, :, :], dec[:, :, :], ACT.Exp).then_inc(ke_done, 1)
                if u == SLOT_KDT + 1:
                    for t in range(2):
                        b = ready(act, ("kdT", t))
                        release(act.activation(kd[:, t, :], b[:, :], ACT.Copy), ("kdT", t))
                if u == SLOT_O + 1:
                    for h in range(HEADS):
                        b = ready(act, ("o", h))
                        release(act.activation(o_sb[:, h, :], b[:, :], ACT.Copy), ("o", h))
                if u == SLOT_SS + 1:
                    for h in range(HEADS):
                        b = ready(act, ("ss", h))
                        release(act.activation(o_rs[:, h, :], b[:, :], ACT.Ln, scale=1.0 / 128, bias=epsc[:, :]), ("ss", h))
                        evacuated(act, ("ss", h))
                        act.activation(o_rs[:, h, :], o_rs[:, h, :], ACT.Exp, scale=-0.5).then_inc(rs_done, 1)
                for p in range(PAIRS):
                    s = U_PAIR + 3 * p + 2
                    if u == s + 1:
                        softmax_exp(p)
                    if u == s + 2:
                        if p:
                            ready(act, ("O", p - 1, 1))
                        copy_probT(p, 1)
                    if u == s + 3:
                        scatter_o(p, 1)
                if u == SLOT_STAT + 1:
                    for g in range(NG):
                        gather_row(m_row, "mT", g)
                if u == SLOT_STAT + 2:
                    for g in range(NG):
                        gather_row(s_row, "sT", g)
                    act.wait_ge(mdiff_done, 1)
                    act.activation(m_row[:, :, :], m_row[:, :, :], ACT.Exp).then_inc(wexp_done, 1)
                if SLOT_BC < u <= SLOT_BC + HEADS:
                    h = u - SLOT_BC - 1
                    act.wait_ge(ybfull_done, h + 1)
                    act.activation(yb_hi[:, h, :], og[:, 0, h, :], ACT.Copy).then_inc(ybhi_done, 1)
                if u in (SLOT_ROW + 1, SLOT_ROW + 2):
                    w = u - SLOT_ROW - 1
                    if w == 1:
                        act.wait_ge(yblo_done, HEADS)
                    for i in range(2):
                        b = ready(act, ("row", w, i))
                        row = (g1_row, g2_row)[w]
                        release(act.activation(row[:, 512 * i:512 * i + 512], b[:, :], ACT.Copy), ("row", w, i))

            def level_exp(j):
                half = 1 << j
                pv = hp[:, :, :].rearrange("p h (blk pos tok) -> p (h blk) pos tok", pos=2, tok=half)
                dv = dec[:, :, :].rearrange("p h (blk pos tok) -> p (h blk) pos tok", pos=2, tok=half)
                act.wait_ge(d1_done, j + 1)
                act.activation(dv[:, :, 1, :], pv[:, :, 1, :], ACT.Exp)
                act.activation(dv[:, :, 0, :], dv[:, :, 0, :], ACT.Exp).then_inc(e_done, 1)

            def softmax_exp(p):
                g, h0, _ = pair(p)
                for hh in range(2):
                    act.wait_ge(nmax_done, 2 * p + hh + 1)
                    at_ = 0
                    for q in range(TT):
                        n = sum(b[0] == q for b in blocks_of(p)) * P
                        col = (g * TT + q) * HEADS + h0 + hh
                        ins = act.activation(prob[:, hh, at_:at_ + n], prob[:, hh, at_:at_ + n], ACT.Exp, scale=SCALE,
                                             bias=nmax[:, col:col + 1], accum_out=ssum[:, col:col + 1])
                        at_ += n
                    ins.then_inc(prob_done, 1)

            def copy_probT(p, hh):
                for j in range(score_banks(p)):
                    b = ready(act, ("T", p, hh, j))
                    n = sum(block_bank(p, i)[0] == j for i in range(len(blocks_of(p)))) * P
                    release(act.activation(probT[:, hh, 3 * P * j:3 * P * j + n], b[:, 0:n], ACT.Copy), ("T", p, hh, j))

            def scatter_o(p, hh):
                g, h0, d = pair(p)
                b = ready(act, ("O", p, hh))
                release(act.activation(og[:, g, h0 + hh, :].rearrange("p (l res) -> p res l", res=d),
                                    b[:, :].rearrange("p (res l) -> p res l", res=d), ACT.Copy), ("O", p, hh))

            def gather_row(dst, name, g):
                d = ORDER[g]
                b = ready(act, (name, g))
                release(act.activation(dst[:, g, :].rearrange("p (l res) -> p res l", res=d),
                                    b[0:HEADS, :].rearrange("p (res l) -> p res l", res=d), ACT.Copy), (name, g))

            def evacuate(u):
                if u < U_HI:
                    for t in range(2):
                        h = 2 * (u % 2) + t
                        if u >= U_HF:
                            evacuated(act, ("g", u - 2, t))
                        b = ready(act, ("g", u, t))
                        ins = act.activation(dec[:, h, :], b[:, :], ACT.Sigmoid)
                        if u < U_HF:
                            ins.then_inc(sig_done, 1)
                        else:
                            release(ins, ("g", u, t))
                elif U_PAIR <= u < U_HG:
                    p, what = divmod(u - U_PAIR, 3)
                    if what == 0:
                        g, h0, d = pair(p)
                        if p:
                            ready(act, ("S", p - 1, 1, score_banks(p - 1) - 1))
                        for t in range(2):
                            b = ready(act, ("g", u, t))
                            release(act.activation(qa[:, t, :].rearrange("p (res l) -> p res l", res=d),
                                                b[:, :].rearrange("p (l res) -> p res l", res=d), ACT.Copy), ("g", u, t))
                elif U_HG <= u < U_GA:
                    for t in range(2):
                        h = 2 * (u - U_HG) + t
                        if h >= 2:
                            act.wait_ge(yfull_done, h - 1)
                        b = ready(act, ("g", u, t))
                        act.activation(sgt[:, h % 2, :], b[:, :], ACT.Sigmoid).then_inc(sig_done, 1)
                    for t in range(2):
                        h = 2 * (u - U_HG) + t
                        act.wait_ge(yfull_done, h + 1)
                        act.activation(ya_hi[:, h, :], yh[:, h, :], ACT.Copy).then_inc(yahi_done, 1)
                elif U_GA <= u < U_A:
                    dst, u0 = (sga, U_GA) if u < U_GB else (sgb, U_GB)
                    if u == U_GA:
                        act.wait_ge(yalo_done, HEADS)
                    for t in range(2):
                        b = ready(act, ("g", u, t))
                        release(act.activation(dst[:, 2 * (u - u0) + t, :], b[:, :], ACT.Sigmoid), ("g", u, t))
                elif U_B <= u < U_OUT:
                    if u == U_B:
                        act.wait_ge(yblo_done, HEADS)
                    for t in range(4):
                        f = 4 * (u - U_B) + t
                        act.wait_ge(mfull_done, f + 1)
                        act.activation(m_hi[:, f, :], sgb[:, f, :], ACT.Copy).then_inc(mhi_done, 1)

            for u in range(U_UP):
                unit_high(u + 1)
                small_results(u)
                evacuate(u)

            for t in range(TT):
                act.wait_ge(x1_done, 3 * TT + t + 1)
                act.activation(xn_ffn[:, t, :], x1[:, t, :], ACT.Square,
                               accum_out=ssq[:, TT + t:TT + t + 1]).then_inc(sq_done, 1)
            round_h(1)

            b_gate = BANKS["gate0"][1]
            CW = convc[:, :]
            with act.Fori(0, FT // 2) as i:
                act.wait_ge(full[3], BANKS["val1"][1] + i)
                high_part(1, 8 * (U_UP + 2) + 16 * i)
                for t in range(2):
                    act.wait_ge(full[t], BANKS[f"gate{t}"][1] + 1 + i)
                    act.activation(conv[:, t, :], bank[t][:, :], ACT.Identity,
                                   scale=CW[:, bass.ds(2 * i + (2 * FT + t), 1)],
                                   bias=CW[:, bass.ds(2 * i + (3 * FT + t), 1)]).then_inc(conv0_done, 1)
                high_part(0, 8 * (U_UP + 4) + 16 * i)
                for t in range(2):
                    act.wait_ge(free[t], BANKS[f"gate{t}"][1] + 1 + i)
                    act.activation(gelu[:, t, :], conv[:, t, :], ACT.Gelu_apprx_tanh).then_inc(gelu_done, 1)
                for t in range(2):
                    act.wait_ge(free[2 + t], BANKS[f"val{t}"][1] + 1 + i)
                    act.activation(act_hi[:, bass.ds(2 * i + t, 1), :].rearrange("p a s -> p (a s)"), gelu[:, t, :],
                                   ACT.Copy).then_inc(ahi_done, 1)
            for u in range(U_DOWN + 1, N_UNITS):
                unit_high(u)
            for t in range(TT):
                act.wait_ge(x2_done, t + 1)
                act.activation(squares[:, t, :], x1[:, t, :], ACT.Square,
                               accum_out=ssq[:, 2 * TT + t:2 * TT + t + 1]).then_inc(sq_done, 1)

        @block.tensor
        def _(pe):
            def mm(o, lhsT, rhs, start=True, stop=True, **kw):
                return pe.matmul(o, lhsT, rhs, start=start, stop=stop, **kw)

            def transpose(o, i):
                return pe.transpose(o, i, ident[0:i.shape[0], 0:i.shape[0]])

            pe.wait_ge(consts, 1)
            pe.wait_ge(vec_in, 16 * 8)
            b = claim(pe, "vec")
            transpose(b[:, 0:84], vec_rows[:, :])
            filled(transpose(b[:, 84:172], conv_rows[:, :]), "vec")

            def modulation(b, col, n, slot):
                pe.wait_ge(ada_in[slot], 16 * (1 if n < 8 else 2 + (n - 8) // 3))
                for t in range(2):
                    for k in range(KT):
                        ins = mm(b[:, col + t:col + t + 1], ada[slot][:, k, t * P:(t + 1) * P], csilu[:, k:k + 1],
                                 k == 0, k == KT - 1)
                return ins

            pe.wait_ge(csilu_done, 1)
            b = claim(pe, "mod1")
            for n in range(8):
                ins = modulation(b, 2 * n, n, n)
            filled(ins, "mod1")

            def transposed_h(which):
                src = xn_in if which == 0 else xn_ffn
                for k in range(KT):
                    b = claim(pe, ("xT", which, k))
                    for t in range(TT):
                        if k == 0:
                            pe.wait_ge(xn_done, which * TT + t + 1)
                        ins = transpose(b[:, t * P:(t + 1) * P], src[:, t, k * P:(k + 1) * P])
                    filled(ins, ("xT", which, k))

            transposed_h(0)

            def unit_parts(u, slot, width):
                pe.wait_ge(lo_done, u + 1)
                return [w[slot][:, :].rearrange("p (k c) -> p k c", c=width) for w in (whi, wlo)]

            def three_passes(o, lhs, rhs, k, last_k, start=None, skip=False):
                for i, (a, bb) in enumerate(((0, 0), (0, 1), (1, 0))):
                    ins = mm(o, lhs[a], rhs[bb], start=(k == 0 and i == 0) if start is None else start and i == 0,
                             stop=k == last_k and i == 2, skip_group_check=skip)
                return ins

            def feature_tile(o, parts, c0, acts, kts=KT):
                for k in range(kts):
                    ins = three_passes(o, [w[:, k, c0:c0 + P] for w in parts], [a[:, k, :] for a in acts], k, kts - 1)
                return ins

            def token_tile(o, parts, acts, tokens, kts=KT):
                for k in range(kts):
                    ins = three_passes(o, [tokens(a[:, k, :]) for a in acts], [w[:, k, :] for w in parts], k, kts - 1)
                return ins

            def plain_tokens(t):
                return lambda a: a[:, t * P:(t + 1) * P]

            def dilated_tokens(t, d):
                if d == 1:
                    return plain_tokens(t)
                return lambda a: a.rearrange("p (l res) -> p res l", res=d)[:, t, :]

            def products(u):
                hT = (h_hi, h_lo)
                n = tiles_of(u)
                width = 512 if U_A <= u < U_OUT else 256
                parts = unit_parts(u, u % 2, width)
                for t in range(n):
                    b = claim(pe, ("g", u, t))
                    if u == 0 and t == 0:
                        pe.wait_ge(h_lo_done, KT)
                    if u == U_A and t == 0:
                        pe.wait_ge(yalo_done, HEADS)
                    if u == U_B and t == 0:
                        pe.wait_ge(yblo_done, HEADS)
                    if u == U_OUT and t == 0:
                        pe.wait_ge(mlo_done, KT)
                    if u >= U_OUT:
                        ins = token_tile(b[:, 0:256], parts, (m_hi, m_lo), plain_tokens(t))
                    elif u >= U_A:
                        ins = feature_tile(b[:, :], parts, t * P, (ya_hi, ya_lo) if u < U_B else (yb_hi, yb_lo), HEADS)
                    elif n == 4:
                        d = 1 if u < U_PAIR else pair((u - U_PAIR) // 3)[2]
                        ins = token_tile(b[:, 0:256], parts, hT, dilated_tokens(t, d))
                    else:
                        ins = feature_tile(b[:, :], parts, t * P, hT)
                    filled(ins, ("g", u, t))

            def scores(p):
                for hh in range(2):
                    for j in range(score_banks(p)):
                        b = claim(pe, ("S", p, hh, j))
                        if p // 2 == 0:
                            runs = [(0, 0, 1), (1, 0, 2)] if j == 0 else [(2, 1, 2), (3, 2, 2)]
                        else:
                            runs = [(i, i, 1) for i in range(TT)]
                        col = 0
                        for q, k, n in runs:
                            ins = mm(b[:, col:col + n * P], qa[:, hh, q * P:(q + 1) * P], ka[:, hh, k * P:(k + n) * P])
                            col += n * P
                        filled(ins, ("S", p, hh, j))

            def small(u):
                if u < MOD_SLOTS:
                    b = claim(pe, ("mod2", u))
                    for i in range(2):
                        n = 8 + 2 * u + i
                        ins = modulation(b, 2 * i, n, (n - 8) % 3)
                    filled(ins, ("mod2", u))
                if u == SLOT_DIAG:
                    for t in range(4):
                        evacuated(pe, ("g", U_HQ + t // 2, t % 2))
                    pe.wait_ge(f_done, HEADS)
                    for h in range(HEADS):
                        b = claim(pe, ("diag", h))
                        for t in range(TT):
                            tok = slice(t * P, (t + 1) * P)
                            ins = mm(b[:, tok], hk[:, h, tok], hq[:, h, tok])
                        filled(ins, ("diag", h))
                if SLOT_LEVEL <= u < SLOT_LEVEL + LEVELS:
                    j = u - SLOT_LEVEL
                    pe.wait_ge(z_done, j + 1)
                    z = zz[j % 2]
                    for i in range(2):
                        b = claim(pe, ("lev", j, i))
                        for n in range(8):
                            h, t = divmod(8 * i + n, TT)
                            zt = z[:, h, t * P:(t + 1) * P]
                            second = zt.rearrange("p (blk pos tok) -> p blk pos tok", pos=2, tok=1 << j)[:, :, 1, :]
                            ins = mm(b[:, n * 64:(n + 1) * 64].rearrange("p (blk tok) -> p blk tok", tok=1 << j), zt, second)
                        filled(ins, ("lev", j, i))
                if u == SLOT_KDT:
                    pe.wait_ge(kdec_done, 1)
                    for t in range(TT):
                        b = claim(pe, ("kdT", t))
                        for h in range(HEADS):
                            ins = transpose(b[:, h * P:(h + 1) * P], zz[1][:, h, t * P:(t + 1) * P])
                        filled(ins, ("kdT", t))
                if u in (SLOT_UPD, SLOT_UPD + 1):
                    for c in (range(4) if u == SLOT_UPD else range(4, NCHUNK - 1)):
                        t, rows = c // 2, slice(64 * (c % 2), 64 * (c % 2) + 64)
                        evacuated(pe, ("kdT", t))
                        b = claim(pe, ("upd", c))
                        for h in range(HEADS):
                            ins = mm(b[:, h * P:(h + 1) * P], kd[rows, t, h * P:(h + 1) * P], hv[rows, t, h * P:(h + 1) * P])
                        filled(ins, ("upd", c))
                if u == SLOT_O:
                    for c in range(NCHUNK - 1):
                        evacuated(pe, ("upd", c))
                    for i in range(2):
                        evacuated(pe, ("lev", LEVELS - 1, i))
                    for h in range(HEADS):
                        b = claim(pe, ("o", h))
                        for t in range(TT):
                            tok = slice(t * P, (t + 1) * P)
                            mm(b[:, tok], hv[:, t, h * P:(h + 1) * P], scT[:, h, tok], start=t == 0, stop=False,
                               skip_group_check=True)
                        for c in range(1, NCHUNK):
                            st = st_a[:, c - 1, :] if c < 5 else st_b[:, c - 5, :]
                            tok = slice(c * CHUNK, (c + 1) * CHUNK)
                            ins = mm(b[:, tok], st[:, h * P:(h + 1) * P], zz[0][:, h, tok], start=False,
                                     stop=c == NCHUNK - 1, skip_group_check=True)
                        filled(ins, ("o", h))
                if u == SLOT_SS:
                    for h in range(HEADS):
                        pe.wait_ge(osq_done, h + 1)
                        b = claim(pe, ("ss", h))
                        filled(mm(b[:, :], ones[:, :], o_sq[:, h, :]), ("ss", h))
                for p in range(PAIRS):
                    s = U_PAIR + 3 * p + 2
                    if u == s:
                        for t in range(2):
                            evacuated(pe, ("g", s - 2, t))
                            evacuated(pe, ("g", s - 1, t))
                        scores(p)
                    if u == s + 1:
                        for hh in range(2):
                            pe.wait_ge(prob_done, 2 * p + hh + 1)
                            bb = [claim(pe, ("T", p, hh, j)) for j in range(score_banks(p))]
                            n_blocks = len(blocks_of(p))
                            for n in range(n_blocks):
                                j, col = block_bank(p, n)
                                ins = transpose(bb[j][:, col:col + P], prob[:, hh, n * P:(n + 1) * P])
                                if n == n_blocks - 1 or block_bank(p, n + 1)[0] != j:
                                    filled(ins, ("T", p, hh, j))
                    if u == s + 2:
                        for t in range(4):
                            evacuated(pe, ("g", s, t))
                        for hh in range(2):
                            b = claim(pe, ("O", p, hh))
                            for j in range(score_banks(p)):
                                evacuated(pe, ("T", p, hh, j))
                            blocks = blocks_of(p)
                            for n, (q, k) in enumerate(blocks):
                                first = n == 0 or blocks[n - 1][0] != q
                                last = n == len(blocks) - 1 or blocks[n + 1][0] != q
                                ins = mm(b[:, q * P:(q + 1) * P], va[:, k, hh * P:(hh + 1) * P],
                                         probT[:, hh, n * P:(n + 1) * P], first, last)
                            filled(ins, ("O", p, hh))
                if u in (SLOT_STAT, SLOT_STAT + 1):
                    name, src = (("mT", nmax), ("sT", ssum))[u - SLOT_STAT]
                    for g in range(NG):
                        b = claim(pe, (name, g))
                        for q in range(TT):
                            col = (g * TT + q) * HEADS
                            ins = transpose(b[0:HEADS, q * P:(q + 1) * P], src[:, col:col + HEADS])
                        filled(ins, (name, g))
                if SLOT_BC <= u < SLOT_BC + HEADS:
                    h = u - SLOT_BC
                    pe.wait_ge(crow_done, NG)
                    for g in range(NG):
                        b = claim(pe, ("bc", h, g))
                        filled(mm(b[:, :], ident[0:HEADS, h:h + 1].broadcast_to([HEADS, P]), m_row[:, g, :]), ("bc", h, g))
                if u in (SLOT_ROW, SLOT_ROW + 1):
                    w = u - SLOT_ROW
                    pe.wait_ge(gp_done, 1)
                    for i in range(2):
                        b = claim(pe, ("row", w, i))
                        for k in range(4):
                            n = 8 * w + 4 * i + k
                            ins = transpose(b[:, k * P:(k + 1) * P], gp[:, n:n + 1].broadcast_to([P, P]))
                        filled(ins, ("row", w, i))

            for u in range(U_UP):
                products(u)
                small(u)

            transposed_h(1)
            pe.wait_ge(h_lo_done, 2 * KT)
            with pe.Fori(0, FT // 2) as i:
                for half, name in enumerate(("gate", "val")):
                    parts = unit_parts(2 * i + U_UP + half, half, 256)
                    for t in range(2):
                        bk, n = BANKS[f"{name}{t}"]
                        pe.wait_ge(free[bk], i + n)
                        feature_tile(bank[bk][:, :], parts, t * P, (h_hi, h_lo)).then_inc(full[bk], 1)
            for t in range(TT):
                for half in range(2):
                    claim(pe, ("y", t, half))
            for i in range(FT // 2):
                u = U_DOWN + i
                parts = unit_parts(u, u % 2, 1024)
                pe.wait_ge(alo_done, 2 * i + 2)
                for t in range(TT):
                    tok = slice(t * P, (t + 1) * P)
                    for half in range(2):
                        for kk in range(2):
                            k = 2 * i + kk
                            ins = three_passes(bank[2 * t + half][:, :], [a[:, k, tok] for a in (act_hi, act_lo)],
                                               [w[:, kk, half * 512:half * 512 + 512] for w in parts], k, FT - 1)
                        if i == FT // 2 - 1:
                            filled(ins, ("y", t, half))
                if i < FT // 2 - 1:
                    ins.then_inc(down_used, 1)

        @block.vector
        def _(dve):
            n_chain = [0]

            def link(ins):
                n_chain[0] += 1
                ins.then_inc(dchain, 1)
                dve.wait_ge(dchain, n_chain[0])

            tt, ts, stt = dve.tensor_tensor, dve.tensor_scalar, dve.scalar_tensor_tensor

            b = ready(dve, "vec")
            link(dve.tensor_copy(vec[:, :], b[:, 0:84]))
            release(dve.tensor_copy(convc[:, :], b[:, 84:172]), "vec")
            tt(lbd[:, :], vec[:, LB:LB + 4], vec[:, LB + 4:LB + 8], ALU.subtract).then_inc(lbd_done, 1)
            dve.wait_ge(csig_done, 1)
            tt(csilu[:, :], csig[:, :], vec[:, C_:C_ + 8], ALU.mult).then_inc(csilu_done, 1)
            dve.wait_ge(lb_done, 1)
            link(ts(oml[:, :], lb[:, :], -1.0, 1.0, ALU.mult, ALU.add))
            dve.wait_ge(rstd_done, 1)
            for t in range(TT):
                ts(xn_in[:, t, :], x_in[:, t, :], rstd[:, t:t + 1], None, ALU.mult).then_inc(xn_done, 1)
            b = ready(dve, "mod1")
            release(tt(mod[:, 0:16], b[:, 0:16], vec[:, B_ADA:B_ADA + 16], ALU.add), "mod1")
            evacuated(dve, "mod1")
            link(stt(a1[:, :], mod[:, 8:16], 1.0, vec[:, G_MIX:G_MIX + 8], ALU.add, ALU.mult))

            def make_h(which):
                a, shift, tmp = (a1, 0, h_tmp) if which == 0 else (a2, 24, h_tmp2)
                for k in range(KT):
                    b = ready(dve, ("xT", which, k))
                    release(ts(tmp[:, k % 2, :], b[:, :], a[:, k:k + 1], mod[:, shift + k:shift + k + 1], ALU.mult,
                            ALU.add), ("xT", which, k))
                    dve.wait_ge(h_hi_done, which * KT + k + 1)
                    tt(h_lo[:, k, :], tmp[:, k % 2, :], h_hi[:, k, :].bitcast(F32), ALU.subtract).then_inc(h_lo_done, 1)

            make_h(0)

            def small_results(u):
                if u == SLOT_DIAG:
                    dve.wait_ge(consts, 2)
                    link(ts(dint[:, :], dint[:, :], 3, None, ALU.bitwise_and))
                    link(ts(dist2[:, :], dint[:, :], FAR, None, ALU.mult))
                    tt(dist2[:, :], dist2[:, :], dist1[:, :], ALU.add)
                if u == 0:
                    dve.memset(scT[:, :, :], 0.0)
                if 0 < u <= MOD_SLOTS:
                    v = u - 1
                    b = ready(dve, ("mod2", v))
                    cols = slice(16 + 4 * v, 20 + 4 * v)
                    release(tt(mod[:, cols], b[:, 0:4], vec[:, cols], ALU.add), ("mod2", v))
                if u == MOD_SLOTS + 1:
                    for v in range(MOD_SLOTS):
                        evacuated(dve, ("mod2", v))
                    stt(a2[:, :], mod[:, 32:40], 1.0, vec[:, G_FFN:G_FFN + 8], ALU.add, ALU.mult)
                    link(ts(gp[:, 0:8], mod[:, 16:24], 1.0, None, ALU.add))
                    ts(gp[:, 8:16], mod[:, 40:48], 1.0, None, ALU.add).then_inc(gp_done, 1)
                if u == SLOT_DIAG + 1:
                    for h in range(HEADS):
                        b = ready(dve, ("diag", h))
                        release(dve.copy_predicated(scT[:, h, :], masks[:, LEVELS, :], b[:, :]), ("diag", h))
                if SLOT_LEVEL < u <= SLOT_LEVEL + LEVELS:
                    level_scores(u - SLOT_LEVEL - 1)
                if SLOT_LEVEL <= u < SLOT_LEVEL + LEVELS:
                    level_factors(u - SLOT_LEVEL)
                if u == SLOT_KDT:
                    dve.wait_ge(eg_done, 1)
                    link(tt(zz[0][:, :, :], hq[:, :, :], dec[:, :, :], ALU.mult))
                    pc = hp[:, :, :].rearrange("p h (c t) -> p (h c) t", t=CHUNK)
                    dc = dec[:, :, :].rearrange("p h (c t) -> p (h c) t", t=CHUNK)
                    tt(dc, pc[:, :, CHUNK - 1:CHUNK].broadcast_to([P, HEADS * NCHUNK, CHUNK]), pc, ALU.subtract).then_inc(kdif_done, 1)
                    dve.wait_ge(ke_done, 1)
                    tt(zz[1][:, :, :], hk[:, :, :], dec[:, :, :], ALU.mult).then_inc(kdec_done, 1)
                if u == SLOT_KDT + 1:
                    dve.wait_ge(kdec_done, 1)
                    for t in range(2, TT):
                        b = ready(dve, ("kdT", t))
                        release(dve.tensor_copy(kd[:, t, :], b[:, :]), ("kdT", t))
                if u == SLOT_UPD + 1:
                    states(range(4))
                if u == SLOT_UPD + 2:
                    states(range(4, NCHUNK - 1))
                if u == SLOT_O + 1:
                    for h in range(HEADS):
                        evacuated(dve, ("o", h))
                        tt(o_sq[:, h, :], o_sb[:, h, :], o_sb[:, h, :], ALU.mult).then_inc(osq_done, 1)
                if u == SLOT_SS + 1:
                    for h in range(HEADS):
                        dve.wait_ge(rs_done, h + 1)
                        stt(yh[:, h, :], o_sb[:, h, :], vec[:, G_HG + h:G_HG + h + 1], o_rs[:, h, :], ALU.mult, ALU.mult)
                for p in range(PAIRS):
                    s = U_PAIR + 3 * p + 2
                    if u == s + 1:
                        softmax_max(p)
                    if u == s + 2:
                        if p:
                            ready(dve, ("O", p - 1, 1))
                        for j in range(score_banks(p)):
                            b = ready(dve, ("T", p, 0, j))
                            n = sum(block_bank(p, i)[0] == j for i in range(len(blocks_of(p)))) * P
                            release(dve.tensor_copy(probT[:, 0, 3 * P * j:3 * P * j + n], b[:, 0:n]), ("T", p, 0, j))
                    if u == s + 3:
                        g, h0, d = pair(p)
                        b = ready(dve, ("O", p, 0))
                        release(dve.tensor_copy(og[:, g, h0, :].rearrange("p (l res) -> p res l", res=d),
                                             b[:, :].rearrange("p (res l) -> p res l", res=d)), ("O", p, 0))
                if u == SLOT_STAT + 2:
                    group_weights()
                if SLOT_BC < u <= SLOT_BC + HEADS:
                    merge_groups(u - SLOT_BC - 1)

            def level_scores(j):
                half = 1 << j
                for i in range(2):
                    b = ready(dve, ("lev", j, i))
                    dst = scT[:, 2 * i:2 * i + 2, :].rearrange("p h (blk pos tok) -> p (h blk) pos tok", pos=2, tok=half)[:, :, 1, :]
                    m = masks[:, j, :].rearrange("p (blk tok) -> p blk tok", tok=half)
                    ins = dve.copy_predicated(dst, m, b[:, :].rearrange("p (blk tok) -> p blk tok", tok=half))
                    release(ins, ("lev", j, i))

            def level_factors(j):
                half = 1 << j
                if j == 0:
                    dve.wait_ge(logf_done, 1)
                else:
                    dve.wait_ge(p_done, j)
                v = {n: t[:, :, :].rearrange("p h (blk pos tok) -> p (h blk) pos tok", pos=2, tok=half)
                     for n, t in (("p", hp), ("d", dec), ("q", hq), ("k", hk), ("z", zz[j % 2]))}
                total = v["p"][:, :, 0, half - 1:half].broadcast_to([P, HEADS * S // (2 * half), half])
                tt(v["d"][:, :, 0, :], total, v["p"][:, :, 0, :], ALU.subtract).then_inc(d1_done, 1)
                dve.wait_ge(e_done, j + 1)
                tt(v["z"][:, :, 1, :], v["q"][:, :, 1, :], v["d"][:, :, 1, :], ALU.mult)
                tt(v["z"][:, :, 0, :], v["k"][:, :, 0, :], v["d"][:, :, 0, :], ALU.mult).then_inc(z_done, 1)
                tt(v["p"][:, :, 1, :], v["p"][:, :, 1, :], total, ALU.add).then_inc(p_done, 1)

            def states(chunks):
                for c in chunks:
                    b = ready(dve, ("upd", c))
                    dst = st_a[:, c, :] if c < 4 else st_b[:, c - 4, :]
                    if c == 0:
                        dve.wait_ge(glast_done, 1)
                        ins = dve.tensor_copy(dst, b[:, :])
                    else:
                        src = st_a[:, c - 1, :] if c < 5 else st_b[:, c - 5, :]
                        for h in range(HEADS):
                            cols = slice(h * P, (h + 1) * P)
                            n = h * NCHUNK + c
                            ins = stt(dst[:, cols], src[:, cols], eglast[:, n:n + 1], b[:, cols], ALU.mult, ALU.add)
                    release(ins, ("upd", c))
                    evacuated(dve, ("upd", c))

            def softmax_max(p):
                g, h0, d = pair(p)
                if p:
                    ready(dve, ("T", p - 1, 1, score_banks(p - 1) - 1))
                for hh in range(2):
                    slope = 2.0 ** (-8.0 * (g * HEADS + h0 + hh + 1) / (NG * HEADS))
                    k = -slope * d / SCALE
                    pr = prob[:, hh, :]
                    if g == 0:
                        b = ready(dve, ("S", p, hh, 0))
                        stt(pr[:, 0:P], dist0[:, P:2 * P], k, b[:, 0:P], ALU.mult, ALU.add)
                        release(stt(pr[:, P:3 * P], dist0[:, :], k, b[:, P:3 * P], ALU.mult, ALU.add), ("S", p, hh, 0))
                        b = ready(dve, ("S", p, hh, 1))
                        for i in range(2):
                            ins = stt(pr[:, (3 + 2 * i) * P:(5 + 2 * i) * P], dist0[:, :], k,
                                      b[:, 2 * i * P:(2 * i + 2) * P], ALU.mult, ALU.add)
                        release(ins, ("S", p, hh, 1))
                        evacuated(dve, ("S", p, hh, 1))
                        dve.tensor_reduce(mx[:, 4 * hh:4 * hh + 1], pr[:, 0:P], AX_X, ALU.max)
                        link(dve.tensor_reduce(mx[:, 4 * hh + 1:4 * hh + 4],
                                               pr[:, P:7 * P].rearrange("p (q k) -> p q k", q=3), AX_X, ALU.max))
                    else:
                        dist = dist1 if g == 1 else dist2
                        b = ready(dve, ("S", p, hh, 0))
                        for i in range(TT):
                            tok = slice(i * P, (i + 1) * P)
                            ins = stt(pr[:, tok], dist[:, :], k, b[:, tok], ALU.mult, ALU.add)
                        release(ins, ("S", p, hh, 0))
                        evacuated(dve, ("S", p, hh, 0))
                        link(dve.tensor_reduce(mx[:, 4 * hh:4 * hh + 4],
                                               pr[:, 0:4 * P].rearrange("p (q k) -> p q k", q=4), AX_X, ALU.max))
                    cols = slice(g * TT * HEADS + h0 + hh, (g + 1) * TT * HEADS, HEADS)
                    ts(nmax[:, cols], mx[:, 4 * hh:4 * hh + 4], -SCALE, None, ALU.mult).then_inc(nmax_done, 1)

            def group_weights():
                for g in range(NG):
                    evacuated(dve, ("mT", g))
                link(tt(inv[:, :], m_row[:, 0, :], m_row[:, 1, :], ALU.min))
                link(tt(inv[:, :], inv[:, :], m_row[:, 2, :], ALU.min))
                for g in range(NG):
                    ins = tt(m_row[:, g, :], inv[:, :], m_row[:, g, :], ALU.subtract)
                ins.then_inc(mdiff_done, 1)
                dve.wait_ge(wexp_done, 1)
                for g in range(NG):
                    evacuated(dve, ("sT", g))
                link(tt(s_row[:, :, :], s_row[:, :, :], m_row[:, :, :], ALU.mult))
                link(tt(inv[:, :], s_row[:, 0, :], s_row[:, 1, :], ALU.add))
                link(tt(inv[:, :], inv[:, :], s_row[:, 2, :], ALU.add))
                link(dve.reciprocal(inv[:, :], inv[:, :]))
                for g in range(NG):
                    tt(m_row[:, g, :], m_row[:, g, :], inv[:, :], ALU.mult).then_inc(crow_done, 1)

            def merge_groups(h):
                for g in range(NG):
                    b = ready(dve, ("bc", h, g))
                    release(tt(og[:, g, h, :], og[:, g, h, :], b[:, :], ALU.mult), ("bc", h, g))
                for g in range(NG):
                    evacuated(dve, ("bc", h, g))
                link(tt(og[:, 0, h, :], og[:, 0, h, :], og[:, 1, h, :], ALU.add))
                tt(og[:, 0, h, :], og[:, 0, h, :], og[:, 2, h, :], ALU.add).then_inc(ybfull_done, 1)
                dve.wait_ge(ybhi_done, h + 1)
                tt(yb_lo[:, h, :], og[:, 0, h, :], yb_hi[:, h, :].bitcast(F32), ALU.subtract).then_inc(yblo_done, 1)

            def evacuate(u):
                if u < U_HF:
                    for t in range(2):
                        h = 2 * u + t
                        dve.wait_ge(sig_done, h + 1)
                        b = ready(dve, ("g", u, t))
                        release(tt(hq[:, h, :], b[:, :], dec[:, h, :], ALU.mult), ("g", u, t))
                elif u < U_HI:
                    for t in range(2):
                        h = 2 * (u - U_HF) + t
                        evacuated(dve, ("g", u, t))
                        link(ts(hp[:, h, :], dec[:, h, :], oml[:, h:h + 1], lb[:, h:h + 1], ALU.mult, ALU.add))
                        ts(hk[:, h, :], hp[:, h, :], -1.0, 1.0, ALU.mult, ALU.add).then_inc(f_done, 1)
                elif u < U_PAIR:
                    for t in range(TT):
                        b = ready(dve, ("g", u, t))
                        c0 = 256 * (u - U_HI)
                        release(dve.tensor_copy(hv[:, t, c0:c0 + 256], b[:, 0:256]), ("g", u, t))
                elif u < U_HG:
                    p, what = divmod(u - U_PAIR, 3)
                    g, h0, d = pair(p)
                    if what == 1:
                        for t in range(2):
                            b = ready(dve, ("g", u, t))
                            release(dve.tensor_copy(ka[:, t, :].rearrange("p (res l) -> p res l", res=d),
                                                 b[:, :].rearrange("p (l res) -> p res l", res=d)), ("g", u, t))
                    if what == 2:
                        if p:
                            ready(dve, ("O", p - 1, 1))
                        for t in range(TT):
                            b = ready(dve, ("g", u, t))
                            release(dve.tensor_copy(va[:, t, :], b[:, 0:256]), ("g", u, t))
                elif u < U_GA:
                    for t in range(2):
                        h = 2 * (u - U_HG) + t
                        dve.wait_ge(sig_done, HEADS + h + 1)
                        b = ready(dve, ("g", u, t))
                        release(tt(sgt[:, h % 2, :], b[:, :], sgt[:, h % 2, :], ALU.mult), ("g", u, t))
                        evacuated(dve, ("g", u, t))
                        tt(yh[:, h, :], yh[:, h, :], sgt[:, h % 2, :], ALU.mult).then_inc(yfull_done, 1)
                    for t in range(2):
                        h = 2 * (u - U_HG) + t
                        dve.wait_ge(yahi_done, h + 1)
                        tt(ya_lo[:, h, :], yh[:, h, :], ya_hi[:, h, :].bitcast(F32), ALU.subtract).then_inc(yalo_done, 1)
                elif U_A <= u < U_B:
                    for t in range(4):
                        f = 4 * (u - U_A) + t
                        if t == 0 and u == U_A:
                            for v in range(U_GA, U_A):
                                for i in range(2):
                                    evacuated(dve, ("g", v, i))
                        b = ready(dve, ("g", u, t))
                        release(tt(sga[:, f, :], sga[:, f, :], b[:, :], ALU.mult), ("g", u, t))
                elif U_B <= u < U_OUT:
                    for t in range(4):
                        f = 4 * (u - U_B) + t
                        b = ready(dve, ("g", u, t))
                        release(tt(sgb[:, f, :], sgb[:, f, :], b[:, :], ALU.mult), ("g", u, t))
                        evacuated(dve, ("g", u, t))
                        tt(sgb[:, f, :], sgb[:, f, :], sga[:, f, :], ALU.add).then_inc(mfull_done, 1)
                        dve.wait_ge(mhi_done, f + 1)
                        tt(m_lo[:, f, :], sgb[:, f, :], m_hi[:, f, :].bitcast(F32), ALU.subtract).then_inc(mlo_done, 1)
                elif u >= U_OUT:
                    if u == U_OUT:
                        dve.wait_ge(x_again, 16)
                        for i in range(2):
                            evacuated(dve, ("row", 0, i))
                    c0 = 256 * (u - U_OUT)
                    cols = slice(c0, c0 + 256)
                    for t in range(TT):
                        b = ready(dve, ("g", u, t))
                        tmp = sgb[:, t, 0:256]
                        release(tt(tmp, b[:, 0:256], g1_row[:, cols], ALU.mult), ("g", u, t))
                        evacuated(dve, ("g", u, t))
                        tt(x1[:, t, cols], x1[:, t, cols], tmp, ALU.add).then_inc(x1_done, 1)

            for u in range(U_UP):
                small_results(u)
                evacuate(u)

            for t in range(TT):
                dve.wait_ge(rstd_done, 2 + t)
                ts(xn_ffn[:, t, :], x1[:, t, :], rstd[:, TT + t:TT + t + 1], None, ALU.mult).then_inc(xn_done, 1)
            make_h(1)

            CW = convc[:, :]
            with dve.Fori(0, FT // 2) as i:
                for t in range(2):
                    dve.wait_ge(conv0_done, 2 * i + t + 1)
                    tt_ = conv[:, t, 1:S]
                    stt(tt_, bank[t][:, 0:S - 1], CW[:, bass.ds(2 * i + (FT + t), 1)], tt_, ALU.mult,
                        ALU.add).then_inc(tap_done, 1)
                    dve.wait_ge(tap_done, 2 * i + t + 1)
                    tt_ = conv[:, t, 2:S]
                    stt(tt_, bank[t][:, 0:S - 2], CW[:, bass.ds(2 * i + t, 1)], tt_, ALU.mult,
                        ALU.add).then_inc(free[t], 1)
                for t in range(2):
                    bk, n = BANKS[f"val{t}"]
                    dve.wait_ge(full[bk], i + (n + 1))
                    dve.wait_ge(gelu_done, 2 * i + t + 1)
                    tt(gelu[:, t, :], gelu[:, t, :], bank[bk][:, :], ALU.mult).then_inc(free[bk], 1)
                for t in range(2):
                    dve.wait_ge(ahi_done, 2 * i + t + 1)
                    hi = act_hi[:, bass.ds(2 * i + t, 1), :].rearrange("p a s -> p (a s)")
                    lo = act_lo[:, bass.ds(2 * i + t, 1), :].rearrange("p a s -> p (a s)")
                    tt(lo, gelu[:, t, :], hi.bitcast(F32), ALU.subtract).then_inc(alo_done, 1)

            dve.wait_ge(gf_in, 16)
            for i in range(2):
                evacuated(dve, ("row", 1, i))
            for t in range(TT):
                for half in range(2):
                    cols = slice(512 * half, 512 * half + 512)
                    b = ready(dve, ("y", t, half))
                    link(tt(gelu[:, half, :], b[:, :], g2_row[:, cols], ALU.mult))
                    ins = tt(x1[:, t, cols], x1[:, t, cols], gelu[:, half, :], ALU.add)
                ins.then_inc(x2_done, 1)
            for t in range(TT):
                dve.wait_ge(rstd_done, 2 + TT + t)
                stt(x1[:, t, :], x1[:, t, :], rstd[:, 2 * TT + t:2 * TT + t + 1], gf_row[:, :], ALU.mult,
                    ALU.mult).then_inc(y_done, 1)


_INS = ["x", "c", "w_ada", "b_ada", "g_norm_mix", "w_in", "lb_logits", "g_hg_norm", "w_branch_a", "w_branch_b",
        "w_out", "g_norm_ffn", "w_up", "conv_w", "conv_b", "w_down", "g_final"]
_OUT = ((1, 512, 1024), "float32")


def kernel(**inputs):
    import concourse.bacc as _bacc
    from concourse.bass_utils import run_bass_kernel_spmd as _run

    nc = _bacc.Bacc("TRN2", target_bir_lowering=False, num_devices=1)
    arrays, args = {}, []
    for name in _INS:
        a = np.ascontiguousarray(inputs[name])
        arrays[f"in_{name}_dram"] = a
        args.append(nc.dram_tensor(f"in_{name}_dram", a.shape, mybir.dt.from_np(a.dtype), kind="ExternalInput").ap())
    shape, dtype = _OUT
    args.append(nc.dram_tensor("out_dram", shape, mybir.dt.from_np(np.dtype(dtype)), kind="ExternalOutput").ap())
    layer_kernel(nc, *args)
    r = _run(nc, [arrays], core_ids=[0])
    return r.results[0]["out_dram"]
```

```python
from contextlib import ExitStack

import numpy as np

import concourse.bass as bass
from concourse import mybir

F32 = mybir.dt.float32
F32R = mybir.dt.float32r
I8 = mybir.dt.int8
ALU = mybir.AluOpType
ACT = mybir.ActivationFunctionType
AX_X = mybir.AxisListType.X

P = 128
D = 1024
S = 512
KT = D // P
TT = S // P
HEADS = 4
E_DIM = 128
CHUNK = 64
NCHUNK = S // CHUNK
HW = HEADS * 128
GROUPS = ((128, 1), (512, 4), (2048, 16))
NG = len(GROUPS)
ORDER = tuple(min(d, 4) for _, d in GROUPS)
D_FF = 2816
FT = D_FF // P
EPS = 1e-6
SCALE = float(E_DIM) ** -0.5
FAR = 1e36
KB = 1024

PAIRS = 2 * NG
U_HQ, U_HF, U_HI = 0, 2, 4
U_PAIR = 6
U_HG = U_PAIR + 3 * PAIRS
U_GA = U_HG + 2
U_GB = U_GA + 4
U_A = U_GB + 4
U_B = U_A + 2
U_OUT = U_B + 2
U_UP = U_OUT + 4
U_DOWN = U_UP + FT
N_UNITS = U_DOWN + FT // 2
C_HG, C_AQ = 3 * HW, 4 * HW
C_AK, C_AV = C_AQ + NG * HW, C_AQ + 2 * NG * HW
C_GATES = C_AQ + 3 * NG * HW

LEVELS = 6
SLOT_DIAG = 4
SLOT_LEVEL = 6
SLOT_KDT, SLOT_UPD, SLOT_O, SLOT_SS = 12, 13, 15, 16
SLOT_STAT = U_PAIR + 3 * PAIRS + 2
SLOT_BC = SLOT_STAT + 3
SLOT_ROW = U_A
MOD_FIRST = 8
MOD_KTS = 5
START = (("ada", 0), ("ada", 4), ("unit", 0), ("ada", 1), ("h", 0), ("ada", 5), ("unit", 1), ("ada", 2), ("h", 1), ("ada", 6), ("ada", 3), ("h", 2), ("ada", 7), ("h", 3), ("unit", 2))
MOD_SLOT, MOD_TWICE = 17, (19, 20, 22, 23, 26)
MOD_UNITS = {}
for _u in range(MOD_SLOT, MOD_SLOT + 11):
    _n = MOD_FIRST + sum(len(v) for v in MOD_UNITS.values())
    MOD_UNITS[_u] = tuple(range(_n, _n + (2 if _u in MOD_TWICE else 1)))

START_ADA = [n for step, n in START if step == "ada"]


def pair(p):
    g = p // 2
    return g, 2 * (p % 2), ORDER[g]


def score_banks(p):
    return 2 if p // 2 == 0 else 1


def plan_banks():
    uses, table, turn = [0] * 8, {}, {"gemm": 0, "small": 0, "start": 0, "fourth": 0}

    def use(name, pool):
        banks = {"gemm": (0, 1, 2), "small": (3, 4, 5, 6, 7), "start": (3, 4, 5, 6), "fourth": (7,)}[pool]
        b = banks[turn[pool] % len(banks)]
        turn[pool] += 1
        table[name] = (b, uses[b])
        uses[b] += 1

    use("vec", "start")
    for k in range(2):
        use(("xT", 0, k), "start")
    for j in range(KT // 2):
        use(("mod1", j), "start")
        if j < KT // 2 - 1:
            for k in (2 * j + 2, 2 * j + 3):
                use(("xT", 0, k), "start")
    for u, t, pool in ((0, 0, "gemm"), (0, 1, "gemm"), (1, 0, "gemm"), (1, 1, "fourth")):
        use(("g", u, t), pool)
    for u in range(U_UP):
        if u >= 2:
            for t in range(tiles_of(u)):
                use(("g", u, t), "gemm")
        for name in small_products(u):
            use(name, "small")
    for k in range(KT):
        use(("xT", 1, k), "small")
    base = list(uses)
    for i, name in enumerate(("gate0", "gate1", "val0", "val1")):
        table[name] = (i, base[i])
        uses[i] += FT // 2
    for b in range(8):
        table[("y", b // 2, b % 2)] = (b, uses[b])
    return table


def tiles_of(u):
    if U_HI <= u < U_PAIR or (U_PAIR <= u < U_HG and (u - U_PAIR) % 3 == 2) or U_A <= u < U_UP:
        return 4
    return 2


def small_products(u):
    names = []
    if u == SLOT_DIAG:
        names += [("diag", h) for h in range(HEADS)]
    if SLOT_LEVEL <= u < SLOT_LEVEL + LEVELS:
        names += [("lev", u - SLOT_LEVEL, h) for h in range(HEADS)]
    if u == SLOT_KDT:
        names += [("kdT", t) for t in range(TT)]
    if u == SLOT_UPD:
        names += [("upd", c) for c in range(4)]
    if u == SLOT_UPD + 1:
        names += [("upd", c) for c in range(4, NCHUNK - 1)]
    if u == SLOT_O:
        names += [("o", h) for h in range(HEADS)]
    if u == SLOT_SS:
        names += [("ss", h) for h in range(HEADS)]
    for p in range(PAIRS):
        s = U_PAIR + 3 * p + 2
        if u == s:
            names += [("S", p, hh, j) for hh in range(2) for j in range(score_banks(p))]
        if u == s + 1:
            names += [("T", p, hh, j) for hh in range(2) for j in range(score_banks(p))]
        if u == s + 2:
            names += [("O", p, hh) for hh in range(2)]
    if u == SLOT_STAT:
        names += [("mT", g) for g in range(NG)]
    if u == SLOT_STAT + 1:
        names += [("sT", g) for g in range(NG)]
    if SLOT_BC <= u < SLOT_BC + HEADS:
        names += [("bc", u - SLOT_BC, g) for g in range(NG)]
    if u in (SLOT_ROW, SLOT_ROW + 1):
        names += [("row", u - SLOT_ROW, i) for i in range(2)]
    if u in MOD_UNITS:
        names.append(("mod2", u))
    return names


BANKS = plan_banks()

BLOCKS0 = [(0, 0), (1, 0), (1, 1), (2, 1), (2, 2), (3, 2), (3, 3)]
BLOCKS1 = [(i, i) for i in range(TT)]


def blocks_of(p):
    return BLOCKS0 if p // 2 == 0 else BLOCKS1


def block_bank(p, n):
    if p // 2 == 0:
        return (0, n * P) if n < 3 else (1, (n - 3) * P)
    return 0, n * P


def layer_kernel(nc, x, c, w_ada, b_ada, g_norm_mix, w_in, lb_logits, g_hg_norm, w_branch_a, w_branch_b, w_out,
                 g_norm_ffn, w_up, conv_w, conv_b, w_down, g_final, out):
    with ExitStack() as ctx:
        BASE = 16512

        def at(name, kb, shape, dt=F32):
            return nc.alloc_sbuf_tensor_at(name, shape, dt, offset=BASE + int(kb * KB))

        raw = [at(f"w_raw{i}", 120 + 8 * i, [P, 2048]) for i in range(2)]
        whi = [at(f"w_hi{i}", 136 + 8 * i, [P, 2048], F32R) for i in range(2)]
        wlo = [at(f"w_lo{i}", 152 + 8 * i, [P, 2048], F32R) for i in range(2)]
        whi.append(at("w_hi_2", 64, [P, 2048], F32R))
        wlo.append(at("w_lo_2", 72, [P, 2048], F32R))
        h_hi = at("h_hi", 168, [P, KT, S], F32R)
        h_lo = at("h_lo", 184, [P, KT, S], F32R)

        x_in = at("x_in", 0, [P, TT, D])
        xn_in = at("xn_in", 16, [P, TT, D])
        ada = [at(f"ada{i}", 32 + 8 * i, [P, KT, 256]) for i in range(MOD_FIRST)]
        part = at("part", 96, [P, 4, 256])
        h_tmp = at("h_tmp", 100, [P, 4, S])
        hq = at("hq", 0, [P, HEADS, S])
        hk = at("hk", 8, [P, HEADS, S])
        hp = at("hp", 16, [P, HEADS, S])
        hv = at("hv", 24, [P, TT, HW])
        dec = at("dec", 32, [P, HEADS, S])
        zz = [at("z0", 40, [P, HEADS, S]), at("z1", 48, [P, HEADS, S])]
        scT = at("scT", 56, [P, HEADS, S])
        kd = at("kd", 8, [P, TT, HW])
        st_a = at("st_a", 16, [P, 4, HW])
        st_b = at("st_b", 32, [P, 3, HW])
        o_sb = at("o_sb", 8, [P, HEADS, S])
        o_sq = at("o_sq", 48, [P, HEADS, S])
        o_rs = at("o_rs", 0, [P, HEADS, S])
        yh = at("yh", 32, [P, HEADS, S])
        sgt = at("sgt", 56, [P, 2, S])
        ya_hi = at("ya_hi", 40, [P, HEADS, S], F32R)
        ya_lo = at("ya_lo", 48, [P, HEADS, S], F32R)
        qa = at("qa", 64, [P, 2, S])
        ka = at("ka", 68, [P, 2, S])
        va = at("va", 72, [P, TT, 256])
        prob = at("prob", 76, [P, 2, 7 * P])
        probT = at("probT", 83, [P, 2, 7 * P])
        og = at("og", 90, [P, NG, HEADS, S])
        m_row = at("m_row", 32, [HEADS, NG, S])
        s_row = at("s_row", 56, [HEADS, NG, S])
        yb_hi = at("yb_hi", 64, [P, HEADS, S], F32R)
        yb_lo = at("yb_lo", 76, [P, HEADS, S], F32R)
        sga = at("sga", 0, [P, KT, S])
        sgb = at("sgb", 16, [P, KT, S])
        m_hi = at("m_hi", 90, [P, KT, S], F32R)
        m_lo = at("m_lo", 32, [P, KT, S], F32R)
        x1 = at("x1", 48, [P, TT, D])
        g1_row = at("g1_row", 72, [P, D])
        g2_row = at("g2_row", 112, [P, D])
        gf_row = at("gf_row", 108, [P, D])
        xn_ffn = at("xn_ffn", 0, [P, TT, D])
        h_tmp2 = [at("h_tmp2a", 116, [P, 2, S]), at("h_tmp2b", 44, [P, 2, S])]
        act_hi = at("act_hi", 0, [P, FT, S], F32R)
        act_lo = at("act_lo", 64, [P, FT, S], F32R)
        conv = at("conv", 44, [P, 2, S])
        gelu = at("gelu", 116, [P, 2, S])
        squares = at("squares", 184, [P, TT, D])
        masks = at("masks", 116, [P, LEVELS, S // 2], I8)
        diag = at("diag", 118, [P, S], I8)
        ada2 = [at(f"ada2_{i}", 16 + 8 * i, [P, KT, 256]) for i in range(2)]
        part2 = [at(f"part2_{i}", kb, [P, 256]) for i, kb in enumerate((78, 81.5, 85, 88.5))]
        off = 200.0

        def small(name, cols, rows=P, dt=F32):
            nonlocal off
            t = at(name, off, [rows, cols], dt)
            off += -(-cols * 4 // 32) * 32 / KB
            return t

        ident = small("ident", P)
        ones = small("ones", P)
        dist0 = small("dist0", 2 * P)
        dist1 = small("dist1", P)
        dist2 = small("dist2", P)
        dint = at("dint", 119, [P, P], mybir.dt.int32)
        vec_rows = small("vec_rows", P, 84)
        conv_rows = small("conv_rows", P, 88)
        vec = small("vec", 84)
        convc = small("convc", 88)
        mod = small("mod", 48)
        csig = small("csig", 8)
        csilu = small("csilu", 8)
        lbd = small("lbd", 4)
        lb = small("lb", 4)
        oml = small("oml", 4)
        a1 = small("a1", 8)
        a2 = small("a2", 8)
        gp = small("gp", 16)
        ssq = small("ssq", 12)
        ssp = small("ssp", 16)
        rstd = small("rstd", 12)
        nmax = small("nmax", 48)
        ssum = small("ssum", 48)
        mx = small("mx", 8)
        eglast = small("eglast", 32)
        epsc = small("epsc", 1)
        mhalf = small("mhalf", 4)
        inv = at("inv", 62, [HEADS, S])
        assert BASE + off * KB <= nc.sbuf_usable_end, off
        B_ADA, G_MIX, G_FFN, G_HG, LB, C_ = 0, 48, 56, 64, 68, 76

        bank = [ctx.enter_context(nc.psum_tensor(f"bank{i}", [P, 512], F32)) for i in range(8)]

        def sem(name):
            return ctx.enter_context(nc.semaphore(name))

        full = [sem(f"bank_full{b}") for b in range(8)]
        free = [sem(f"bank_free{b}") for b in range(8)]
        raw_in = [sem(f"raw_in{i}") for i in range(2)]
        hi_done = sem("hi_done")
        lo_done = sem("lo_done")
        down_used = sem("down_used")
        x_in_s = [sem(f"x_landed{t}") for t in range(TT)]
        x_again = sem("x_again")
        vec_in = sem("vec_in")
        ada_in = [sem(f"ada_in{i}") for i in range(MOD_FIRST)]
        ada2_in = [sem(f"ada2_in{i}") for i in range(2)]
        part_done = sem("part_done")
        scaled_done = sem("scaled_done")
        rest_done = sem("rest_done")
        mod1_done = sem("mod1_done")
        part_chain = [sem("part_chain0"), sem("part_chain1")]
        gf_in = sem("gf_in")
        masks_done = sem("masks_done")
        consts = sem("consts")
        dchain = sem("dve_chain")
        glast_done = sem("glast_done")
        pchain = sem("pool_chain")
        csig_done, csilu_done, lbd_done = sem("csig_done"), sem("csilu_done"), sem("lbd_done")
        lb_done = sem("lb_done")
        sq_done = sem("sq_done")
        rstd_done = sem("rstd_done")
        xn_done = [sem("xn_act"), sem("xn_dve")]
        h_hi_done = sem("h_hi_done")
        h_lo_done = [sem("h_lo_even"), sem("h_lo_odd")]
        ssp_done = sem("ssp_done")
        ssq_done = sem("ssq_done")
        sig_done = sem("sig_done")
        f_done, logf_done = sem("f_done"), sem("logf_done")
        d1_done, e_done, z_done, p_done = sem("d1_done"), sem("e_done"), sem("z_done"), sem("p_done")
        eg_done, kdif_done, ke_done, kdec_done = sem("eg_done"), sem("kdif_done"), sem("ke_done"), sem("kdec_done")
        osq_done, rs_done, yfull_done, yahi_done, yalo_done = (
            sem("osq_done"), sem("rs_done"), sem("yfull_done"), sem("yahi_done"), sem("yalo_done"))
        nmax_done, prob_done = sem("nmax_done"), sem("prob_done")
        mdiff_done, wexp_done, crow_done = sem("mdiff_done"), sem("wexp_done"), sem("crow_done")
        ybfull_done, ybhi_done, yblo_done = sem("ybfull_done"), sem("ybhi_done"), sem("yblo_done")
        mfull_done, mhi_done, mlo_done = sem("mfull_done"), sem("mhi_done"), sem("mlo_done")
        gp_done, x1_done = sem("gp_done"), sem("x1_done")
        conv0_done, tap_done, gelu_done, ahi_done, alo_done = (
            sem("conv0_done"), sem("tap_done"), sem("gelu_done"), sem("ahi_done"), sem("alo_done"))
        x2_done, y_done, out_done = sem("x2_done"), sem("y_done"), sem("out_done")

        def claim(eng, name):
            b, n = BANKS[name]
            if n:
                eng.wait_ge(free[b], n)
            return bank[b]

        def filled(ins, name):
            ins.then_inc(full[BANKS[name][0]], 1)

        def ready(eng, name):
            b, n = BANKS[name]
            eng.wait_ge(full[b], n + 1)
            return bank[b]

        def release(ins, name):
            ins.then_inc(free[BANKS[name][0]], 1)

        def evacuated(eng, name):
            b, n = BANKS[name]
            eng.wait_ge(free[b], n + 1)

        def scaled_before(n):
            return START_ADA.index(n) * (KT - MOD_KTS)

        def h_part(which, k):
            return h_tmp[:, k % 4, :] if which == 0 else h_tmp2[k // 2 % 2][:, k % 2, :]

        def cols_of(w, c0):
            return w[0][:, bass.ds(c0, 256)].rearrange("(k p) c -> p k c", p=P)

        def unit_source(u):
            if u < U_PAIR:
                return cols_of(w_in, 256 * u)
            if u < U_HG:
                p, what = divmod(u - U_PAIR, 3)
                return cols_of(w_in, (C_AQ, C_AK, C_AV)[what] + 256 * p)
            if u < U_GA:
                return cols_of(w_in, C_HG + 256 * (u - U_HG))
            if u < U_A:
                return cols_of(w_in, C_GATES + 256 * (u - U_GA))
            if u < U_OUT:
                w, j = (w_branch_a, u - U_A) if u < U_B else (w_branch_b, u - U_B)
                return w[0][:, 512 * j:512 * j + 512].rearrange("(k p) c -> p k c", p=P)
            return cols_of(w_out, 256 * (u - U_OUT))

        x_tok = x[0].rearrange("(t p) d -> p t d", p=P)
        out_tok = out[0].rearrange("(t p) d -> p t d", p=P)

        block = ctx.enter_context(nc.Block())

        @block.sync
        def _(sp):
            def rows(dst, r0, src, n):
                sp.dma_start(dst[r0:r0 + n, :], src).then_inc(vec_in, 16)

            rows(vec_rows, C_, c.rearrange("b (k p) -> (b k) p", p=P), 8)
            rows(vec_rows, B_ADA, b_ada.rearrange("l (k p) -> (l k) p", p=P), 48)
            rows(vec_rows, G_MIX, g_norm_mix.rearrange("l (k p) -> (l k) p", p=P), 8)
            rows(vec_rows, G_FFN, g_norm_ffn.rearrange("l (k p) -> (l k) p", p=P), 8)
            rows(vec_rows, G_HG, g_hg_norm.rearrange("l h p -> (l h) p"), 4)
            rows(vec_rows, LB, lb_logits.rearrange("l (k p) -> (l k) p", p=P), 8)
            rows(conv_rows, 0, conv_w.rearrange("l j (k p) -> (l j k) p", p=P), 66)
            rows(conv_rows, 66, conv_b.rearrange("l (k p) -> (l k) p", p=P), 22)
            def load_unit(u, src, slot):
                if not isinstance(u, int) or u >= 2:
                    sp.wait_ge(hi_done, u - 1)
                    sp.wait_ge(lo_done, u - 1)
                width = src.shape[2]
                sp.dma_start(raw[slot][:, :].rearrange("p (k c) -> p k c", c=width), src).then_inc(raw_in[slot], 16)

            for t in range(TT):
                sp.dma_start(x_in[:, t, :], x_tok[:, t, :]).then_inc(x_in_s[t], 16)
            for step, n in START:
                if step == "ada":
                    sp.dma_start(ada[n][:, :, :], cols_of(w_ada, 256 * n)).then_inc(ada_in[n], 16)
                if step == "unit":
                    load_unit(n, unit_source(n), n % 2)
            for u in range(U_UP):
                if u == U_B + 2:
                    ready(sp, ("g", U_B - 1, 3))
                    sp.wait_ge(yblo_done, HEADS)
                    sp.dma_start(x1[:, :, :], x_tok).then_inc(x_again, 16)
                    sp.dma_start(gf_row[:, :], g_final.rearrange("(a d) -> a d", a=1).broadcast_to([P, D])).then_inc(gf_in, 16)
                if u >= 3:
                    load_unit(u, unit_source(u), u % 2)
                if u == MOD_SLOT:
                    ready(sp, ("o", HEADS - 1))
                for n in MOD_UNITS.get(u, ()):
                    if n >= MOD_FIRST + 2:
                        sp.wait_ge(part_done, n - 1)
                    sp.dma_start(ada2[n % 2][:, :, :], cols_of(w_ada, 256 * n)).then_inc(ada2_in[n % 2], 16)
            with sp.Fori(0, FT // 2) as i:
                load_unit(2 * i + U_UP, cols_of(w_up, i * 256), 0)
                load_unit(2 * i + U_UP + 1, cols_of(w_up, i * 256 + D_FF), 1)

            def down_rows(i):
                return w_down[0][bass.ds(i * 256, 256), :].rearrange("(k p) c -> p k c", p=P)

            with sp.Fori(0, FT // 4) as i:
                load_unit(2 * i + U_DOWN, down_rows(2 * i), 0)
                load_unit(2 * i + U_DOWN + 1, down_rows(2 * i + 1), 1)
            load_unit(N_UNITS - 1, down_rows(FT // 2 - 1), 0)

            for t in range(TT):
                sp.wait_ge(y_done, t + 1)
                sp.dma_start(out_tok[:, t, :], x1[:, t, :]).then_inc(out_done, 16)
            sp.wait_ge(out_done, 16 * TT)

        @block.gpsimd
        def _(pool):
            n_chain = [0]

            def link(ins):
                n_chain[0] += 1
                ins.then_inc(pchain, 1)
                pool.wait_ge(pchain, n_chain[0])

            def select(t, pattern, base, mult, op=ALU.is_ge, fill=0.0):
                link(pool.affine_select(out=t, in_=t, compare_op=op, fill=fill, base=base, pattern=pattern,
                                        channel_multiplier=mult))

            link(pool.memset(ident[:, :], 0.0))
            select(ident[:, :], [[-1, P]], 0, 1, ALU.not_equal, 1.0)
            link(pool.memset(ones[:, :], 1.0))
            link(pool.memset(mhalf[:, :], -0.5))
            pool.memset(epsc[:, :], EPS).then_inc(consts, 1)

            def inverse_root(first, n):
                cols = slice(first, first + n)
                link(pool.tensor_scalar(rstd[:, cols], ssq[:, cols], 1.0 / D, EPS, ALU.mult, ALU.add))
                pool.tensor_tensor(rstd[:, cols], rstd[:, cols], mhalf[:, 0:n], ALU.pow).then_inc(rstd_done, 1)

            def build_distances():
                link(pool.memset(diag[:, :], 1.0))
                select(diag[:, :].rearrange("p (a t) -> p a t", a=4), [[0, 4], [1, P]], 0, -1, ALU.is_equal)
                for dist, n in ((dist0, 2), (dist1, 1)):
                    link(pool.iota(dist[:, :], [[-1, n * P]], base=(n - 1) * P, channel_multiplier=1,
                                   allow_small_or_imprecise_dtypes=True))
                    select(dist[:, :], [[-1, n * P]], (n - 1) * P, 1, fill=FAR)
                    if n == 2:
                        select(dist[:, :], [[1, n * P]], 0, -1, fill=FAR)
                pool.iota(dint[:, :], [[-1, P]], base=P, channel_multiplier=1).then_inc(consts, 1)

            def build_masks(levels):
                for j in levels:
                    half = 1 << j
                    nb = P // (2 * half)
                    m = masks[:, j, :].rearrange("p (rep blk tok) -> p rep blk tok", rep=4, blk=nb)
                    link(pool.memset(masks[:, j, :], 1.0))
                    select(m, [[0, 4], [-2 * half, nb], [0, half]], 0, 1)
                    pool.affine_select(out=m, in_=m, compare_op=ALU.is_ge, fill=0.0, base=half - 1,
                                       pattern=[[0, 4], [2 * half, nb], [0, half]],
                                       channel_multiplier=-1).then_inc(masks_done, 1)

            pool.wait_ge(sq_done, TT)
            inverse_root(0, TT)

            def low_h(which, k):
                pool.wait_ge(h_hi_done, which * KT + k + 1)
                pool.tensor_tensor(h_lo[:, k, :], h_part(which, k), h_hi[:, k, :].bitcast(F32),
                                   ALU.subtract).then_inc(h_lo_done[1], 1)

            def low_part(u, slot, parts=None):
                parts = slot if parts is None else parts
                pool.wait_ge(hi_done, u + 1)
                pool.tensor_tensor(wlo[parts][:, :], raw[slot][:, :], whi[parts][:, :].bitcast(F32),
                                   ALU.subtract).then_inc(lo_done, 1)

            for step, n in START:
                if step == "ada":
                    unit = ada[n]
                    for k in range(MOD_KTS + 1, KT):
                        pool.wait_ge(scaled_done, scaled_before(n) + k - MOD_KTS + 1)
                        ins = pool.tensor_tensor(unit[:, MOD_KTS, :], unit[:, MOD_KTS, :], unit[:, k, :], ALU.add)
                        if k < KT - 1:
                            link(ins)
                    ins.then_inc(rest_done, 1)
                if step == "unit" and n == 1:
                    pool.wait_ge(lo_done, 1)
                    low_part(1, 1)
                if step == "h":
                    low_h(0, 2 * n + 1)
            low_part(2, 0, parts=2)
            build_distances()
            for u in range(3, 6):
                low_part(u, u % 2)
                build_masks((2 * u - 6, 2 * u - 5))
            with pool.Fori(0, U_UP // 2 - 3) as i:
                low_part(2 * i + 6, 0)
                low_part(2 * i + 7, 1)
            low_part(U_UP, 0)
            pool.wait_ge(ssq_done, 1)
            inverse_root(TT, TT)
            low_part(U_UP + 1, 1)
            for k in range(1, KT, 2):
                low_h(1, k)
            with pool.Fori(0, (N_UNITS - U_UP) // 2 - 1) as i:
                low_part(2 * i + U_UP + 2, 0)
                low_part(2 * i + U_UP + 3, 1)
            low_part(N_UNITS - 1, 0)
            for t in range(TT):
                pool.wait_ge(sq_done, TT + 1 + t)
                inverse_root(2 * TT + t, 1)

        @block.scalar
        def _(act):
            def high_part(slot, landed, parts=None):
                act.wait_ge(raw_in[slot], landed)
                parts = slot if parts is None else parts
                act.activation(whi[parts][:, :], raw[slot][:, :], ACT.Copy).then_inc(hi_done, 1)

            def unit_high(u):
                if u > U_DOWN + 1:
                    act.wait_ge(down_used, u - 1 - U_DOWN)
                elif u == 2:
                    act.wait_ge(part_done, 4)
                elif u > 2:
                    ready(act, ("g", u - 2, tiles_of(u - 2) - 1))
                high_part(u % 2, 16 * (u // 2 + 1), 2 if u == 2 else None)

            evacuated(act, "vec")
            act.activation(csig[:, :], vec[:, C_:C_ + 8], ACT.Sigmoid).then_inc(csig_done, 1)
            act.wait_ge(lbd_done, 1)
            act.activation(lb[:, :], lbd[:, :], ACT.Sigmoid).then_inc(lb_done, 1)
            for t in range(TT):
                act.wait_ge(x_in_s[t], 16)
                act.activation(squares[:, t, :], x_in[:, t, :], ACT.Square,
                               accum_out=ssq[:, t:t + 1]).then_inc(sq_done, 1)
            act.wait_ge(rstd_done, 1)
            for t in range(TT // 2):
                act.activation(xn_in[:, t, :], x_in[:, t, :], ACT.Copy, scale=rstd[:, t:t + 1]).then_inc(xn_done[0], 1)

            def first_h(j):
                act.wait_ge(mod1_done, j + 1)
                for k in (2 * j, 2 * j + 1):
                    b = ready(act, ("xT", 0, k))
                    if k >= 4:
                        act.wait_ge(h_lo_done[k % 2], (k - 4) // 2 + 1)
                    release(act.activation(h_part(0, k), b[:, :], ACT.Identity, scale=a1[:, k:k + 1],
                                           bias=mod[:, k:k + 1]), ("xT", 0, k))
                for k in (2 * j, 2 * j + 1):
                    evacuated(act, ("xT", 0, k))
                    act.activation(h_hi[:, k, :], h_part(0, k), ACT.Copy).then_inc(h_hi_done, 1)

            act.wait_ge(csilu_done, 1)
            for step, n in START:
                if step == "ada":
                    act.wait_ge(ada_in[n], 16)
                    for k in range(MOD_KTS, KT):
                        act.activation(ada[n][:, k, :], ada[n][:, k, :], ACT.Copy,
                                       scale=csilu[:, k:k + 1]).then_inc(scaled_done, 1)
                if step == "unit":
                    unit_high(n)
                if step == "h":
                    first_h(n)

            def small_results(u):
                if u == SLOT_DIAG:
                    act.wait_ge(f_done, HEADS)
                    act.activation(hp[:, :, :], hp[:, :, :], ACT.Ln).then_inc(logf_done, 1)
                if SLOT_LEVEL <= u < SLOT_LEVEL + LEVELS:
                    level_exp(u - SLOT_LEVEL)
                if u == SLOT_KDT:
                    act.wait_ge(p_done, LEVELS)
                    act.activation(dec[:, :, :], hp[:, :, :], ACT.Exp).then_inc(eg_done, 1)
                    g_last = hp[:, :, :].rearrange("p h (c t) -> p (h c) t", t=CHUNK)[:, :, CHUNK - 1]
                    act.activation(eglast[:, :], g_last, ACT.Exp).then_inc(glast_done, 1)
                    act.wait_ge(kdif_done, 1)
                    act.activation(dec[:, :, :], dec[:, :, :], ACT.Exp).then_inc(ke_done, 1)
                if u == SLOT_KDT + 1:
                    for t in range(2, TT):
                        b = ready(act, ("kdT", t))
                        release(act.activation(kd[:, t, :], b[:, :], ACT.Copy), ("kdT", t))
                if u == SLOT_O + 1:
                    for h in range(HEADS):
                        b = ready(act, ("o", h))
                        release(act.activation(o_sb[:, h, :], b[:, :], ACT.Copy), ("o", h))
                if u == SLOT_SS + 1:
                    for h in range(HEADS):
                        b = ready(act, ("ss", h))
                        release(act.activation(o_rs[:, h, :], b[:, :], ACT.Ln, scale=1.0 / 128, bias=epsc[:, :]), ("ss", h))
                    for h in range(HEADS):
                        evacuated(act, ("ss", h))
                        act.activation(o_rs[:, h, :], o_rs[:, h, :], ACT.Exp, scale=-0.5).then_inc(rs_done, 1)
                for p in range(PAIRS):
                    s = U_PAIR + 3 * p + 2
                    if u == s + 1:
                        softmax_exp(p)
                    if u == s + 2:
                        if p:
                            ready(act, ("O", p - 1, 1))
                        copy_probT(p, 1)
                    if u == s + 3:
                        scatter_o(p, 1)
                if u == SLOT_STAT + 1:
                    for g in range(NG):
                        gather_row(m_row, "mT", g)
                if u == SLOT_STAT + 2:
                    for g in range(NG):
                        gather_row(s_row, "sT", g)
                    act.wait_ge(mdiff_done, 1)
                    act.activation(m_row[:, :, :], m_row[:, :, :], ACT.Exp).then_inc(wexp_done, 1)
                if SLOT_BC < u <= SLOT_BC + HEADS:
                    h = u - SLOT_BC - 1
                    act.wait_ge(ybfull_done, h + 1)
                    act.activation(yb_hi[:, h, :], og[:, 0, h, :], ACT.Copy).then_inc(ybhi_done, 1)
                if u in (SLOT_ROW + 1, SLOT_ROW + 2):
                    w = u - SLOT_ROW - 1
                    if w == 1:
                        act.wait_ge(yblo_done, HEADS)
                    for i in range(2):
                        b = ready(act, ("row", w, i))
                        row = (g1_row, g2_row)[w]
                        release(act.activation(row[:, 512 * i:512 * i + 512], b[:, :], ACT.Copy), ("row", w, i))

            def level_exp(j):
                half = 1 << j
                pv = hp[:, :, :].rearrange("p h (blk pos tok) -> p (h blk) pos tok", pos=2, tok=half)
                dv = dec[:, :, :].rearrange("p h (blk pos tok) -> p (h blk) pos tok", pos=2, tok=half)
                act.wait_ge(d1_done, j + 1)
                act.activation(dv[:, :, 1, :], pv[:, :, 1, :], ACT.Exp)
                act.activation(dv[:, :, 0, :], dv[:, :, 0, :], ACT.Exp).then_inc(e_done, 1)

            def softmax_exp(p):
                g, h0, _ = pair(p)
                for hh in range(2):
                    act.wait_ge(nmax_done, 2 * p + hh + 1)
                    at_ = 0
                    for q in range(TT):
                        n = sum(b[0] == q for b in blocks_of(p)) * P
                        col = (g * TT + q) * HEADS + h0 + hh
                        ins = act.activation(prob[:, hh, at_:at_ + n], prob[:, hh, at_:at_ + n], ACT.Exp, scale=SCALE,
                                             bias=nmax[:, col:col + 1], accum_out=ssum[:, col:col + 1])
                        at_ += n
                    ins.then_inc(prob_done, 1)

            def copy_probT(p, hh):
                for j in range(score_banks(p)):
                    b = ready(act, ("T", p, hh, j))
                    n = sum(block_bank(p, i)[0] == j for i in range(len(blocks_of(p)))) * P
                    release(act.activation(probT[:, hh, 3 * P * j:3 * P * j + n], b[:, 0:n], ACT.Copy), ("T", p, hh, j))

            def scatter_o(p, hh):
                g, h0, d = pair(p)
                b = ready(act, ("O", p, hh))
                release(act.activation(og[:, g, h0 + hh, :].rearrange("p (l res) -> p res l", res=d),
                                    b[:, :].rearrange("p (res l) -> p res l", res=d), ACT.Copy), ("O", p, hh))

            def gather_row(dst, name, g):
                d = ORDER[g]
                b = ready(act, (name, g))
                release(act.activation(dst[:, g, :].rearrange("p (l res) -> p res l", res=d),
                                    b[0:HEADS, :].rearrange("p (res l) -> p res l", res=d), ACT.Copy), (name, g))

            def evacuate(u):
                if u < U_HI:
                    for t in range(2):
                        h = 2 * (u % 2) + t
                        if u >= U_HF:
                            evacuated(act, ("g", u - 2, t))
                        b = ready(act, ("g", u, t))
                        ins = act.activation(dec[:, h, :], b[:, :], ACT.Sigmoid)
                        if u < U_HF:
                            ins.then_inc(sig_done, 1)
                        else:
                            release(ins, ("g", u, t))
                elif U_PAIR <= u < U_HG:
                    p, what = divmod(u - U_PAIR, 3)
                    if what == 0:
                        g, h0, d = pair(p)
                        if p:
                            ready(act, ("S", p - 1, 1, score_banks(p - 1) - 1))
                        for t in range(2):
                            b = ready(act, ("g", u, t))
                            release(act.activation(qa[:, t, :].rearrange("p (res l) -> p res l", res=d),
                                                b[:, :].rearrange("p (l res) -> p res l", res=d), ACT.Copy), ("g", u, t))
                elif U_HG <= u < U_GA:
                    for t in range(2):
                        h = 2 * (u - U_HG) + t
                        if h >= 2:
                            act.wait_ge(yfull_done, h - 1)
                        b = ready(act, ("g", u, t))
                        act.activation(sgt[:, h % 2, :], b[:, :], ACT.Sigmoid).then_inc(sig_done, 1)
                    for t in range(2):
                        h = 2 * (u - U_HG) + t
                        act.wait_ge(yfull_done, h + 1)
                        act.activation(ya_hi[:, h, :], yh[:, h, :], ACT.Copy).then_inc(yahi_done, 1)
                elif U_GA <= u < U_A:
                    dst, u0 = (sga, U_GA) if u < U_GB else (sgb, U_GB)
                    if u == U_GA:
                        act.wait_ge(yalo_done, HEADS)
                    for t in range(2):
                        b = ready(act, ("g", u, t))
                        release(act.activation(dst[:, 2 * (u - u0) + t, :], b[:, :], ACT.Sigmoid), ("g", u, t))
                elif U_B <= u < U_OUT:
                    if u == U_B:
                        act.wait_ge(yblo_done, HEADS)
                    for t in range(4):
                        f = 4 * (u - U_B) + t
                        act.wait_ge(mfull_done, f + 1)
                        act.activation(m_hi[:, f, :], sgb[:, f, :], ACT.Copy).then_inc(mhi_done, 1)
                elif u >= U_OUT:
                    v = u - U_OUT
                    for t in range(TT):
                        act.wait_ge(x1_done, TT * v + t + 1)
                        ins = act.activation(xn_ffn[:, t, 256 * v:256 * v + 256], x1[:, t, 256 * v:256 * v + 256],
                                             ACT.Square, accum_out=ssp[:, 4 * t + v:4 * t + v + 1])
                    ins.then_inc(ssp_done, 1)

            for u in range(U_UP):
                if u >= 2:
                    unit_high(u + 1)
                small_results(u)
                evacuate(u)

            high_part(1, 8 * (U_UP + 2))
            act.wait_ge(rstd_done, 2)
            act.activation(xn_ffn[:, 3, :], x1[:, 3, :], ACT.Copy, scale=rstd[:, TT + 3:TT + 4]).then_inc(xn_done[0], 1)
            for k in range(KT):
                evacuated(act, ("xT", 1, k))
                act.activation(h_hi[:, k, :], h_part(1, k), ACT.Copy).then_inc(h_hi_done, 1)

            CW = convc[:, :]
            with act.Fori(0, FT // 2) as i:
                for t in range(2):
                    act.wait_ge(full[t], BANKS[f"gate{t}"][1] + 1 + i)
                    act.activation(conv[:, t, :], bank[t][:, :], ACT.Identity,
                                   scale=CW[:, bass.ds(2 * i + (2 * FT + t), 1)],
                                   bias=CW[:, bass.ds(2 * i + (3 * FT + t), 1)]).then_inc(conv0_done, 1)
                high_part(0, 8 * (U_UP + 4) + 16 * i)
                for t in range(2):
                    act.wait_ge(free[t], BANKS[f"gate{t}"][1] + 1 + i)
                    act.activation(gelu[:, t, :], conv[:, t, :], ACT.Gelu_apprx_tanh).then_inc(gelu_done, 1)
                for t in range(2):
                    act.wait_ge(free[2 + t], BANKS[f"val{t}"][1] + 1 + i)
                    act.activation(act_hi[:, bass.ds(2 * i + t, 1), :].rearrange("p a s -> p (a s)"), gelu[:, t, :],
                                   ACT.Copy).then_inc(ahi_done, 1)
                high_part(1, 8 * (U_UP + 4) + 16 * i)
            for u in range(U_DOWN + 2, N_UNITS):
                unit_high(u)
            for t in range(TT):
                act.wait_ge(x2_done, t + 1)
                act.activation(squares[:, t, :], x1[:, t, :], ACT.Square,
                               accum_out=ssq[:, 2 * TT + t:2 * TT + t + 1]).then_inc(sq_done, 1)

        @block.tensor
        def _(pe):
            def mm(o, lhsT, rhs, start=True, stop=True, **kw):
                return pe.matmul(o, lhsT, rhs, start=start, stop=stop, **kw)

            def transpose(o, i):
                return pe.transpose(o, i, ident[0:i.shape[0], 0:i.shape[0]])

            pe.wait_ge(consts, 1)
            pe.wait_ge(vec_in, 16 * 8)
            b = claim(pe, "vec")
            transpose(b[:, 0:84], vec_rows[:, :])
            filled(transpose(b[:, 84:172], conv_rows[:, :]), "vec")

            def modulation(b, col, n, sums):
                pe.wait_ge(part_done, n + 1)
                for t in range(2):
                    ins = mm(b[:, col + t:col + t + 1], sums[:, t * P:(t + 1) * P], ones[:, 0:1])
                return ins

            def transposed_h(which, k):
                src = xn_in if which == 0 else xn_ffn
                b = claim(pe, ("xT", which, k))
                if k == 0:
                    pe.wait_ge(xn_done[0], TT // 2 + which)
                    pe.wait_ge(xn_done[1], TT // 2 + which * (TT - 1))
                for t in range(TT):
                    ins = transpose(b[:, t * P:(t + 1) * P], src[:, t, k * P:(k + 1) * P])
                filled(ins, ("xT", which, k))

            def unit_parts(u, slot, width):
                pe.wait_ge(lo_done, u + 1)
                return [w[slot][:, :].rearrange("p (k c) -> p k c", c=width) for w in (whi, wlo)]

            def three_passes(o, lhs, rhs, k, last_k, start=None, skip=False):
                for i, (a, bb) in enumerate(((0, 0), (0, 1), (1, 0))):
                    ins = mm(o, lhs[a], rhs[bb], start=(k == 0 and i == 0) if start is None else start and i == 0,
                             stop=k == last_k and i == 2, skip_group_check=skip)
                return ins

            def feature_tile(o, parts, c0, acts, kts=KT, h_count=None):
                for k in range(kts):
                    if h_count is not None:
                        pe.wait_ge(h_lo_done[k % 2], h_count + k // 2 + 1)
                    ins = three_passes(o, [w[:, k, c0:c0 + P] for w in parts], [a[:, k, :] for a in acts], k, kts - 1)
                return ins

            def token_tile(o, parts, acts, tokens, m_count=False):
                for k in range(KT):
                    if m_count:
                        pe.wait_ge(mlo_done, k + 1)
                    ins = three_passes(o, [tokens(a[:, k, :]) for a in acts], [w[:, k, :] for w in parts], k, KT - 1)
                return ins

            def plain_tokens(t):
                return lambda a: a[:, t * P:(t + 1) * P]

            def dilated_tokens(t, d):
                if d == 1:
                    return plain_tokens(t)
                return lambda a: a.rearrange("p (l res) -> p res l", res=d)[:, t, :]

            def products(u):
                hT = (h_hi, h_lo)
                n = tiles_of(u)
                width = 512 if U_A <= u < U_OUT else 256
                parts = unit_parts(u, 2 if u == 2 else u % 2, width)
                for t in range(n):
                    b = claim(pe, ("g", u, t))
                    if u == U_A and t == 0:
                        pe.wait_ge(yalo_done, HEADS)
                    if u == U_B and t == 0:
                        pe.wait_ge(yblo_done, HEADS)
                    if u >= U_OUT:
                        ins = token_tile(b[:, 0:256], parts, (m_hi, m_lo), plain_tokens(t), m_count=u == U_OUT and t == 0)
                    elif u >= U_A:
                        ins = feature_tile(b[:, :], parts, t * P, (ya_hi, ya_lo) if u < U_B else (yb_hi, yb_lo), HEADS)
                    elif n == 4:
                        d = 1 if u < U_PAIR else pair((u - U_PAIR) // 3)[2]
                        ins = token_tile(b[:, 0:256], parts, hT, dilated_tokens(t, d))
                    else:
                        ins = feature_tile(b[:, :], parts, t * P, hT)
                    filled(ins, ("g", u, t))

            def scores(p):
                for hh in range(2):
                    for j in range(score_banks(p)):
                        b = claim(pe, ("S", p, hh, j))
                        if p // 2 == 0:
                            runs = [(0, 0, 1), (1, 0, 2)] if j == 0 else [(2, 1, 2), (3, 2, 2)]
                        else:
                            runs = [(i, i, 1) for i in range(TT)]
                        col = 0
                        for q, k, n in runs:
                            ins = mm(b[:, col:col + n * P], qa[:, hh, q * P:(q + 1) * P], ka[:, hh, k * P:(k + n) * P])
                            col += n * P
                        filled(ins, ("S", p, hh, j))

            def small(u):
                if u == SLOT_DIAG:
                    for t in range(4):
                        evacuated(pe, ("g", U_HQ + t // 2, t % 2))
                    pe.wait_ge(f_done, HEADS)
                    for h in range(HEADS):
                        b = claim(pe, ("diag", h))
                        for t in range(TT):
                            tok = slice(t * P, (t + 1) * P)
                            ins = mm(b[:, tok], hk[:, h, tok], hq[:, h, tok])
                        filled(ins, ("diag", h))
                if SLOT_LEVEL <= u < SLOT_LEVEL + LEVELS:
                    j = u - SLOT_LEVEL
                    pe.wait_ge(z_done, j + 1)
                    z = zz[j % 2]
                    for h in range(HEADS):
                        b = claim(pe, ("lev", j, h))
                        for t in range(TT):
                            tok = slice(t * P, (t + 1) * P)
                            ins = mm(b[:, tok], z[:, h, tok], z[:, h, tok])
                        filled(ins, ("lev", j, h))
                if u == SLOT_KDT:
                    pe.wait_ge(kdec_done, 1)
                    for t in range(TT):
                        b = claim(pe, ("kdT", t))
                        for h in range(HEADS):
                            ins = transpose(b[:, h * P:(h + 1) * P], zz[1][:, h, t * P:(t + 1) * P])
                        filled(ins, ("kdT", t))
                if u in (SLOT_UPD, SLOT_UPD + 1):
                    for c in (range(4) if u == SLOT_UPD else range(4, NCHUNK - 1)):
                        t, rows = c // 2, slice(64 * (c % 2), 64 * (c % 2) + 64)
                        evacuated(pe, ("kdT", t))
                        b = claim(pe, ("upd", c))
                        for h in range(HEADS):
                            ins = mm(b[:, h * P:(h + 1) * P], kd[rows, t, h * P:(h + 1) * P], hv[rows, t, h * P:(h + 1) * P])
                        filled(ins, ("upd", c))
                if u == SLOT_O:
                    for c in range(NCHUNK - 1):
                        evacuated(pe, ("upd", c))
                    for h in range(HEADS):
                        evacuated(pe, ("lev", LEVELS - 1, h))
                    for h in range(HEADS):
                        b = claim(pe, ("o", h))
                        for t in range(TT):
                            tok = slice(t * P, (t + 1) * P)
                            mm(b[:, tok], hv[:, t, h * P:(h + 1) * P], scT[:, h, tok], start=t == 0, stop=False,
                               skip_group_check=True)
                        for c in range(1, NCHUNK):
                            st = st_a[:, c - 1, :] if c < 5 else st_b[:, c - 5, :]
                            tok = slice(c * CHUNK, (c + 1) * CHUNK)
                            ins = mm(b[:, tok], st[:, h * P:(h + 1) * P], zz[0][:, h, tok], start=False,
                                     stop=c == NCHUNK - 1, skip_group_check=True)
                        filled(ins, ("o", h))
                if u == SLOT_SS:
                    for h in range(HEADS):
                        pe.wait_ge(osq_done, h + 1)
                        b = claim(pe, ("ss", h))
                        filled(mm(b[:, :], ones[:, :], o_sq[:, h, :]), ("ss", h))
                for p in range(PAIRS):
                    s = U_PAIR + 3 * p + 2
                    if u == s:
                        for t in range(2):
                            evacuated(pe, ("g", s - 2, t))
                            evacuated(pe, ("g", s - 1, t))
                        scores(p)
                    if u == s + 1:
                        for hh in range(2):
                            pe.wait_ge(prob_done, 2 * p + hh + 1)
                            bb = [claim(pe, ("T", p, hh, j)) for j in range(score_banks(p))]
                            n_blocks = len(blocks_of(p))
                            for n in range(n_blocks):
                                j, col = block_bank(p, n)
                                ins = transpose(bb[j][:, col:col + P], prob[:, hh, n * P:(n + 1) * P])
                                if n == n_blocks - 1 or block_bank(p, n + 1)[0] != j:
                                    filled(ins, ("T", p, hh, j))
                    if u == s + 2:
                        for t in range(4):
                            evacuated(pe, ("g", s, t))
                        for hh in range(2):
                            b = claim(pe, ("O", p, hh))
                            for j in range(score_banks(p)):
                                evacuated(pe, ("T", p, hh, j))
                            blocks = blocks_of(p)
                            for n, (q, k) in enumerate(blocks):
                                first = n == 0 or blocks[n - 1][0] != q
                                last = n == len(blocks) - 1 or blocks[n + 1][0] != q
                                ins = mm(b[:, q * P:(q + 1) * P], va[:, k, hh * P:(hh + 1) * P],
                                         probT[:, hh, n * P:(n + 1) * P], first, last)
                            filled(ins, ("O", p, hh))
                if u in (SLOT_STAT, SLOT_STAT + 1):
                    name, src = (("mT", nmax), ("sT", ssum))[u - SLOT_STAT]
                    for g in range(NG):
                        b = claim(pe, (name, g))
                        for q in range(TT):
                            col = (g * TT + q) * HEADS
                            ins = transpose(b[0:HEADS, q * P:(q + 1) * P], src[:, col:col + HEADS])
                        filled(ins, (name, g))
                if SLOT_BC <= u < SLOT_BC + HEADS:
                    h = u - SLOT_BC
                    pe.wait_ge(crow_done, NG)
                    for g in range(NG):
                        b = claim(pe, ("bc", h, g))
                        filled(mm(b[:, :], ident[0:HEADS, h:h + 1].broadcast_to([HEADS, P]), m_row[:, g, :]), ("bc", h, g))
                if u in (SLOT_ROW, SLOT_ROW + 1):
                    w = u - SLOT_ROW
                    pe.wait_ge(gp_done, 1)
                    for i in range(2):
                        b = claim(pe, ("row", w, i))
                        for k in range(4):
                            n = 8 * w + 4 * i + k
                            ins = transpose(b[:, k * P:(k + 1) * P], gp[:, n:n + 1].broadcast_to([P, P]))
                        filled(ins, ("row", w, i))
                if u in MOD_UNITS:
                    b = claim(pe, ("mod2", u))
                    for i, n in enumerate(MOD_UNITS[u]):
                        ins = modulation(b, 2 * i, n, part2[n % 4])
                    filled(ins, ("mod2", u))

            def growing_products(j, u):
                parts = unit_parts(u, u, 256)
                for t in range(2):
                    b = claim(pe, ("g", u, t)) if j == 0 else bank[BANKS["g", u, t][0]]
                    for k in (2 * j, 2 * j + 1):
                        if t == 0:
                            pe.wait_ge(h_lo_done[k % 2], k // 2 + 1)
                        ins = three_passes(b[:, :], [w[:, k, t * P:(t + 1) * P] for w in parts],
                                           [a[:, k, :] for a in (h_hi, h_lo)], k, KT - 1, skip=True)
                    if j == KT // 2 - 1:
                        filled(ins, ("g", u, t))

            for k in range(2):
                transposed_h(0, k)
            for j in range(KT // 2):
                b = claim(pe, ("mod1", j))
                for i in range(2):
                    n = 2 * j + i
                    ins = modulation(b, 2 * i, n, part[:, n % 4, :])
                filled(ins, ("mod1", j))
                if j:
                    growing_products(j - 1, 0)
                    growing_products(j - 1, 1)
                if j < KT // 2 - 1:
                    for k in (2 * j + 2, 2 * j + 3):
                        transposed_h(0, k)
            growing_products(KT // 2 - 1, 0)
            growing_products(KT // 2 - 1, 1)
            for u in range(U_UP):
                if u >= 2:
                    products(u)
                small(u)

            for k in range(KT):
                transposed_h(1, k)
            with pe.Fori(0, FT // 2) as i:
                for half, name in enumerate(("gate", "val")):
                    parts = unit_parts(2 * i + U_UP + half, half, 256)
                    for t in range(2):
                        bk, n = BANKS[f"{name}{t}"]
                        pe.wait_ge(free[bk], i + n)
                        feature_tile(bank[bk][:, :], parts, t * P, (h_hi, h_lo),
                                     h_count=KT // 2 if name == "gate" and t == 0 else None).then_inc(full[bk], 1)
            for t in range(TT):
                for half in range(2):
                    claim(pe, ("y", t, half))
            for i in range(FT // 2):
                u = U_DOWN + i
                parts = unit_parts(u, u % 2, 1024)
                pe.wait_ge(alo_done, 2 * i + 2)
                for t in range(TT):
                    tok = slice(t * P, (t + 1) * P)
                    for half in range(2):
                        for kk in range(2):
                            k = 2 * i + kk
                            ins = three_passes(bank[2 * t + half][:, :], [a[:, k, tok] for a in (act_hi, act_lo)],
                                               [w[:, kk, half * 512:half * 512 + 512] for w in parts], k, FT - 1)
                        if i == FT // 2 - 1:
                            filled(ins, ("y", t, half))
                if i < FT // 2 - 1:
                    ins.then_inc(down_used, 1)

        @block.vector
        def _(dve):
            n_chain = [0]

            def link(ins):
                n_chain[0] += 1
                ins.then_inc(dchain, 1)
                dve.wait_ge(dchain, n_chain[0])

            tt, ts, stt = dve.tensor_tensor, dve.tensor_scalar, dve.scalar_tensor_tensor

            b = ready(dve, "vec")
            link(dve.tensor_copy(vec[:, :], b[:, 0:84]))
            release(dve.tensor_copy(convc[:, :], b[:, 84:172]), "vec")
            tt(lbd[:, :], vec[:, LB:LB + 4], vec[:, LB + 4:LB + 8], ALU.subtract).then_inc(lbd_done, 1)
            dve.wait_ge(csig_done, 1)
            tt(csilu[:, :], csig[:, :], vec[:, C_:C_ + 8], ALU.mult).then_inc(csilu_done, 1)
            dve.wait_ge(lb_done, 1)
            link(ts(oml[:, :], lb[:, :], -1.0, 1.0, ALU.mult, ALU.add))

            dve.wait_ge(rstd_done, 1)
            for t in range(TT // 2, TT):
                dve.wait_ge(x_in_s[t], 16)
                ts(xn_in[:, t, :], x_in[:, t, :], rstd[:, t:t + 1], None, ALU.mult).then_inc(xn_done[1], 1)

            n_part = [0, 0]

            def partial_sums(unit, sums, kts=KT, rest=0):
                dve.wait_ge(csilu_done, 1)
                for k in range(kts):
                    dst = sums if k % 2 == 0 else unit[:, 1, :]
                    sc = csilu[:, k:k + 1]
                    if k >= 2:
                        dve.wait_ge(part_chain[k % 2], n_part[k % 2])
                        ins = stt(dst, unit[:, k, :], sc, dst, ALU.mult, ALU.add)
                    else:
                        ins = ts(dst, unit[:, k, :], sc, None, ALU.mult)
                    ins.then_inc(part_chain[k % 2], 1)
                    n_part[k % 2] += 1
                for i in range(2):
                    dve.wait_ge(part_chain[i], n_part[i])
                ins = tt(sums, sums, unit[:, 1, :], ALU.add)
                if rest:
                    link(ins)
                    dve.wait_ge(rest_done, rest)
                    ins = tt(sums, sums, unit[:, kts, :], ALU.add)
                ins.then_inc(part_done, 1)

            def low_h(which, k):
                dve.wait_ge(h_hi_done, which * KT + k + 1)
                tt(h_lo[:, k, :], h_part(which, k), h_hi[:, k, :].bitcast(F32), ALU.subtract).then_inc(h_lo_done[0], 1)

            for j in range(KT // 2):
                for i in range(2):
                    n = j + i * KT // 2
                    dve.wait_ge(ada_in[n], 16)
                    if j >= 2:
                        ready(dve, ("mod1", j - 2))
                    partial_sums(ada[n], part[:, (2 * j + i) % 4, :], MOD_KTS, START_ADA.index(n) + 1)
                    if i == 0 and j:
                        low_h(0, 2 * j - 2)
                b = ready(dve, ("mod1", j))
                cols, scales = slice(2 * j, 2 * j + 2), slice(KT + 2 * j, KT + 2 * j + 2)
                tt(mod[:, cols], b[:, 0:2], vec[:, B_ADA + 2 * j:B_ADA + 2 * j + 2], ALU.add)
                release(tt(mod[:, scales], b[:, 2:4], vec[:, B_ADA + KT + 2 * j:B_ADA + KT + 2 * j + 2], ALU.add), ("mod1", j))
                evacuated(dve, ("mod1", j))
                stt(a1[:, cols], mod[:, scales], 1.0, vec[:, G_MIX + 2 * j:G_MIX + 2 * j + 2], ALU.add,
                    ALU.mult).then_inc(mod1_done, 1)
                if j == 0:
                    dve.wait_ge(hi_done, 1)
                    tt(wlo[0][:, :], raw[0][:, :], whi[0][:, :].bitcast(F32), ALU.subtract).then_inc(lo_done, 1)
            low_h(0, KT - 2)

            def make_h():
                for k in range(KT):
                    b = ready(dve, ("xT", 1, k))
                    if k >= 5 and k % 2:
                        dve.wait_ge(h_lo_done[1], KT // 2 + (k - 4) // 2 + 1)
                    release(ts(h_part(1, k), b[:, :], a2[:, k:k + 1], mod[:, 24 + k:25 + k], ALU.mult, ALU.add),
                            ("xT", 1, k))
                    if k % 2:
                        low_h(1, k - 1)

            def small_results(u):
                if u == SLOT_DIAG:
                    dve.wait_ge(consts, 2)
                    link(ts(dint[:, :], dint[:, :], 3, None, ALU.bitwise_and))
                    link(ts(dist2[:, :], dint[:, :], FAR, None, ALU.mult))
                    tt(dist2[:, :], dist2[:, :], dist1[:, :], ALU.add)
                if u == 0:
                    dve.memset(scT[:, :, :], 0.0)
                if u - 1 in MOD_UNITS:
                    units = MOD_UNITS[u - 1]
                    b = ready(dve, ("mod2", u - 1))
                    cols = slice(2 * units[0], 2 * units[-1] + 2)
                    release(tt(mod[:, cols], b[:, 0:2 * len(units)], vec[:, cols], ALU.add), ("mod2", u - 1))
                if u == max(MOD_UNITS) + 1:
                    for v in MOD_UNITS:
                        evacuated(dve, ("mod2", v))
                    stt(a2[:, :], mod[:, 32:40], 1.0, vec[:, G_FFN:G_FFN + 8], ALU.add, ALU.mult)
                    link(ts(gp[:, 0:8], mod[:, 16:24], 1.0, None, ALU.add))
                    ts(gp[:, 8:16], mod[:, 40:48], 1.0, None, ALU.add).then_inc(gp_done, 1)
                if u == SLOT_DIAG + 1:
                    for h in range(HEADS):
                        b = ready(dve, ("diag", h))
                        release(dve.copy_predicated(scT[:, h, :], diag[:, :], b[:, :]), ("diag", h))
                if SLOT_LEVEL < u <= SLOT_LEVEL + LEVELS:
                    level_scores(u - SLOT_LEVEL - 1)
                if SLOT_LEVEL <= u < SLOT_LEVEL + LEVELS:
                    level_factors(u - SLOT_LEVEL)
                if u == SLOT_KDT:
                    dve.wait_ge(eg_done, 1)
                    link(tt(zz[0][:, :, :], hq[:, :, :], dec[:, :, :], ALU.mult))
                    pc = hp[:, :, :].rearrange("p h (c t) -> p (h c) t", t=CHUNK)
                    dc = dec[:, :, :].rearrange("p h (c t) -> p (h c) t", t=CHUNK)
                    tt(dc, pc[:, :, CHUNK - 1:CHUNK].broadcast_to([P, HEADS * NCHUNK, CHUNK]), pc, ALU.subtract).then_inc(kdif_done, 1)
                    dve.wait_ge(ke_done, 1)
                    tt(zz[1][:, :, :], hk[:, :, :], dec[:, :, :], ALU.mult).then_inc(kdec_done, 1)
                if u == SLOT_KDT + 1:
                    dve.wait_ge(kdec_done, 1)
                    for t in range(2):
                        b = ready(dve, ("kdT", t))
                        release(dve.tensor_copy(kd[:, t, :], b[:, :]), ("kdT", t))
                if u == SLOT_UPD + 1:
                    states(range(4))
                if u == SLOT_UPD + 2:
                    states(range(4, NCHUNK - 1))
                if u == SLOT_O + 1:
                    for h in range(HEADS):
                        evacuated(dve, ("o", h))
                        tt(o_sq[:, h, :], o_sb[:, h, :], o_sb[:, h, :], ALU.mult).then_inc(osq_done, 1)
                for p in range(PAIRS):
                    s = U_PAIR + 3 * p + 2
                    if u == s + 1:
                        softmax_max(p)
                    if u == s + 2:
                        if p:
                            ready(dve, ("O", p - 1, 1))
                        for j in range(score_banks(p)):
                            b = ready(dve, ("T", p, 0, j))
                            n = sum(block_bank(p, i)[0] == j for i in range(len(blocks_of(p)))) * P
                            release(dve.tensor_copy(probT[:, 0, 3 * P * j:3 * P * j + n], b[:, 0:n]), ("T", p, 0, j))
                    if u == s + 3:
                        g, h0, d = pair(p)
                        b = ready(dve, ("O", p, 0))
                        release(dve.tensor_copy(og[:, g, h0, :].rearrange("p (l res) -> p res l", res=d),
                                             b[:, :].rearrange("p (res l) -> p res l", res=d)), ("O", p, 0))
                if u == SLOT_STAT + 2:
                    group_weights()
                if SLOT_BC < u <= SLOT_BC + HEADS:
                    merge_groups(u - SLOT_BC - 1)

            def level_scores(j):
                half = 1 << j
                m = masks[:, j, :].rearrange("p (blk tok) -> p blk tok", tok=half)
                dve.wait_ge(masks_done, j + 1)
                for h in range(HEADS):
                    b = ready(dve, ("lev", j, h))
                    second = [a.rearrange("p (blk pos tok) -> p blk pos tok", pos=2, tok=half)[:, :, 1, :]
                              for a in (scT[:, h, :], b[:, :])]
                    release(dve.copy_predicated(second[0], m, second[1]), ("lev", j, h))

            def level_factors(j):
                half = 1 << j
                if j == 0:
                    dve.wait_ge(logf_done, 1)
                else:
                    dve.wait_ge(p_done, j)
                v = {n: t[:, :, :].rearrange("p h (blk pos tok) -> p (h blk) pos tok", pos=2, tok=half)
                     for n, t in (("p", hp), ("d", dec), ("q", hq), ("k", hk), ("z", zz[j % 2]))}
                total = v["p"][:, :, 0, half - 1:half].broadcast_to([P, HEADS * S // (2 * half), half])
                tt(v["d"][:, :, 0, :], total, v["p"][:, :, 0, :], ALU.subtract).then_inc(d1_done, 1)
                dve.wait_ge(e_done, j + 1)
                tt(v["z"][:, :, 1, :], v["q"][:, :, 1, :], v["d"][:, :, 1, :], ALU.mult)
                tt(v["z"][:, :, 0, :], v["k"][:, :, 0, :], v["d"][:, :, 0, :], ALU.mult).then_inc(z_done, 1)
                tt(v["p"][:, :, 1, :], v["p"][:, :, 1, :], total, ALU.add).then_inc(p_done, 1)

            def states(chunks):
                for c in chunks:
                    b = ready(dve, ("upd", c))
                    dst = st_a[:, c, :] if c < 4 else st_b[:, c - 4, :]
                    if c == 0:
                        dve.wait_ge(glast_done, 1)
                        ins = dve.tensor_copy(dst, b[:, :])
                    else:
                        src = st_a[:, c - 1, :] if c < 5 else st_b[:, c - 5, :]
                        for h in range(HEADS):
                            cols = slice(h * P, (h + 1) * P)
                            n = h * NCHUNK + c
                            ins = stt(dst[:, cols], src[:, cols], eglast[:, n:n + 1], b[:, cols], ALU.mult, ALU.add)
                    release(ins, ("upd", c))
                    evacuated(dve, ("upd", c))

            def softmax_max(p):
                g, h0, d = pair(p)
                if p:
                    ready(dve, ("T", p - 1, 1, score_banks(p - 1) - 1))
                for hh in range(2):
                    slope = 2.0 ** (-8.0 * (g * HEADS + h0 + hh + 1) / (NG * HEADS))
                    k = -slope * d / SCALE
                    pr = prob[:, hh, :]
                    if g == 0:
                        b = ready(dve, ("S", p, hh, 0))
                        stt(pr[:, 0:P], dist0[:, P:2 * P], k, b[:, 0:P], ALU.mult, ALU.add)
                        release(stt(pr[:, P:3 * P], dist0[:, :], k, b[:, P:3 * P], ALU.mult, ALU.add), ("S", p, hh, 0))
                        b = ready(dve, ("S", p, hh, 1))
                        for i in range(2):
                            ins = stt(pr[:, (3 + 2 * i) * P:(5 + 2 * i) * P], dist0[:, :], k,
                                      b[:, 2 * i * P:(2 * i + 2) * P], ALU.mult, ALU.add)
                        release(ins, ("S", p, hh, 1))
                        evacuated(dve, ("S", p, hh, 1))
                        dve.tensor_reduce(mx[:, 4 * hh:4 * hh + 1], pr[:, 0:P], AX_X, ALU.max)
                        link(dve.tensor_reduce(mx[:, 4 * hh + 1:4 * hh + 4],
                                               pr[:, P:7 * P].rearrange("p (q k) -> p q k", q=3), AX_X, ALU.max))
                    else:
                        dist = dist1 if g == 1 else dist2
                        b = ready(dve, ("S", p, hh, 0))
                        for i in range(TT):
                            tok = slice(i * P, (i + 1) * P)
                            ins = stt(pr[:, tok], dist[:, :], k, b[:, tok], ALU.mult, ALU.add)
                        release(ins, ("S", p, hh, 0))
                        evacuated(dve, ("S", p, hh, 0))
                        link(dve.tensor_reduce(mx[:, 4 * hh:4 * hh + 4],
                                               pr[:, 0:4 * P].rearrange("p (q k) -> p q k", q=4), AX_X, ALU.max))
                    cols = slice(g * TT * HEADS + h0 + hh, (g + 1) * TT * HEADS, HEADS)
                    ts(nmax[:, cols], mx[:, 4 * hh:4 * hh + 4], -SCALE, None, ALU.mult).then_inc(nmax_done, 1)

            def group_weights():
                for g in range(NG):
                    evacuated(dve, ("mT", g))
                link(tt(inv[:, :], m_row[:, 0, :], m_row[:, 1, :], ALU.min))
                link(tt(inv[:, :], inv[:, :], m_row[:, 2, :], ALU.min))
                for g in range(NG):
                    ins = tt(m_row[:, g, :], inv[:, :], m_row[:, g, :], ALU.subtract)
                ins.then_inc(mdiff_done, 1)
                dve.wait_ge(wexp_done, 1)
                for g in range(NG):
                    evacuated(dve, ("sT", g))
                link(tt(s_row[:, :, :], s_row[:, :, :], m_row[:, :, :], ALU.mult))
                link(tt(inv[:, :], s_row[:, 0, :], s_row[:, 1, :], ALU.add))
                link(tt(inv[:, :], inv[:, :], s_row[:, 2, :], ALU.add))
                link(dve.reciprocal(inv[:, :], inv[:, :]))
                for g in range(NG):
                    tt(m_row[:, g, :], m_row[:, g, :], inv[:, :], ALU.mult).then_inc(crow_done, 1)

            def merge_groups(h):
                for g in range(NG):
                    b = ready(dve, ("bc", h, g))
                    release(tt(og[:, g, h, :], og[:, g, h, :], b[:, :], ALU.mult), ("bc", h, g))
                for g in range(NG):
                    evacuated(dve, ("bc", h, g))
                link(tt(og[:, 0, h, :], og[:, 0, h, :], og[:, 1, h, :], ALU.add))
                tt(og[:, 0, h, :], og[:, 0, h, :], og[:, 2, h, :], ALU.add).then_inc(ybfull_done, 1)
                dve.wait_ge(ybhi_done, h + 1)
                tt(yb_lo[:, h, :], og[:, 0, h, :], yb_hi[:, h, :].bitcast(F32), ALU.subtract).then_inc(yblo_done, 1)

            def evacuate(u):
                if u < U_HF:
                    for t in range(2):
                        h = 2 * u + t
                        dve.wait_ge(sig_done, h + 1)
                        b = ready(dve, ("g", u, t))
                        release(tt(hq[:, h, :], b[:, :], dec[:, h, :], ALU.mult), ("g", u, t))
                elif u < U_HI:
                    for t in range(2):
                        h = 2 * (u - U_HF) + t
                        evacuated(dve, ("g", u, t))
                        link(ts(hp[:, h, :], dec[:, h, :], oml[:, h:h + 1], lb[:, h:h + 1], ALU.mult, ALU.add))
                        ts(hk[:, h, :], hp[:, h, :], -1.0, 1.0, ALU.mult, ALU.add).then_inc(f_done, 1)
                elif u < U_PAIR:
                    for t in range(TT):
                        b = ready(dve, ("g", u, t))
                        c0 = 256 * (u - U_HI)
                        release(dve.tensor_copy(hv[:, t, c0:c0 + 256], b[:, 0:256]), ("g", u, t))
                elif u < U_HG:
                    p, what = divmod(u - U_PAIR, 3)
                    g, h0, d = pair(p)
                    if what == 1:
                        for t in range(2):
                            b = ready(dve, ("g", u, t))
                            release(dve.tensor_copy(ka[:, t, :].rearrange("p (res l) -> p res l", res=d),
                                                 b[:, :].rearrange("p (l res) -> p res l", res=d)), ("g", u, t))
                    if what == 2:
                        if p:
                            ready(dve, ("O", p - 1, 1))
                        for t in range(TT):
                            b = ready(dve, ("g", u, t))
                            release(dve.tensor_copy(va[:, t, :], b[:, 0:256]), ("g", u, t))
                elif u < U_GA:
                    for t in range(2):
                        h = 2 * (u - U_HG) + t
                        dve.wait_ge(sig_done, HEADS + h + 1)
                        b = ready(dve, ("g", u, t))
                        release(tt(sgt[:, h % 2, :], b[:, :], sgt[:, h % 2, :], ALU.mult), ("g", u, t))
                        evacuated(dve, ("g", u, t))
                        tt(yh[:, h, :], yh[:, h, :], sgt[:, h % 2, :], ALU.mult).then_inc(yfull_done, 1)
                    for t in range(2):
                        h = 2 * (u - U_HG) + t
                        dve.wait_ge(yahi_done, h + 1)
                        tt(ya_lo[:, h, :], yh[:, h, :], ya_hi[:, h, :].bitcast(F32), ALU.subtract).then_inc(yalo_done, 1)
                elif U_A <= u < U_B:
                    for t in range(4):
                        f = 4 * (u - U_A) + t
                        if t == 0 and u == U_A:
                            for v in range(U_GA, U_A):
                                for i in range(2):
                                    evacuated(dve, ("g", v, i))
                        b = ready(dve, ("g", u, t))
                        release(tt(sga[:, f, :], sga[:, f, :], b[:, :], ALU.mult), ("g", u, t))
                elif U_B <= u < U_OUT:
                    for t in range(4):
                        f = 4 * (u - U_B) + t
                        b = ready(dve, ("g", u, t))
                        release(tt(sgb[:, f, :], sgb[:, f, :], b[:, :], ALU.mult), ("g", u, t))
                        evacuated(dve, ("g", u, t))
                        tt(sgb[:, f, :], sgb[:, f, :], sga[:, f, :], ALU.add).then_inc(mfull_done, 1)
                        dve.wait_ge(mhi_done, f + 1)
                        tt(m_lo[:, f, :], sgb[:, f, :], m_hi[:, f, :].bitcast(F32), ALU.subtract).then_inc(mlo_done, 1)
                elif u >= U_OUT:
                    if u == U_OUT:
                        dve.wait_ge(x_again, 16)
                        for i in range(2):
                            evacuated(dve, ("row", 0, i))
                    c0 = 256 * (u - U_OUT)
                    cols = slice(c0, c0 + 256)
                    for t in range(TT):
                        b = ready(dve, ("g", u, t))
                        tmp = sgb[:, t, 0:256]
                        release(tt(tmp, b[:, 0:256], g1_row[:, cols], ALU.mult), ("g", u, t))
                        evacuated(dve, ("g", u, t))
                        tt(x1[:, t, cols], x1[:, t, cols], tmp, ALU.add).then_inc(x1_done, 1)

            for u in range(U_UP):
                small_results(u)
                for n in MOD_UNITS.get(u, ()):
                    dve.wait_ge(ada2_in[n % 2], 16 * ((n - MOD_FIRST) // 2 + 1))
                    if n >= MOD_FIRST + 4:
                        ready(dve, ("mod2", max(v for v in MOD_UNITS if MOD_UNITS[v][0] <= n - 4)))
                    partial_sums(ada2[n % 2], part2[n % 4][:, :])
                evacuate(u)
                if u == SLOT_SS + 1:
                    for h in range(HEADS):
                        dve.wait_ge(rs_done, h + 1)
                        stt(yh[:, h, :], o_sb[:, h, :], vec[:, G_HG + h:G_HG + h + 1], o_rs[:, h, :], ALU.mult, ALU.mult)

            dve.wait_ge(ssp_done, 4)
            dve.tensor_reduce(ssq[:, TT:2 * TT], ssp[:, :].rearrange("p (t n) -> p t n", n=4), AX_X,
                              ALU.add).then_inc(ssq_done, 1)
            dve.wait_ge(rstd_done, 2)
            for t in range(TT - 1):
                ts(xn_ffn[:, t, :], x1[:, t, :], rstd[:, TT + t:TT + t + 1], None, ALU.mult).then_inc(xn_done[1], 1)
            make_h()

            CW = convc[:, :]
            with dve.Fori(0, FT // 2) as i:
                for t in range(2):
                    dve.wait_ge(conv0_done, 2 * i + t + 1)
                    tt_ = conv[:, t, 1:S]
                    stt(tt_, bank[t][:, 0:S - 1], CW[:, bass.ds(2 * i + (FT + t), 1)], tt_, ALU.mult,
                        ALU.add).then_inc(tap_done, 1)
                    dve.wait_ge(tap_done, 2 * i + t + 1)
                    tt_ = conv[:, t, 2:S]
                    stt(tt_, bank[t][:, 0:S - 2], CW[:, bass.ds(2 * i + t, 1)], tt_, ALU.mult,
                        ALU.add).then_inc(free[t], 1)
                for t in range(2):
                    bk, n = BANKS[f"val{t}"]
                    dve.wait_ge(full[bk], i + (n + 1))
                    dve.wait_ge(gelu_done, 2 * i + t + 1)
                    tt(gelu[:, t, :], gelu[:, t, :], bank[bk][:, :], ALU.mult).then_inc(free[bk], 1)
                for t in range(2):
                    dve.wait_ge(ahi_done, 2 * i + t + 1)
                    hi = act_hi[:, bass.ds(2 * i + t, 1), :].rearrange("p a s -> p (a s)")
                    lo = act_lo[:, bass.ds(2 * i + t, 1), :].rearrange("p a s -> p (a s)")
                    tt(lo, gelu[:, t, :], hi.bitcast(F32), ALU.subtract).then_inc(alo_done, 1)

            dve.wait_ge(gf_in, 16)
            for i in range(2):
                evacuated(dve, ("row", 1, i))
            for t in range(TT):
                for half in range(2):
                    cols = slice(512 * half, 512 * half + 512)
                    b = ready(dve, ("y", t, half))
                    link(tt(gelu[:, half, :], b[:, :], g2_row[:, cols], ALU.mult))
                    ins = tt(x1[:, t, cols], x1[:, t, cols], gelu[:, half, :], ALU.add)
                ins.then_inc(x2_done, 1)
            for t in range(TT):
                dve.wait_ge(rstd_done, 3 + t)
                stt(x1[:, t, :], x1[:, t, :], rstd[:, 2 * TT + t:2 * TT + t + 1], gf_row[:, :], ALU.mult,
                    ALU.mult).then_inc(y_done, 1)


_INS = ["x", "c", "w_ada", "b_ada", "g_norm_mix", "w_in", "lb_logits", "g_hg_norm", "w_branch_a", "w_branch_b",
        "w_out", "g_norm_ffn", "w_up", "conv_w", "conv_b", "w_down", "g_final"]
_OUT = ((1, 512, 1024), "float32")


def kernel(**inputs):
    import concourse.bacc as _bacc
    from concourse.bass_utils import run_bass_kernel_spmd as _run

    nc = _bacc.Bacc("TRN2", target_bir_lowering=False, num_devices=1)
    arrays, args = {}, []
    for name in _INS:
        a = np.ascontiguousarray(inputs[name])
        arrays[f"in_{name}_dram"] = a
        args.append(nc.dram_tensor(f"in_{name}_dram", a.shape, mybir.dt.from_np(a.dtype), kind="ExternalInput").ap())
    shape, dtype = _OUT
    args.append(nc.dram_tensor("out_dram", shape, mybir.dt.from_np(np.dtype(dtype)), kind="ExternalOutput").ap())
    layer_kernel(nc, *args)
    r = _run(nc, [arrays], core_ids=[0])
    return r.results[0]["out_dram"]
```

```python
from contextlib import ExitStack

import numpy as np

import concourse.bass as bass
from concourse import mybir

F32 = mybir.dt.float32
F32R = mybir.dt.float32r
I8 = mybir.dt.int8
ALU = mybir.AluOpType
ACT = mybir.ActivationFunctionType
AX_X = mybir.AxisListType.X

P = 128
D = 1024
S = 512
KT = D // P
TT = S // P
HEADS = 4
E_DIM = 128
CHUNK = 64
NCHUNK = S // CHUNK
HW = HEADS * 128
GROUPS = ((128, 1), (512, 4), (2048, 16))
NG = len(GROUPS)
ORDER = tuple(min(d, 4) for _, d in GROUPS)
D_FF = 2816
FT = D_FF // P
EPS = 1e-6
SCALE = float(E_DIM) ** -0.5
FAR = 1e36
KB = 1024

PAIRS = 2 * NG
U_HQ, U_HF, U_HI = 0, 2, 4
U_PAIR = 6
U_HG = U_PAIR + 3 * PAIRS
U_GA = U_HG + 2
U_GB = U_GA + 4
U_A = U_GB + 4
U_B = U_A + 2
U_OUT = U_B + 2
U_UP = U_OUT + 4
U_DOWN = U_UP + FT
N_UNITS = U_DOWN + FT // 2
C_HG, C_AQ = 3 * HW, 4 * HW
C_AK, C_AV = C_AQ + NG * HW, C_AQ + 2 * NG * HW
C_GATES = C_AQ + 3 * NG * HW

LEVELS = 6
SLOT_DIAG = 4
SLOT_LEVEL = 6
SLOT_KDT, SLOT_UPD, SLOT_O, SLOT_SS = 12, 13, 15, 16
SLOT_STAT = U_PAIR + 3 * PAIRS + 2
SLOT_BC = SLOT_STAT + 3
SLOT_ROW = U_A
MOD_FIRST = 8
MOD_KTS = 5
START = (("ada", 0), ("x", 0), ("vec", 0), ("xn", 0), ("ada", 4), ("share", 0), ("ada", 1), ("h", 0), ("ada", 5), ("share", 1),
         ("ada", 2), ("h", 1), ("ada", 6), ("share", 2), ("ada", 3), ("h", 2), ("ada", 7), ("share", 3), ("h", 3), ("unit", 2))
MOD_SLOT, MOD_TWICE = 17, (19, 20, 22, 23, 26)
MOD_UNITS = {}
for _u in range(MOD_SLOT, MOD_SLOT + 11):
    _n = MOD_FIRST + sum(len(v) for v in MOD_UNITS.values())
    MOD_UNITS[_u] = tuple(range(_n, _n + (2 if _u in MOD_TWICE else 1)))

START_ADA = [n for step, n in START if step == "ada"]


def pair(p):
    g = p // 2
    return g, 2 * (p % 2), ORDER[g]


def score_banks(p):
    return 2 if p // 2 == 0 else 1


def plan_banks():
    uses, table, turn = [0] * 8, {}, {"gemm": 0, "small": 0, "start": 0, "fourth": 0, "gates": 0}

    def use(name, pool):
        banks = {"gemm": (0, 1, 2), "small": (3, 4, 5, 6, 7), "start": (3, 4, 5, 6), "fourth": (7,),
                 "gates": (0, 1, 2)}[pool]
        b = banks[turn[pool] % len(banks)]
        turn[pool] += 1
        table[name] = (b, uses[b])
        uses[b] += 1

    use("cT", "start")
    use("vec", "start")
    for k in range(2):
        use(("xT", 0, k), "start")
    for j in range(KT // 2):
        use(("mod1", j), "start")
        if j < KT // 2 - 1:
            for k in (2 * j + 2, 2 * j + 3):
                use(("xT", 0, k), "start")
    for u, t, pool in ((0, 0, "gemm"), (0, 1, "gemm"), (1, 0, "gemm"), (1, 1, "fourth")):
        use(("g", u, t), pool)
    for u in range(U_UP):
        if u >= 2:
            for t in range(tiles_of(u)):
                use(("g", u, t), "gemm")
        for name in small_products(u):
            use(name, "small")
    for k in range(KT):
        use(("xT", 1, k), "gates" if k < 3 else "small")
    base = list(uses)
    for i, name in enumerate(("gate0", "gate1", "val0", "val1")):
        table[name] = (i, base[i])
        uses[i] += FT // 2
    for b in range(8):
        table[("y", b // 2, b % 2)] = (b, uses[b])
    return table


def tiles_of(u):
    if U_HI <= u < U_PAIR or (U_PAIR <= u < U_HG and (u - U_PAIR) % 3 == 2) or U_A <= u < U_UP:
        return 4
    return 2


def small_products(u):
    names = []
    if u == SLOT_DIAG:
        names += [("diag", h) for h in range(HEADS)]
    if SLOT_LEVEL <= u < SLOT_LEVEL + LEVELS:
        names += [("lev", u - SLOT_LEVEL, h) for h in range(HEADS)]
    if u == SLOT_KDT:
        names += [("kdT", t) for t in range(TT)]
    if u == SLOT_UPD:
        names += [("upd", c) for c in range(4)]
    if u == SLOT_UPD + 1:
        names += [("upd", c) for c in range(4, NCHUNK - 1)]
    if u == SLOT_O:
        names += [("o", h) for h in range(HEADS)]
    if u == SLOT_SS:
        names += [("ss", h) for h in range(HEADS)]
    for p in range(PAIRS):
        s = U_PAIR + 3 * p + 2
        if u == s:
            names += [("S", p, hh, j) for hh in range(2) for j in range(score_banks(p))]
        if u == s + 1:
            names += [("T", p, hh, j) for hh in range(2) for j in range(score_banks(p))]
        if u == s + 2:
            names += [("O", p, hh) for hh in range(2)]
    if u == SLOT_STAT:
        names += [("mT", g) for g in range(NG)]
    if u == SLOT_STAT + 1:
        names += [("sT", g) for g in range(NG)]
    if SLOT_BC <= u < SLOT_BC + HEADS:
        names += [("bc", u - SLOT_BC, g) for g in range(NG)]
    if u in (SLOT_ROW, SLOT_ROW + 1):
        names += [("row", u - SLOT_ROW, i) for i in range(2)]
    if u in MOD_UNITS:
        names.append(("mod2", u))
    return names


BANKS = plan_banks()

BLOCKS0 = [(0, 0), (1, 0), (1, 1), (2, 1), (2, 2), (3, 2), (3, 3)]
BLOCKS1 = [(i, i) for i in range(TT)]


def blocks_of(p):
    return BLOCKS0 if p // 2 == 0 else BLOCKS1


def block_bank(p, n):
    if p // 2 == 0:
        return (0, n * P) if n < 3 else (1, (n - 3) * P)
    return 0, n * P


def layer_kernel(nc, x, c, w_ada, b_ada, g_norm_mix, w_in, lb_logits, g_hg_norm, w_branch_a, w_branch_b, w_out,
                 g_norm_ffn, w_up, conv_w, conv_b, w_down, g_final, out):
    with ExitStack() as ctx:
        BASE = 16512

        def at(name, kb, shape, dt=F32):
            return nc.alloc_sbuf_tensor_at(name, shape, dt, offset=BASE + int(kb * KB))

        raw = [at(f"w_raw{i}", 120 + 8 * i, [P, 2048]) for i in range(2)]
        whi = [at(f"w_hi{i}", 136 + 8 * i, [P, 2048], F32R) for i in range(2)]
        wlo = [at(f"w_lo{i}", 152 + 8 * i, [P, 2048], F32R) for i in range(2)]
        raw.append(at("w_raw_2", 48, [P, 2048]))
        whi.append(at("w_hi_2", 64, [P, 2048], F32R))
        wlo.append(at("w_lo_2", 72, [P, 2048], F32R))
        h_hi = at("h_hi", 168, [P, KT, S], F32R)
        h_lo = at("h_lo", 184, [P, KT, S], F32R)

        x_in = at("x_in", 0, [P, TT, D])
        xn_in = at("xn_in", 16, [P, TT, D])
        ada = [at(f"ada{i}", 32 + 8 * i, [P, KT, 256]) for i in range(MOD_FIRST)]
        part = at("part", 96, [P, 4, 256])
        h_tmp = at("h_tmp", 100, [P, 4, S])
        hq = at("hq", 0, [P, HEADS, S])
        hk = at("hk", 8, [P, HEADS, S])
        hp = at("hp", 16, [P, HEADS, S])
        hv = at("hv", 24, [P, TT, HW])
        dec = at("dec", 32, [P, HEADS, S])
        zz = [at("z0", 40, [P, HEADS, S]), at("z1", 48, [P, HEADS, S])]
        q_odd = at("q_odd", 48, [P, HEADS, S])
        scT = at("scT", 56, [P, HEADS, S])
        kd = at("kd", 8, [P, TT, HW])
        st_a = at("st_a", 16, [P, 4, HW])
        st_b = at("st_b", 32, [P, 3, HW])
        o_sb = at("o_sb", 8, [P, HEADS, S])
        o_sq = at("o_sq", 48, [P, HEADS, S])
        o_rs = at("o_rs", 0, [P, HEADS, S])
        yh = at("yh", 32, [P, HEADS, S])
        sgt = at("sgt", 56, [P, 2, S])
        ya_hi = at("ya_hi", 40, [P, HEADS, S], F32R)
        ya_lo = at("ya_lo", 48, [P, HEADS, S], F32R)
        qa = at("qa", 64, [P, 2, S])
        ka = at("ka", 68, [P, 2, S])
        va = at("va", 72, [P, TT, 256])
        prob = at("prob", 76, [P, 2, 7 * P])
        probT = at("probT", 83, [P, 2, 7 * P])
        og = at("og", 90, [P, NG, HEADS, S])
        m_row = at("m_row", 32, [HEADS, NG, S])
        s_row = at("s_row", 56, [HEADS, NG, S])
        wg_hi = at("wg_hi", 56, [HEADS, NG, S], F32R)
        wg_lo = at("wg_lo", 32, [HEADS, NG, S], F32R)
        yb_hi = at("yb_hi", 64, [P, HEADS, S], F32R)
        yb_lo = at("yb_lo", 76, [P, HEADS, S], F32R)
        sga = at("sga", 0, [P, KT, S])
        sgb = at("sgb", 16, [P, KT, S])
        m_hi = at("m_hi", 90, [P, KT, S], F32R)
        m_lo = at("m_lo", 32, [P, KT, S], F32R)
        x1 = at("x1", 48, [P, TT, D])
        g1_row = at("g1_row", 72, [P, D])
        g2_row = at("g2_row", 112, [P, D])
        gf_row = at("gf_row", 108, [P, D])
        xn_ffn = at("xn_ffn", 0, [P, TT, D])
        h_tmp2 = [at("h_tmp2a", 116, [P, 2, S]), at("h_tmp2b", 44, [P, 2, S])]
        act_hi = at("act_hi", 0, [P, FT, S], F32R)
        act_lo = at("act_lo", 64, [P, FT, S], F32R)
        conv = at("conv", 44, [P, 2, S])
        gelu = at("gelu", 116, [P, 2, S])
        xg = at("xg", 168, [P, TT, D])
        squares = at("squares", 184, [P, TT, D])
        masks = at("masks", 116, [P, LEVELS, S // 2], I8)
        diag = at("diag", 118, [P, S], I8)
        ada2 = [at(f"ada2_{i}", 16 + 8 * i, [P, KT, 256]) for i in range(2)]
        part2 = [at(f"part2_{i}", kb, [P, 256]) for i, kb in enumerate((78, 81.5, 85, 88.5))]
        B_ADA, G_MIX, G_FFN, G_HG, LB, N_VEC = 0, 48, 56, 64, 68, 76
        off = 200.0

        def small(name, cols, rows=P, dt=F32):
            nonlocal off
            t = at(name, off, [rows, cols], dt)
            off += -(-cols * 4 // 32) * 32 / KB
            return t

        ident = small("ident", P)
        ones = small("ones", P)
        dist0 = small("dist0", 2 * P)
        dist1 = small("dist1", P)
        dist2 = small("dist2", P)
        dint = at("dint", 119, [P, P], mybir.dt.int32)
        c_rows = small("c_rows", P, KT)
        vec_rows = small("vec_rows", P, N_VEC)
        conv_rows = small("conv_rows", P, 88)
        vec = small("vec", N_VEC)
        convc = small("convc", 88)
        mod = small("mod", 48)
        csig = small("csig", 8)
        csilu = small("csilu", 8)
        lbd = small("lbd", 4)
        lb = small("lb", 4)
        oml = small("oml", 4)
        a1 = small("a1", 8)
        a2 = small("a2", 8)
        gp = small("gp", 16)
        ssq = small("ssq", 12)
        ssp = small("ssp", 16)
        rstd = small("rstd", 12)
        nmax = small("nmax", 48)
        ssum = small("ssum", 48)
        mx = small("mx", 8)
        eglast = small("eglast", 32)
        epsc = small("epsc", 1)
        mhalf = small("mhalf", 4)
        pick = small("pick", HEADS, HEADS, F32R)
        inv = at("inv", 62, [HEADS, S])
        assert BASE + off * KB <= nc.sbuf_usable_end, off

        bank = [ctx.enter_context(nc.psum_tensor(f"bank{i}", [P, 512], F32)) for i in range(8)]

        def sem(name):
            return ctx.enter_context(nc.semaphore(name))

        full = [sem(f"bank_full{b}") for b in range(8)]
        free = [sem(f"bank_free{b}") for b in range(8)]
        raw_in = [sem(f"raw_in{i}") for i in range(2)]
        hi_done = sem("hi_done")
        share_in = [sem(f"share_in{j}") for j in range(KT // 2)]
        hi_share, lo_share = sem("hi_share"), sem("lo_share")
        lo_done = sem("lo_done")
        down_used = sem("down_used")
        x_in_s = [sem(f"x_landed{t}") for t in range(TT)]
        x_again = sem("x_again")
        c_in, vec_in = sem("c_in"), sem("vec_in")
        ada_in = [sem(f"ada_in{i}") for i in range(MOD_FIRST)]
        ada2_in = [sem(f"ada2_in{i}") for i in range(2)]
        part_done = sem("part_done")
        scaled_done = sem("scaled_done")
        rest_done = sem("rest_done")
        mod1_done = sem("mod1_done")
        part_chain = [sem("part_chain0"), sem("part_chain1")]
        gf_in = sem("gf_in")
        masks_done = sem("masks_done")
        consts = sem("consts")
        dchain = sem("dve_chain")
        glast_done = sem("glast_done")
        pchain = sem("pool_chain")
        csig_done, lbd_done = sem("csig_done"), sem("lbd_done")
        lb_done = sem("lb_done")
        sq_done = sem("sq_done")
        rstd_done = sem("rstd_done")
        xn_done = [sem("xn_act"), sem("xn_dve")]
        h_hi_done = sem("h_hi_done")
        h_lo_done = [sem("h_lo_even"), sem("h_lo_odd")]
        ssp_done = sem("ssp_done")
        ssq_done = sem("ssq_done")
        sig_done = sem("sig_done")
        f_done, logf_done = sem("f_done"), sem("logf_done")
        d1_done, e_done, z_done, p_done = sem("d1_done"), sem("e_done"), sem("z_done"), sem("p_done")
        eg_done, kdif_done, ke_done, kdec_done = sem("eg_done"), sem("kdif_done"), sem("ke_done"), sem("kdec_done")
        odd_done = sem("odd_done")
        osq_done, rs_done, yfull_done, yahi_done, yalo_done = (
            sem("osq_done"), sem("rs_done"), sem("yfull_done"), sem("yahi_done"), sem("yalo_done"))
        nmax_done, prob_done = sem("nmax_done"), sem("prob_done")
        pick_done = sem("pick_done")
        mdiff_done, wexp_done, crow_done = sem("mdiff_done"), sem("wexp_done"), sem("crow_done")
        ybfull_done, ybhi_done, yblo_done = sem("ybfull_done"), sem("ybhi_done"), sem("yblo_done")
        mfull_done, mhi_done, mlo_done = sem("mfull_done"), sem("mhi_done"), sem("mlo_done")
        gp_done, x1_done = sem("gp_done"), sem("x1_done")
        conv0_done, tap_done, gelu_done, ahi_done, alo_done = (
            sem("conv0_done"), sem("tap_done"), sem("gelu_done"), sem("ahi_done"), sem("alo_done"))
        xg_done, xg_last = sem("xg_done"), sem("xg_last")
        y_last = [sem("y_last_tile_2"), sem("y_last_half_0"), sem("y_last_half_1")]
        x2_done, y_done, out_done = sem("x2_done"), sem("y_done"), sem("out_done")

        def claim(eng, name):
            b, n = BANKS[name]
            if n:
                eng.wait_ge(free[b], n)
            return bank[b]

        def filled(ins, name):
            ins.then_inc(full[BANKS[name][0]], 1)

        def ready(eng, name):
            b, n = BANKS[name]
            eng.wait_ge(full[b], n + 1)
            return bank[b]

        def release(ins, name):
            ins.then_inc(free[BANKS[name][0]], 1)

        def evacuated(eng, name):
            b, n = BANKS[name]
            eng.wait_ge(free[b], n + 1)

        def scaled_before(n):
            return START_ADA.index(n) * (KT - MOD_KTS)

        def h_part(which, k):
            return h_tmp[:, k % 4, :] if which == 0 else h_tmp2[k // 2 % 2][:, k % 2, :]

        def cols_of(w, c0):
            return w[0][:, bass.ds(c0, 256)].rearrange("(k p) c -> p k c", p=P)

        def unit_source(u):
            if u < U_PAIR:
                return cols_of(w_in, 256 * u)
            if u < U_HG:
                p, what = divmod(u - U_PAIR, 3)
                return cols_of(w_in, (C_AQ, C_AK, C_AV)[what] + 256 * p)
            if u < U_GA:
                return cols_of(w_in, C_HG + 256 * (u - U_HG))
            if u < U_A:
                return cols_of(w_in, C_GATES + 256 * (u - U_GA))
            if u < U_OUT:
                w, j = (w_branch_a, u - U_A) if u < U_B else (w_branch_b, u - U_B)
                return w[0][:, 512 * j:512 * j + 512].rearrange("(k p) c -> p k c", p=P)
            return cols_of(w_out, 256 * (u - U_OUT))

        x_tok = x[0].rearrange("(t p) d -> p t d", p=P)
        out_tok = out[0].rearrange("(t p) d -> p t d", p=P)

        block = ctx.enter_context(nc.Block())

        @block.sync
        def _(sp):
            def rows(dst, r0, src, n):
                sp.dma_start(dst[r0:r0 + n, :], src).then_inc(vec_in, 16)

            def load_unit(u, src, slot):
                sp.wait_ge(hi_done, u - 1)
                sp.wait_ge(lo_done, u - 1)
                width = src.shape[2]
                sp.dma_start(raw[slot][:, :].rearrange("p (k c) -> p k c", c=width), src).then_inc(raw_in[slot], 16)

            sp.dma_start(c_rows[:, :], c.rearrange("b (k p) -> (b k) p", p=P)).then_inc(c_in, 16)
            for step, n in START:
                if step == "x":
                    for t in range(TT):
                        sp.dma_start(x_in[:, t, :], x_tok[:, t, :]).then_inc(x_in_s[t], 16)
                if step == "vec":
                    rows(vec_rows, B_ADA, b_ada.rearrange("l (k p) -> (l k) p", p=P), 48)
                    rows(vec_rows, G_MIX, g_norm_mix.rearrange("l (k p) -> (l k) p", p=P), 8)
                    rows(vec_rows, G_FFN, g_norm_ffn.rearrange("l (k p) -> (l k) p", p=P), 8)
                    rows(vec_rows, G_HG, g_hg_norm.rearrange("l h p -> (l h) p"), 4)
                    rows(vec_rows, LB, lb_logits.rearrange("l (k p) -> (l k) p", p=P), 8)
                    rows(conv_rows, 0, conv_w.rearrange("l j (k p) -> (l j k) p", p=P), 66)
                    rows(conv_rows, 66, conv_b.rearrange("l (k p) -> (l k) p", p=P), 22)
                if step == "ada":
                    sp.dma_start(ada[n][:, :, :], cols_of(w_ada, 256 * n)).then_inc(ada_in[n], 16)
                if step == "share":
                    for u in range(2):
                        sp.dma_start(raw[u][:, 512 * n:512 * n + 512].rearrange("p (k c) -> p k c", c=256),
                                     unit_source(u)[:, 2 * n:2 * n + 2, :]).then_inc(share_in[n], 16)
                if step == "unit":
                    sp.wait_ge(part_done, 5)
                    sp.dma_start(raw[2][:, :].rearrange("p (k c) -> p k c", c=256), unit_source(n)).then_inc(raw_in[0], 16)
            for u in range(U_UP):
                if u == U_B + 2:
                    ready(sp, ("g", U_B - 1, 3))
                    sp.wait_ge(yblo_done, HEADS)
                    sp.dma_start(x1[:, :, :], x_tok).then_inc(x_again, 16)
                    sp.dma_start(gf_row[:, :], g_final.rearrange("(a d) -> a d", a=1).broadcast_to([P, D])).then_inc(gf_in, 16)
                if u >= 3:
                    load_unit(u, unit_source(u), u % 2)
                if u == MOD_SLOT:
                    ready(sp, ("o", HEADS - 1))
                for n in MOD_UNITS.get(u, ()):
                    if n >= MOD_FIRST + 2:
                        sp.wait_ge(part_done, n - 1)
                    sp.dma_start(ada2[n % 2][:, :, :], cols_of(w_ada, 256 * n)).then_inc(ada2_in[n % 2], 16)
            with sp.Fori(0, FT // 2) as i:
                load_unit(2 * i + U_UP, cols_of(w_up, i * 256), 0)
                load_unit(2 * i + U_UP + 1, cols_of(w_up, i * 256 + D_FF), 1)

            def down_rows(i):
                return w_down[0][bass.ds(i * 256, 256), :].rearrange("(k p) c -> p k c", p=P)

            with sp.Fori(0, FT // 4) as i:
                load_unit(2 * i + U_DOWN, down_rows(2 * i), 0)
                load_unit(2 * i + U_DOWN + 1, down_rows(2 * i + 1), 1)
            load_unit(N_UNITS - 1, down_rows(FT // 2 - 1), 0)

            pieces = [(t, slice(0, D)) for t in range(TT - 1)] + [(TT - 1, slice(512 * i, 512 * i + 512)) for i in range(2)]
            for i, (t, cols) in enumerate(pieces):
                if t < TT - 2:
                    sp.wait_ge(y_done, t + 1)
                else:
                    sp.wait_ge(y_last[i - (TT - 2)], 1)
                sp.dma_start(out_tok[:, t, cols], x1[:, t, cols]).then_inc(out_done, 16)
            sp.wait_ge(out_done, 16 * (TT + 1))

        @block.gpsimd
        def _(pool):
            n_chain = [0]

            def link(ins):
                n_chain[0] += 1
                ins.then_inc(pchain, 1)
                pool.wait_ge(pchain, n_chain[0])

            def select(t, pattern, base, mult, op=ALU.is_ge, fill=0.0):
                link(pool.affine_select(out=t, in_=t, compare_op=op, fill=fill, base=base, pattern=pattern,
                                        channel_multiplier=mult))

            link(pool.memset(ident[:, :], 0.0))
            select(ident[:, :], [[-1, P]], 0, 1, ALU.not_equal, 1.0)
            link(pool.memset(ones[:, :], 1.0))
            link(pool.memset(mhalf[:, :], -0.5))
            pool.memset(epsc[:, :], EPS).then_inc(consts, 1)

            def inverse_root(first, n):
                cols = slice(first, first + n)
                link(pool.tensor_scalar(rstd[:, cols], ssq[:, cols], 1.0 / D, EPS, ALU.mult, ALU.add))
                pool.tensor_tensor(rstd[:, cols], rstd[:, cols], mhalf[:, 0:n], ALU.pow).then_inc(rstd_done, 1)

            def build_distances():
                link(pool.memset(diag[:, :], 1.0))
                select(diag[:, :].rearrange("p (a t) -> p a t", a=4), [[0, 4], [1, P]], 0, -1, ALU.is_equal)
                for dist, n in ((dist0, 2), (dist1, 1)):
                    link(pool.iota(dist[:, :], [[-1, n * P]], base=(n - 1) * P, channel_multiplier=1,
                                   allow_small_or_imprecise_dtypes=True))
                    select(dist[:, :], [[-1, n * P]], (n - 1) * P, 1, fill=FAR)
                    if n == 2:
                        select(dist[:, :], [[1, n * P]], 0, -1, fill=FAR)
                pool.iota(dint[:, :], [[-1, P]], base=P, channel_multiplier=1).then_inc(consts, 1)

            def build_masks(levels):
                for j in levels:
                    half = 1 << j
                    nb = P // (2 * half)
                    m = masks[:, j, :].rearrange("p (rep blk tok) -> p rep blk tok", rep=4, blk=nb)
                    link(pool.memset(masks[:, j, :], 1.0))
                    select(m, [[0, 4], [-2 * half, nb], [0, half]], 0, 1)
                    pool.affine_select(out=m, in_=m, compare_op=ALU.is_ge, fill=0.0, base=half - 1,
                                       pattern=[[0, 4], [2 * half, nb], [0, half]],
                                       channel_multiplier=-1).then_inc(masks_done, 1)

            def low_h(which, k):
                pool.wait_ge(h_hi_done, which * KT + k + 1)
                pool.tensor_tensor(h_lo[:, k, :], h_part(which, k), h_hi[:, k, :].bitcast(F32),
                                   ALU.subtract).then_inc(h_lo_done[1], 1)

            def low_part(u, slot):
                pool.wait_ge(hi_done, u + 1)
                pool.tensor_tensor(wlo[slot][:, :], raw[slot][:, :], whi[slot][:, :].bitcast(F32),
                                   ALU.subtract).then_inc(lo_done, 1)

            for step, n in START:
                if step == "ada":
                    unit = ada[n]
                    for k in range(MOD_KTS + 1, KT):
                        pool.wait_ge(scaled_done, scaled_before(n) + k - MOD_KTS + 1)
                        ins = pool.tensor_tensor(unit[:, MOD_KTS, :], unit[:, MOD_KTS, :], unit[:, k, :], ALU.add)
                        if k < KT - 1:
                            link(ins)
                    ins.then_inc(rest_done, 1)
                if step == "x":
                    pool.wait_ge(sq_done, TT)
                    inverse_root(0, TT)
                if step == "share":
                    for u in range(2):
                        cols = slice(512 * n, 512 * n + 512)
                        if n < KT // 2 - 1:
                            pool.wait_ge(hi_share, 2 * n + u + 1)
                        else:
                            pool.wait_ge(hi_done, u + 1)
                        pool.tensor_tensor(wlo[u][:, cols], raw[u][:, cols], whi[u][:, cols].bitcast(F32),
                                           ALU.subtract).then_inc(lo_share if n < KT // 2 - 1 else lo_done, 1)
                if step == "h":
                    low_h(0, 2 * n + 1)
            low_part(2, 2)
            build_distances()
            for u, levels in ((3, (0,)), (4, (1, 2)), (5, (3, 4, 5))):
                low_part(u, u % 2)
                build_masks(levels)
            with pool.Fori(0, U_UP // 2 - 3) as i:
                low_part(2 * i + 6, 0)
                low_part(2 * i + 7, 1)
            low_part(U_UP, 0)
            for t in range(TT):
                pool.wait_ge(ssq_done, t + 1)
                inverse_root(TT + t, 1)
            low_part(U_UP + 1, 1)
            pool.wait_ge(h_lo_done[1], KT // 2 + 1)
            for k in range(3, KT, 2):
                low_h(1, k)
            with pool.Fori(0, (N_UNITS - U_UP) // 2 - 1) as i:
                low_part(2 * i + U_UP + 2, 0)
                low_part(2 * i + U_UP + 3, 1)
            low_part(N_UNITS - 1, 0)
            for t in range(TT):
                if t < TT - 2:
                    if t == 0:
                        pool.wait_ge(gf_in, 16)
                    pool.wait_ge(x2_done, 2 * t + 2)
                    pool.tensor_tensor(xg[:, t, :], x1[:, t, :], gf_row[:, :], ALU.mult).then_inc(xg_done, 1)
                pool.wait_ge(sq_done, TT + 2 * t + 2)
                col = 2 * TT + t
                link(pool.tensor_tensor(ssq[:, col:col + 1], ssp[:, 2 * t:2 * t + 1], ssp[:, 2 * t + 1:2 * t + 2], ALU.add))
                inverse_root(col, 1)

        @block.scalar
        def _(act):
            def high_part(slot, landed, bufs=None):
                bufs = slot if bufs is None else bufs
                act.wait_ge(raw_in[slot], landed - 16)
                act.activation(whi[bufs][:, :], raw[bufs][:, :], ACT.Copy).then_inc(hi_done, 1)

            def unit_high(u):
                if u > U_DOWN + 1:
                    act.wait_ge(down_used, u - 1 - U_DOWN)
                elif u == 2:
                    act.wait_ge(part_done, 4)
                elif u > 2:
                    ready(act, ("g", u - 2, tiles_of(u - 2) - 1))
                high_part(u % 2, 16 * (u // 2 + 1), 2 if u == 2 else None)

            b = ready(act, "cT")
            act.activation(csig[:, :], b[:, 0:KT], ACT.Sigmoid).then_inc(csig_done, 1)
            def first_h(j):
                act.wait_ge(mod1_done, j + 1)
                for k in (2 * j, 2 * j + 1):
                    b = ready(act, ("xT", 0, k))
                    if k >= 4:
                        act.wait_ge(h_lo_done[k % 2], (k - 4) // 2 + 1)
                    release(act.activation(h_part(0, k), b[:, :], ACT.Identity, scale=a1[:, k:k + 1],
                                           bias=mod[:, k:k + 1]), ("xT", 0, k))
                for k in (2 * j, 2 * j + 1):
                    evacuated(act, ("xT", 0, k))
                    act.activation(h_hi[:, k, :], h_part(0, k), ACT.Copy).then_inc(h_hi_done, 1)

            act.wait_ge(consts, 1)
            act.activation(pick[:, :], ident[0:HEADS, 0:HEADS], ACT.Copy).then_inc(pick_done, 1)
            evacuated(act, "cT")
            for step, n in START:
                if step == "ada":
                    act.wait_ge(ada_in[n], 16)
                    for k in range(MOD_KTS, KT):
                        act.activation(ada[n][:, k, :], ada[n][:, k, :], ACT.Copy,
                                       scale=csilu[:, k:k + 1]).then_inc(scaled_done, 1)
                if step == "x":
                    for t in range(TT):
                        act.wait_ge(x_in_s[t], 16)
                        act.activation(squares[:, t, :], x_in[:, t, :], ACT.Square,
                                       accum_out=ssq[:, t:t + 1]).then_inc(sq_done, 1)
                if step == "xn":
                    act.wait_ge(rstd_done, 1)
                    for t in range(TT // 2):
                        act.activation(xn_in[:, t, :], x_in[:, t, :], ACT.Copy, scale=rstd[:, t:t + 1]).then_inc(xn_done[0], 1)
                if step == "share":
                    if n == 1:
                        act.wait_ge(lbd_done, 1)
                        act.activation(lb[:, :], lbd[:, :], ACT.Sigmoid).then_inc(lb_done, 1)
                    act.wait_ge(share_in[n], 16 * 2)
                    for u in range(2):
                        cols = slice(512 * n, 512 * n + 512)
                        act.activation(whi[u][:, cols], raw[u][:, cols],
                                       ACT.Copy).then_inc(hi_share if n < KT // 2 - 1 else hi_done, 1)
                if step == "unit":
                    unit_high(n)
                if step == "h":
                    first_h(n)

            def small_results(u):
                if u == SLOT_DIAG:
                    act.wait_ge(f_done, HEADS)
                    act.activation(hp[:, :, :], hp[:, :, :], ACT.Ln).then_inc(logf_done, 1)
                if SLOT_LEVEL <= u < SLOT_LEVEL + LEVELS:
                    level_exp(u - SLOT_LEVEL)
                if u == SLOT_KDT:
                    act.wait_ge(p_done, LEVELS)
                    act.activation(dec[:, :, :], hp[:, :, :], ACT.Exp).then_inc(eg_done, 1)
                    g_last = hp[:, :, :].rearrange("p h (c t) -> p (h c) t", t=CHUNK)[:, :, CHUNK - 1]
                    act.activation(eglast[:, :], g_last, ACT.Exp).then_inc(glast_done, 1)
                    act.wait_ge(kdif_done, 1)
                    act.activation(dec[:, :, :], dec[:, :, :], ACT.Exp).then_inc(ke_done, 1)
                if u == SLOT_KDT + 1:
                    b = ready(act, ("kdT", TT - 1))
                    release(act.activation(kd[:, TT - 1, :], b[:, :], ACT.Copy), ("kdT", TT - 1))
                if u == SLOT_O + 1:
                    for h in range(HEADS):
                        b = ready(act, ("o", h))
                        release(act.activation(o_sb[:, h, :], b[:, :], ACT.Copy), ("o", h))
                if u == SLOT_SS + 1:
                    for h in range(HEADS):
                        b = ready(act, ("ss", h))
                        release(act.activation(o_rs[:, h, :], b[:, :], ACT.Ln, scale=1.0 / 128, bias=epsc[:, :]), ("ss", h))
                    for h in range(HEADS):
                        evacuated(act, ("ss", h))
                        act.activation(o_rs[:, h, :], o_rs[:, h, :], ACT.Exp, scale=-0.5).then_inc(rs_done, 1)
                for p in range(PAIRS):
                    s = U_PAIR + 3 * p + 2
                    if u == s + 1:
                        softmax_exp(p)
                    if u == s + 2:
                        if p:
                            ready(act, ("O", p - 1, 1))
                        copy_probT(p, 1)
                    if u == s + 3:
                        scatter_o(p, 1)
                if u == SLOT_STAT + 1:
                    for g in range(NG):
                        gather_row(m_row, "mT", g)
                if u == SLOT_STAT + 2:
                    for g in range(NG):
                        gather_row(s_row, "sT", g)
                    act.wait_ge(mdiff_done, 1)
                    act.activation(m_row[:, :, :], m_row[:, :, :], ACT.Exp).then_inc(wexp_done, 1)
                if SLOT_BC < u <= SLOT_BC + HEADS:
                    h = u - SLOT_BC - 1
                    act.wait_ge(ybfull_done, h + 1)
                    act.activation(yb_hi[:, h, :], og[:, 0, h, :], ACT.Copy).then_inc(ybhi_done, 1)
                if u in (SLOT_ROW + 1, SLOT_ROW + 2):
                    w = u - SLOT_ROW - 1
                    if w == 1:
                        act.wait_ge(yblo_done, HEADS)
                    for i in range(2):
                        b = ready(act, ("row", w, i))
                        row = (g1_row, g2_row)[w]
                        release(act.activation(row[:, 512 * i:512 * i + 512], b[:, :], ACT.Copy), ("row", w, i))

            def level_exp(j):
                half = 1 << j
                pv = hp[:, :, :].rearrange("p h (blk pos tok) -> p (h blk) pos tok", pos=2, tok=half)
                dv = dec[:, :, :].rearrange("p h (blk pos tok) -> p (h blk) pos tok", pos=2, tok=half)
                act.wait_ge(d1_done, j + 1)
                act.activation(dv[:, :, 1, :], pv[:, :, 1, :], ACT.Exp)
                act.activation(dv[:, :, 0, :], dv[:, :, 0, :], ACT.Exp).then_inc(e_done, 1)

            def softmax_exp(p):
                g, h0, _ = pair(p)
                for hh in range(2):
                    act.wait_ge(nmax_done, 2 * p + hh + 1)
                    at_ = 0
                    for q in range(TT):
                        n = sum(b[0] == q for b in blocks_of(p)) * P
                        col = (g * TT + q) * HEADS + h0 + hh
                        ins = act.activation(prob[:, hh, at_:at_ + n], prob[:, hh, at_:at_ + n], ACT.Exp, scale=SCALE,
                                             bias=nmax[:, col:col + 1], accum_out=ssum[:, col:col + 1])
                        at_ += n
                    ins.then_inc(prob_done, 1)

            def copy_probT(p, hh):
                for j in range(score_banks(p)):
                    b = ready(act, ("T", p, hh, j))
                    n = sum(block_bank(p, i)[0] == j for i in range(len(blocks_of(p)))) * P
                    release(act.activation(probT[:, hh, 3 * P * j:3 * P * j + n], b[:, 0:n], ACT.Copy), ("T", p, hh, j))

            def scatter_o(p, hh):
                g, h0, d = pair(p)
                b = ready(act, ("O", p, hh))
                release(act.activation(og[:, g, h0 + hh, :].rearrange("p (l res) -> p res l", res=d),
                                    b[:, :].rearrange("p (res l) -> p res l", res=d), ACT.Copy), ("O", p, hh))

            def gather_row(dst, name, g):
                d = ORDER[g]
                b = ready(act, (name, g))
                release(act.activation(dst[:, g, :].rearrange("p (l res) -> p res l", res=d),
                                    b[0:HEADS, :].rearrange("p (res l) -> p res l", res=d), ACT.Copy), (name, g))

            def evacuate(u):
                if u < U_HI:
                    for t in range(2):
                        h = 2 * (u % 2) + t
                        if u >= U_HF:
                            evacuated(act, ("g", u - 2, t))
                        b = ready(act, ("g", u, t))
                        ins = act.activation(dec[:, h, :], b[:, :], ACT.Sigmoid)
                        if u < U_HF:
                            ins.then_inc(sig_done, 1)
                        else:
                            release(ins, ("g", u, t))
                elif U_PAIR <= u < U_HG:
                    p, what = divmod(u - U_PAIR, 3)
                    if what == 0:
                        g, h0, d = pair(p)
                        if p:
                            ready(act, ("S", p - 1, 1, score_banks(p - 1) - 1))
                        for t in range(2):
                            b = ready(act, ("g", u, t))
                            release(act.activation(qa[:, t, :].rearrange("p (res l) -> p res l", res=d),
                                                b[:, :].rearrange("p (l res) -> p res l", res=d), ACT.Copy), ("g", u, t))
                elif U_HG <= u < U_GA:
                    for t in range(2):
                        h = 2 * (u - U_HG) + t
                        if h >= 2:
                            act.wait_ge(yfull_done, h - 1)
                        b = ready(act, ("g", u, t))
                        act.activation(sgt[:, h % 2, :], b[:, :], ACT.Sigmoid).then_inc(sig_done, 1)
                    for t in range(2):
                        h = 2 * (u - U_HG) + t
                        act.wait_ge(yfull_done, h + 1)
                        act.activation(ya_hi[:, h, :], yh[:, h, :], ACT.Copy).then_inc(yahi_done, 1)
                elif U_GA <= u < U_A:
                    dst, u0 = (sga, U_GA) if u < U_GB else (sgb, U_GB)
                    if u == U_GA:
                        act.wait_ge(yalo_done, HEADS)
                    for t in range(2):
                        b = ready(act, ("g", u, t))
                        release(act.activation(dst[:, 2 * (u - u0) + t, :], b[:, :], ACT.Sigmoid), ("g", u, t))
                elif U_B <= u < U_OUT:
                    if u == U_B:
                        act.wait_ge(yblo_done, HEADS)
                    for t in range(4):
                        f = 4 * (u - U_B) + t
                        act.wait_ge(mfull_done, f + 1)
                        act.activation(m_hi[:, f, :], sgb[:, f, :], ACT.Copy).then_inc(mhi_done, 1)
                elif u >= U_OUT:
                    v = u - U_OUT
                    for t in range(TT):
                        act.wait_ge(x1_done, TT * v + t + 1)
                        act.activation(xn_ffn[:, t, 256 * v:256 * v + 256], x1[:, t, 256 * v:256 * v + 256],
                                       ACT.Square, accum_out=ssp[:, 4 * t + v:4 * t + v + 1]).then_inc(ssp_done, 1)
                        if u == U_UP - 1 and t == 2:
                            for i in range(2):
                                xn_again(i, slice(0, D))

            def xn_again(t, cols):
                act.wait_ge(rstd_done, 2 + t)
                act.activation(xn_ffn[:, t, cols], x1[:, t, cols], ACT.Copy,
                               scale=rstd[:, TT + t:TT + t + 1]).then_inc(xn_done[0], 1)

            for u in range(U_UP):
                if u >= 2:
                    unit_high(u + 1)
                small_results(u)
                evacuate(u)

            xn_again(TT - 1, slice(512, D))
            high_part(1, 8 * (U_UP + 2))
            for k in range(KT):
                evacuated(act, ("xT", 1, k))
                act.activation(h_hi[:, k, :], h_part(1, k), ACT.Copy).then_inc(h_hi_done, 1)

            CW = convc[:, :]
            with act.Fori(0, FT // 2) as i:
                for t in range(2):
                    act.wait_ge(full[t], BANKS[f"gate{t}"][1] + 1 + i)
                    act.activation(conv[:, t, :], bank[t][:, :], ACT.Identity,
                                   scale=CW[:, bass.ds(2 * i + (2 * FT + t), 1)],
                                   bias=CW[:, bass.ds(2 * i + (3 * FT + t), 1)]).then_inc(conv0_done, 1)
                high_part(0, 8 * (U_UP + 4) + 16 * i)
                for t in range(2):
                    act.wait_ge(free[t], BANKS[f"gate{t}"][1] + 1 + i)
                    act.activation(gelu[:, t, :], conv[:, t, :], ACT.Gelu_apprx_tanh).then_inc(gelu_done, 1)
                for t in range(2):
                    act.wait_ge(free[2 + t], BANKS[f"val{t}"][1] + 1 + i)
                    act.activation(act_hi[:, bass.ds(2 * i + t, 1), :].rearrange("p a s -> p (a s)"), gelu[:, t, :],
                                   ACT.Copy).then_inc(ahi_done, 1)
                high_part(1, 8 * (U_UP + 4) + 16 * i)
            for u in range(U_DOWN + 2, N_UNITS):
                unit_high(u)
            def scaled_out(t, cols, landed):
                act.wait_ge(rstd_done, 2 + TT + t)
                act.activation(x1[:, t, cols], xg[:, t, cols], ACT.Copy,
                               scale=rstd[:, 2 * TT + t:2 * TT + t + 1]).then_inc(landed, 1)

            for t in range(TT):
                for half in range(2):
                    act.wait_ge(x2_done, 2 * t + half + 1)
                    cols = slice(512 * half, 512 * half + 512)
                    act.activation(squares[:, t, cols], x1[:, t, cols], ACT.Square,
                                   accum_out=ssp[:, 2 * t + half:2 * t + half + 1]).then_inc(sq_done, 1)
                if 0 < t < TT - 1:
                    act.wait_ge(xg_done, t)
                    scaled_out(t - 1, slice(0, D), y_done)
            act.wait_ge(xg_last, 1)
            for half in range(2):
                scaled_out(TT - 1, slice(512 * half, 512 * half + 512), y_last[half + 1])

        @block.tensor
        def _(pe):
            def mm(o, lhsT, rhs, start=True, stop=True, **kw):
                return pe.matmul(o, lhsT, rhs, start=start, stop=stop, **kw)

            def transpose(o, i):
                return pe.transpose(o, i, ident[0:i.shape[0], 0:i.shape[0]])

            pe.wait_ge(consts, 1)
            pe.wait_ge(c_in, 16)
            b = claim(pe, "cT")
            filled(transpose(b[:, 0:KT], c_rows[:, :]), "cT")
            pe.wait_ge(vec_in, 16 * 7)
            b = claim(pe, "vec")
            transpose(b[:, 0:N_VEC], vec_rows[:, :])
            filled(transpose(b[:, N_VEC:N_VEC + 88], conv_rows[:, :]), "vec")

            def modulation(b, col, n, sums):
                pe.wait_ge(part_done, n + 1)
                for t in range(2):
                    ins = mm(b[:, col + t:col + t + 1], sums[:, t * P:(t + 1) * P], ones[:, 0:1])
                return ins

            def transposed_x(k):
                b = claim(pe, ("xT", 0, k))
                if k == 0:
                    pe.wait_ge(xn_done[0], TT // 2)
                    pe.wait_ge(xn_done[1], TT // 2)
                for t in range(TT):
                    ins = transpose(b[:, t * P:(t + 1) * P], xn_in[:, t, k * P:(k + 1) * P])
                filled(ins, ("xT", 0, k))

            def unit_parts(u, slot, width):
                pe.wait_ge(lo_done, u + 1)
                return [w[slot][:, :].rearrange("p (k c) -> p k c", c=width) for w in (whi, wlo)]

            def three_passes(o, lhs, rhs, k, last_k, start=None, skip=False):
                for i, (a, bb) in enumerate(((0, 0), (0, 1), (1, 0))):
                    ins = mm(o, lhs[a], rhs[bb], start=(k == 0 and i == 0) if start is None else start and i == 0,
                             stop=k == last_k and i == 2, skip_group_check=skip)
                return ins

            def feature_tile(o, parts, c0, acts, kts=KT):
                for k in range(kts):
                    ins = three_passes(o, [w[:, k, c0:c0 + P] for w in parts], [a[:, k, :] for a in acts], k, kts - 1)
                return ins

            def token_tile(o, parts, acts, tokens, kts=range(KT)):
                for k in kts:
                    if acts[0] is m_hi:
                        pe.wait_ge(mlo_done, k + 1)
                    ins = three_passes(o, [tokens(a[:, k, :]) for a in acts], [w[:, k, :] for w in parts], k, KT - 1)
                return ins

            def plain_tokens(t):
                return lambda a: a[:, t * P:(t + 1) * P]

            def dilated_tokens(t, d):
                if d == 1:
                    return plain_tokens(t)
                return lambda a: a.rearrange("p (l res) -> p res l", res=d)[:, t, :]

            def products(u):
                hT = (h_hi, h_lo)
                n = tiles_of(u)
                width = 512 if U_A <= u < U_OUT else 256
                parts = unit_parts(u, 2 if u == 2 else u % 2, width)
                for t in range(n):
                    b = claim(pe, ("g", u, t))
                    if u == U_A and t == 0:
                        pe.wait_ge(yalo_done, HEADS)
                    if u == U_B and t == 0:
                        pe.wait_ge(yblo_done, HEADS)
                    if u >= U_OUT:
                        merged = (m_hi, m_lo)
                        if u == U_OUT and t == 0:
                            token_tile(b[:, 0:256], parts, merged, plain_tokens(0), range(KT - 1))
                            b1 = claim(pe, ("g", u, 1))
                            token_tile(b1[:, 0:256], parts, merged, plain_tokens(1), range(KT - 1))
                        kts = range(KT - 1, KT) if u == U_OUT and t < 2 else range(KT)
                        ins = token_tile(b[:, 0:256], parts, merged, plain_tokens(t), kts)
                    elif u >= U_A:
                        ins = feature_tile(b[:, :], parts, t * P, (ya_hi, ya_lo) if u < U_B else (yb_hi, yb_lo), HEADS)
                    elif n == 4:
                        d = 1 if u < U_PAIR else pair((u - U_PAIR) // 3)[2]
                        ins = token_tile(b[:, 0:256], parts, hT, dilated_tokens(t, d))
                    else:
                        ins = feature_tile(b[:, :], parts, t * P, hT)
                    filled(ins, ("g", u, t))

            def scores(p):
                for hh in range(2):
                    for j in range(score_banks(p)):
                        b = claim(pe, ("S", p, hh, j))
                        if p // 2 == 0:
                            runs = [(0, 0, 1), (1, 0, 2)] if j == 0 else [(2, 1, 2), (3, 2, 2)]
                        else:
                            runs = [(i, i, 1) for i in range(TT)]
                        col = 0
                        for q, k, n in runs:
                            ins = mm(b[:, col:col + n * P], qa[:, hh, q * P:(q + 1) * P], ka[:, hh, k * P:(k + n) * P])
                            col += n * P
                        filled(ins, ("S", p, hh, j))

            def small(u):
                if u == SLOT_DIAG:
                    for t in range(4):
                        evacuated(pe, ("g", U_HQ + t // 2, t % 2))
                    pe.wait_ge(f_done, HEADS)
                    for h in range(HEADS):
                        b = claim(pe, ("diag", h))
                        for t in range(TT):
                            tok = slice(t * P, (t + 1) * P)
                            ins = mm(b[:, tok], hk[:, h, tok], hq[:, h, tok])
                        filled(ins, ("diag", h))
                if SLOT_LEVEL <= u < SLOT_LEVEL + LEVELS:
                    j = u - SLOT_LEVEL
                    pe.wait_ge(z_done, j + 1)
                    z = zz[j % 2]
                    for h in range(HEADS):
                        b = claim(pe, ("lev", j, h))
                        for t in range(TT):
                            tok = slice(t * P, (t + 1) * P)
                            ins = mm(b[:, tok], z[:, h, tok], z[:, h, tok])
                        filled(ins, ("lev", j, h))
                if u == SLOT_KDT:
                    pe.wait_ge(kdec_done, 1)
                    for t in range(TT):
                        b = claim(pe, ("kdT", t))
                        for h in range(HEADS):
                            ins = transpose(b[:, h * P:(h + 1) * P], zz[1][:, h, t * P:(t + 1) * P])
                        filled(ins, ("kdT", t))
                if u in (SLOT_UPD, SLOT_UPD + 1):
                    for c in (range(4) if u == SLOT_UPD else range(4, NCHUNK - 1)):
                        t, rows = c // 2, slice(64 * (c % 2), 64 * (c % 2) + 64)
                        evacuated(pe, ("kdT", t))
                        b = claim(pe, ("upd", c))
                        for h in range(HEADS):
                            ins = mm(b[:, h * P:(h + 1) * P], kd[rows, t, h * P:(h + 1) * P], hv[rows, t, h * P:(h + 1) * P])
                        filled(ins, ("upd", c))
                if u == SLOT_O:
                    pe.wait_ge(odd_done, 1)
                    for c in range(NCHUNK - 1):
                        evacuated(pe, ("upd", c))
                    for h in range(HEADS):
                        evacuated(pe, ("lev", LEVELS - 1, h))
                    for h in range(HEADS):
                        b = claim(pe, ("o", h))
                        for t in range(TT):
                            tok = slice(t * P, (t + 1) * P)
                            mm(b[:, tok], hv[:, t, h * P:(h + 1) * P], scT[:, h, tok], start=t == 0, stop=False,
                               skip_group_check=True)
                        for c in range(1, NCHUNK):
                            st = st_a[:, c - 1, :] if c < 5 else st_b[:, c - 5, :]
                            tok = slice(c // 2 * P, c // 2 * P + P)
                            ins = mm(b[:, tok], st[:, h * P:(h + 1) * P], (zz[0], q_odd)[c % 2][:, h, tok], start=False,
                                     stop=c == NCHUNK - 1, skip_group_check=True)
                        filled(ins, ("o", h))
                if u == SLOT_SS:
                    for h in range(HEADS):
                        pe.wait_ge(osq_done, h + 1)
                        b = claim(pe, ("ss", h))
                        filled(mm(b[:, :], ones[:, :], o_sq[:, h, :]), ("ss", h))
                for p in range(PAIRS):
                    s = U_PAIR + 3 * p + 2
                    if u == s:
                        for t in range(2):
                            evacuated(pe, ("g", s - 2, t))
                            evacuated(pe, ("g", s - 1, t))
                        scores(p)
                    if u == s + 1:
                        for hh in range(2):
                            pe.wait_ge(prob_done, 2 * p + hh + 1)
                            bb = [claim(pe, ("T", p, hh, j)) for j in range(score_banks(p))]
                            n_blocks = len(blocks_of(p))
                            for n in range(n_blocks):
                                j, col = block_bank(p, n)
                                ins = transpose(bb[j][:, col:col + P], prob[:, hh, n * P:(n + 1) * P])
                                if n == n_blocks - 1 or block_bank(p, n + 1)[0] != j:
                                    filled(ins, ("T", p, hh, j))
                    if u == s + 2:
                        for t in range(4):
                            evacuated(pe, ("g", s, t))
                        for hh in range(2):
                            b = claim(pe, ("O", p, hh))
                            for j in range(score_banks(p)):
                                evacuated(pe, ("T", p, hh, j))
                            blocks = blocks_of(p)
                            for n, (q, k) in enumerate(blocks):
                                first = n == 0 or blocks[n - 1][0] != q
                                last = n == len(blocks) - 1 or blocks[n + 1][0] != q
                                ins = mm(b[:, q * P:(q + 1) * P], va[:, k, hh * P:(hh + 1) * P],
                                         probT[:, hh, n * P:(n + 1) * P], first, last)
                            filled(ins, ("O", p, hh))
                if u in (SLOT_STAT, SLOT_STAT + 1):
                    name, src = (("mT", nmax), ("sT", ssum))[u - SLOT_STAT]
                    for g in range(NG):
                        b = claim(pe, (name, g))
                        for q in range(TT):
                            col = (g * TT + q) * HEADS
                            ins = transpose(b[0:HEADS, q * P:(q + 1) * P], src[:, col:col + HEADS])
                        filled(ins, (name, g))
                if SLOT_BC <= u < SLOT_BC + HEADS:
                    h = u - SLOT_BC
                    pe.wait_ge(crow_done, 1)
                    pe.wait_ge(pick_done, 1)
                    for g in range(NG):
                        b = claim(pe, ("bc", h, g))
                        rows = pick[:, h:h + 1].broadcast_to([HEADS, P])
                        mm(b[:, :], rows, wg_hi[:, g, :], stop=False)
                        filled(mm(b[:, :], rows, wg_lo[:, g, :], start=False), ("bc", h, g))
                if u in (SLOT_ROW, SLOT_ROW + 1):
                    w = u - SLOT_ROW
                    pe.wait_ge(gp_done, 1)
                    for i in range(2):
                        b = claim(pe, ("row", w, i))
                        for k in range(4):
                            n = 8 * w + 4 * i + k
                            ins = transpose(b[:, k * P:(k + 1) * P], gp[:, n:n + 1].broadcast_to([P, P]))
                        filled(ins, ("row", w, i))
                if u in MOD_UNITS:
                    b = claim(pe, ("mod2", u))
                    for i, n in enumerate(MOD_UNITS[u]):
                        ins = modulation(b, 2 * i, n, part2[n % 4])
                    filled(ins, ("mod2", u))

            def growing_products(j, u):
                if j < KT // 2 - 1:
                    pe.wait_ge(lo_share, 2 * j + u + 1)
                else:
                    pe.wait_ge(lo_done, u + 1)
                parts = [w[u][:, :].rearrange("p (k c) -> p k c", c=256) for w in (whi, wlo)]
                for t in range(2):
                    b = claim(pe, ("g", u, t)) if j == 0 else bank[BANKS["g", u, t][0]]
                    for k in (2 * j, 2 * j + 1):
                        if t == 0:
                            pe.wait_ge(h_lo_done[k % 2], k // 2 + 1)
                        ins = three_passes(b[:, :], [w[:, k, t * P:(t + 1) * P] for w in parts],
                                           [a[:, k, :] for a in (h_hi, h_lo)], k, KT - 1, skip=True)
                    if j == KT // 2 - 1:
                        filled(ins, ("g", u, t))

            for k in range(2):
                transposed_x(k)
            for j in range(KT // 2):
                b = claim(pe, ("mod1", j))
                for i in range(2):
                    n = 2 * j + i
                    ins = modulation(b, 2 * i, n, part[:, n % 4, :])
                filled(ins, ("mod1", j))
                if j:
                    growing_products(j - 1, 0)
                    growing_products(j - 1, 1)
                if j < KT // 2 - 1:
                    for k in (2 * j + 2, 2 * j + 3):
                        transposed_x(k)
            growing_products(KT // 2 - 1, 0)
            growing_products(KT // 2 - 1, 1)
            for u in range(U_UP):
                if u >= 2:
                    products(u)
                small(u)

            for t in range(TT):
                pe.wait_ge(xn_done[t // 2], TT // 2 + t % 2 + 1)
                for k in (3, 4, 5, 6, 7, 0, 1, 2) if t == 0 else range(KT):
                    b = claim(pe, ("xT", 1, k)) if t == 0 else bank[BANKS["xT", 1, k][0]]
                    if t == TT - 1 and k == KT // 2:
                        pe.wait_ge(xn_done[0], TT // 2 + 3)
                    ins = transpose(b[:, t * P:(t + 1) * P], xn_ffn[:, t, k * P:(k + 1) * P])
                    if t == TT - 1:
                        filled(ins, ("xT", 1, k))
            with pe.Fori(0, FT // 2) as i:
                for half, name in enumerate(("gate", "val")):
                    parts = unit_parts(2 * i + U_UP + half, half, 256)
                    two = [BANKS[f"{name}{t}"] for t in range(2)]
                    if name == "gate":
                        for bk, n in two:
                            pe.wait_ge(free[bk], i + n)
                        for k in range(KT):
                            pe.wait_ge(h_lo_done[k % 2], KT // 2 + k // 2 + 1)
                            for t, (bk, _) in enumerate(two):
                                ins = three_passes(bank[bk][:, :], [a[:, k, t * P:(t + 1) * P] for a in parts],
                                                   [a[:, k, :] for a in (h_hi, h_lo)], k, KT - 1, skip=True)
                                if k == KT - 1:
                                    ins.then_inc(full[bk], 1)
                        continue
                    for t, (bk, n) in enumerate(two):
                        pe.wait_ge(free[bk], i + n)
                        feature_tile(bank[bk][:, :], parts, t * P, (h_hi, h_lo)).then_inc(full[bk], 1)
            for i in range(FT // 2):
                u = U_DOWN + i
                parts = unit_parts(u, u % 2, 1024)
                pe.wait_ge(alo_done, 2 * i + 2)
                for t in range(TT):
                    tok = slice(t * P, (t + 1) * P)
                    for half in range(2):
                        if i == 0:
                            claim(pe, ("y", t, half))
                        for kk in range(2):
                            k = 2 * i + kk
                            ins = three_passes(bank[2 * t + half][:, :], [a[:, k, tok] for a in (act_hi, act_lo)],
                                               [w[:, kk, half * 512:half * 512 + 512] for w in parts], k, FT - 1)
                        if i == FT // 2 - 1:
                            filled(ins, ("y", t, half))
                if i < FT // 2 - 1:
                    ins.then_inc(down_used, 1)

        @block.vector
        def _(dve):
            n_chain = [0]

            def link(ins):
                n_chain[0] += 1
                ins.then_inc(dchain, 1)
                dve.wait_ge(dchain, n_chain[0])

            tt, ts, stt = dve.tensor_tensor, dve.tensor_scalar, dve.scalar_tensor_tensor

            b = ready(dve, "cT")
            dve.wait_ge(csig_done, 1)
            ins = tt(csilu[:, :], csig[:, :], b[:, 0:KT], ALU.mult)
            release(ins, "cT")
            evacuated(dve, "cT")

            n_part = [0, 0]

            def partial_sums(unit, sums, kts=KT, rest=0):
                for k in range(kts):
                    dst = sums if k % 2 == 0 else unit[:, 1, :]
                    sc = csilu[:, k:k + 1]
                    if k >= 2:
                        dve.wait_ge(part_chain[k % 2], n_part[k % 2])
                        ins = stt(dst, unit[:, k, :], sc, dst, ALU.mult, ALU.add)
                    else:
                        ins = ts(dst, unit[:, k, :], sc, None, ALU.mult)
                    ins.then_inc(part_chain[k % 2], 1)
                    n_part[k % 2] += 1
                for i in range(2):
                    dve.wait_ge(part_chain[i], n_part[i])
                ins = tt(sums, sums, unit[:, 1, :], ALU.add)
                if rest:
                    link(ins)
                    dve.wait_ge(rest_done, rest)
                    ins = tt(sums, sums, unit[:, kts, :], ALU.add)
                ins.then_inc(part_done, 1)

            def low_h(which, k):
                dve.wait_ge(h_hi_done, which * KT + k + 1)
                tt(h_lo[:, k, :], h_part(which, k), h_hi[:, k, :].bitcast(F32), ALU.subtract).then_inc(h_lo_done[k % 2], 1)

            for j in range(KT // 2):
                for i in range(2):
                    n = j + i * KT // 2
                    dve.wait_ge(ada_in[n], 16)
                    if j >= 2:
                        ready(dve, ("mod1", j - 2))
                    partial_sums(ada[n], part[:, (2 * j + i) % 4, :], MOD_KTS, START_ADA.index(n) + 1)
                    if i == 0 and j:
                        low_h(0, 2 * j - 2)
                    elif i == 0:
                        dve.wait_ge(rstd_done, 1)
                        for t in range(TT // 2, TT):
                            dve.wait_ge(x_in_s[t], 16)
                            ts(xn_in[:, t, :], x_in[:, t, :], rstd[:, t:t + 1], None, ALU.mult).then_inc(xn_done[1], 1)
                if j == 0:
                    b = ready(dve, "vec")
                    link(dve.tensor_copy(vec[:, :], b[:, 0:N_VEC]))
                    release(dve.tensor_copy(convc[:, :], b[:, N_VEC:N_VEC + 88]), "vec")
                    tt(lbd[:, :], vec[:, LB:LB + 4], vec[:, LB + 4:LB + 8], ALU.subtract).then_inc(lbd_done, 1)
                b = ready(dve, ("mod1", j))
                cols, scales = slice(2 * j, 2 * j + 2), slice(KT + 2 * j, KT + 2 * j + 2)
                tt(mod[:, cols], b[:, 0:2], vec[:, B_ADA + 2 * j:B_ADA + 2 * j + 2], ALU.add)
                release(tt(mod[:, scales], b[:, 2:4], vec[:, B_ADA + KT + 2 * j:B_ADA + KT + 2 * j + 2], ALU.add), ("mod1", j))
                evacuated(dve, ("mod1", j))
                stt(a1[:, cols], mod[:, scales], 1.0, vec[:, G_MIX + 2 * j:G_MIX + 2 * j + 2], ALU.add,
                    ALU.mult).then_inc(mod1_done, 1)
            low_h(0, KT - 2)
            dve.wait_ge(lb_done, 1)
            link(ts(oml[:, :], lb[:, :], -1.0, 1.0, ALU.mult, ALU.add))

            def make_h():
                for k in range(KT):
                    b = ready(dve, ("xT", 1, k))
                    if k >= 5 and k % 2:
                        dve.wait_ge(h_lo_done[1], KT // 2 + (k - 4) // 2 + 1)
                    release(ts(h_part(1, k), b[:, :], a2[:, k:k + 1], mod[:, 24 + k:25 + k], ALU.mult, ALU.add),
                            ("xT", 1, k))
                    if k % 2:
                        low_h(1, k - 1)
                    if k == 1:
                        low_h(1, 1)

            def small_results(u):
                if u == SLOT_DIAG:
                    dve.wait_ge(consts, 2)
                    link(ts(dint[:, :], dint[:, :], 3, None, ALU.bitwise_and))
                    link(ts(dist2[:, :], dint[:, :], FAR, None, ALU.mult))
                    tt(dist2[:, :], dist2[:, :], dist1[:, :], ALU.add)
                if u == 0:
                    dve.memset(scT[:, :, :], 0.0)
                if u - 1 in MOD_UNITS:
                    units = MOD_UNITS[u - 1]
                    b = ready(dve, ("mod2", u - 1))
                    cols = slice(2 * units[0], 2 * units[-1] + 2)
                    release(tt(mod[:, cols], b[:, 0:2 * len(units)], vec[:, cols], ALU.add), ("mod2", u - 1))
                if u == max(MOD_UNITS) + 1:
                    for v in MOD_UNITS:
                        evacuated(dve, ("mod2", v))
                    stt(a2[:, :], mod[:, 32:40], 1.0, vec[:, G_FFN:G_FFN + 8], ALU.add, ALU.mult)
                    link(ts(gp[:, 0:8], mod[:, 16:24], 1.0, None, ALU.add))
                    ts(gp[:, 8:16], mod[:, 40:48], 1.0, None, ALU.add).then_inc(gp_done, 1)
                if u == SLOT_DIAG + 1:
                    for h in range(HEADS):
                        b = ready(dve, ("diag", h))
                        release(dve.copy_predicated(scT[:, h, :], diag[:, :], b[:, :]), ("diag", h))
                if SLOT_LEVEL < u <= SLOT_LEVEL + LEVELS:
                    level_scores(u - SLOT_LEVEL - 1)
                if SLOT_LEVEL <= u < SLOT_LEVEL + LEVELS:
                    level_factors(u - SLOT_LEVEL)
                if u == SLOT_KDT:
                    dve.wait_ge(eg_done, 1)
                    link(tt(zz[0][:, :, :], hq[:, :, :], dec[:, :, :], ALU.mult))
                    pc = hp[:, :, :].rearrange("p h (c t) -> p (h c) t", t=CHUNK)
                    dc = dec[:, :, :].rearrange("p h (c t) -> p (h c) t", t=CHUNK)
                    tt(dc, pc[:, :, CHUNK - 1:CHUNK].broadcast_to([P, HEADS * NCHUNK, CHUNK]), pc, ALU.subtract).then_inc(kdif_done, 1)
                    dve.wait_ge(ke_done, 1)
                    tt(zz[1][:, :, :], hk[:, :, :], dec[:, :, :], ALU.mult).then_inc(kdec_done, 1)
                if u == SLOT_KDT + 1:
                    dve.wait_ge(kdec_done, 1)
                    for t in range(TT - 1):
                        b = ready(dve, ("kdT", t))
                        release(dve.tensor_copy(kd[:, t, :], b[:, :]), ("kdT", t))
                if u == SLOT_UPD + 1:
                    ready(dve, ("kdT", TT - 1))
                    z_even, z_odd = (a[:, :, :].rearrange("p h (t two c) -> p (h t) two c", two=2, c=CHUNK)
                                     for a in (zz[0], q_odd))
                    dve.memset(z_odd[:, :, 0, :], 0.0)
                    link(dve.tensor_copy(z_odd[:, :, 1, :], z_even[:, :, 1, :]))
                    dve.memset(z_even[:, :, 1, :], 0.0).then_inc(odd_done, 1)
                    states(range(4))
                if u == SLOT_UPD + 2:
                    states(range(4, NCHUNK - 1))
                if u == SLOT_O + 1:
                    for h in range(HEADS):
                        evacuated(dve, ("o", h))
                        tt(o_sq[:, h, :], o_sb[:, h, :], o_sb[:, h, :], ALU.mult).then_inc(osq_done, 1)
                for p in range(PAIRS):
                    s = U_PAIR + 3 * p + 2
                    if u == s + 1:
                        softmax_max(p)
                    if u == s + 2:
                        if p:
                            ready(dve, ("O", p - 1, 1))
                        for j in range(score_banks(p)):
                            b = ready(dve, ("T", p, 0, j))
                            n = sum(block_bank(p, i)[0] == j for i in range(len(blocks_of(p)))) * P
                            release(dve.tensor_copy(probT[:, 0, 3 * P * j:3 * P * j + n], b[:, 0:n]), ("T", p, 0, j))
                    if u == s + 3:
                        g, h0, d = pair(p)
                        b = ready(dve, ("O", p, 0))
                        release(dve.tensor_copy(og[:, g, h0, :].rearrange("p (l res) -> p res l", res=d),
                                             b[:, :].rearrange("p (res l) -> p res l", res=d)), ("O", p, 0))
                if u == SLOT_STAT + 2:
                    group_weights()
                if SLOT_BC < u <= SLOT_BC + HEADS:
                    merge_groups(u - SLOT_BC - 1)

            def level_scores(j):
                half = 1 << j
                m = masks[:, j, :].rearrange("p (blk tok) -> p blk tok", tok=half)
                dve.wait_ge(masks_done, j + 1)
                for h in range(HEADS):
                    b = ready(dve, ("lev", j, h))
                    second = [a.rearrange("p (blk pos tok) -> p blk pos tok", pos=2, tok=half)[:, :, 1, :]
                              for a in (scT[:, h, :], b[:, :])]
                    release(dve.copy_predicated(second[0], m, second[1]), ("lev", j, h))

            def level_factors(j):
                half = 1 << j
                if j == 0:
                    dve.wait_ge(logf_done, 1)
                else:
                    dve.wait_ge(p_done, j)
                v = {n: t[:, :, :].rearrange("p h (blk pos tok) -> p (h blk) pos tok", pos=2, tok=half)
                     for n, t in (("p", hp), ("d", dec), ("q", hq), ("k", hk), ("z", zz[j % 2]))}
                total = v["p"][:, :, 0, half - 1:half].broadcast_to([P, HEADS * S // (2 * half), half])
                tt(v["d"][:, :, 0, :], total, v["p"][:, :, 0, :], ALU.subtract).then_inc(d1_done, 1)
                dve.wait_ge(e_done, j + 1)
                tt(v["z"][:, :, 1, :], v["q"][:, :, 1, :], v["d"][:, :, 1, :], ALU.mult)
                tt(v["z"][:, :, 0, :], v["k"][:, :, 0, :], v["d"][:, :, 0, :], ALU.mult).then_inc(z_done, 1)
                tt(v["p"][:, :, 1, :], v["p"][:, :, 1, :], total, ALU.add).then_inc(p_done, 1)

            def states(chunks):
                for c in chunks:
                    b = ready(dve, ("upd", c))
                    dst = st_a[:, c, :] if c < 4 else st_b[:, c - 4, :]
                    if c == 0:
                        dve.wait_ge(glast_done, 1)
                        ins = dve.tensor_copy(dst, b[:, :])
                    else:
                        src = st_a[:, c - 1, :] if c < 5 else st_b[:, c - 5, :]
                        for h in range(HEADS):
                            cols = slice(h * P, (h + 1) * P)
                            n = h * NCHUNK + c
                            ins = stt(dst[:, cols], src[:, cols], eglast[:, n:n + 1], b[:, cols], ALU.mult, ALU.add)
                    release(ins, ("upd", c))
                    evacuated(dve, ("upd", c))

            def softmax_max(p):
                g, h0, d = pair(p)
                if p:
                    ready(dve, ("T", p - 1, 1, score_banks(p - 1) - 1))
                for hh in range(2):
                    slope = 2.0 ** (-8.0 * (g * HEADS + h0 + hh + 1) / (NG * HEADS))
                    k = -slope * d / SCALE
                    pr = prob[:, hh, :]
                    if g == 0:
                        b = ready(dve, ("S", p, hh, 0))
                        stt(pr[:, 0:P], dist0[:, P:2 * P], k, b[:, 0:P], ALU.mult, ALU.add)
                        release(stt(pr[:, P:3 * P], dist0[:, :], k, b[:, P:3 * P], ALU.mult, ALU.add), ("S", p, hh, 0))
                        b = ready(dve, ("S", p, hh, 1))
                        for i in range(2):
                            ins = stt(pr[:, (3 + 2 * i) * P:(5 + 2 * i) * P], dist0[:, :], k,
                                      b[:, 2 * i * P:(2 * i + 2) * P], ALU.mult, ALU.add)
                        release(ins, ("S", p, hh, 1))
                        evacuated(dve, ("S", p, hh, 1))
                        dve.tensor_reduce(mx[:, 4 * hh:4 * hh + 1], pr[:, 0:P], AX_X, ALU.max)
                        link(dve.tensor_reduce(mx[:, 4 * hh + 1:4 * hh + 4],
                                               pr[:, P:7 * P].rearrange("p (q k) -> p q k", q=3), AX_X, ALU.max))
                    else:
                        dist = dist1 if g == 1 else dist2
                        b = ready(dve, ("S", p, hh, 0))
                        for i in range(TT):
                            tok = slice(i * P, (i + 1) * P)
                            ins = stt(pr[:, tok], dist[:, :], k, b[:, tok], ALU.mult, ALU.add)
                        release(ins, ("S", p, hh, 0))
                        evacuated(dve, ("S", p, hh, 0))
                        link(dve.tensor_reduce(mx[:, 4 * hh:4 * hh + 4],
                                               pr[:, 0:4 * P].rearrange("p (q k) -> p q k", q=4), AX_X, ALU.max))
                    cols = slice(g * TT * HEADS + h0 + hh, (g + 1) * TT * HEADS, HEADS)
                    ts(nmax[:, cols], mx[:, 4 * hh:4 * hh + 4], -SCALE, None, ALU.mult).then_inc(nmax_done, 1)

            def group_weights():
                for g in range(NG):
                    evacuated(dve, ("mT", g))
                link(tt(inv[:, :], m_row[:, 0, :], m_row[:, 1, :], ALU.min))
                link(tt(inv[:, :], inv[:, :], m_row[:, 2, :], ALU.min))
                for g in range(NG):
                    ins = tt(m_row[:, g, :], inv[:, :], m_row[:, g, :], ALU.subtract)
                ins.then_inc(mdiff_done, 1)
                dve.wait_ge(wexp_done, 1)
                for g in range(NG):
                    evacuated(dve, ("sT", g))
                link(tt(s_row[:, :, :], s_row[:, :, :], m_row[:, :, :], ALU.mult))
                link(tt(inv[:, :], s_row[:, 0, :], s_row[:, 1, :], ALU.add))
                link(tt(inv[:, :], inv[:, :], s_row[:, 2, :], ALU.add))
                link(dve.reciprocal(inv[:, :], inv[:, :]))
                for g in range(NG):
                    ins = tt(m_row[:, g, :], m_row[:, g, :], inv[:, :], ALU.mult)
                link(ins)
                link(dve.tensor_copy(wg_hi[:, :, :], m_row[:, :, :]))
                tt(wg_lo[:, :, :], m_row[:, :, :], wg_hi[:, :, :].bitcast(F32), ALU.subtract).then_inc(crow_done, 1)

            def merge_groups(h):
                for g in range(NG):
                    b = ready(dve, ("bc", h, g))
                    release(tt(og[:, g, h, :], og[:, g, h, :], b[:, :], ALU.mult), ("bc", h, g))
                for g in range(NG):
                    evacuated(dve, ("bc", h, g))
                link(tt(og[:, 0, h, :], og[:, 0, h, :], og[:, 1, h, :], ALU.add))
                tt(og[:, 0, h, :], og[:, 0, h, :], og[:, 2, h, :], ALU.add).then_inc(ybfull_done, 1)
                dve.wait_ge(ybhi_done, h + 1)
                tt(yb_lo[:, h, :], og[:, 0, h, :], yb_hi[:, h, :].bitcast(F32), ALU.subtract).then_inc(yblo_done, 1)

            def evacuate(u):
                if u < U_HF:
                    for t in range(2):
                        h = 2 * u + t
                        dve.wait_ge(sig_done, h + 1)
                        b = ready(dve, ("g", u, t))
                        release(tt(hq[:, h, :], b[:, :], dec[:, h, :], ALU.mult), ("g", u, t))
                elif u < U_HI:
                    for t in range(2):
                        h = 2 * (u - U_HF) + t
                        evacuated(dve, ("g", u, t))
                        link(ts(hp[:, h, :], dec[:, h, :], oml[:, h:h + 1], lb[:, h:h + 1], ALU.mult, ALU.add))
                        ts(hk[:, h, :], hp[:, h, :], -1.0, 1.0, ALU.mult, ALU.add).then_inc(f_done, 1)
                elif u < U_PAIR:
                    for t in range(TT):
                        b = ready(dve, ("g", u, t))
                        c0 = 256 * (u - U_HI)
                        release(dve.tensor_copy(hv[:, t, c0:c0 + 256], b[:, 0:256]), ("g", u, t))
                elif u < U_HG:
                    p, what = divmod(u - U_PAIR, 3)
                    g, h0, d = pair(p)
                    if what == 1:
                        for t in range(2):
                            b = ready(dve, ("g", u, t))
                            release(dve.tensor_copy(ka[:, t, :].rearrange("p (res l) -> p res l", res=d),
                                                 b[:, :].rearrange("p (l res) -> p res l", res=d)), ("g", u, t))
                    if what == 2:
                        if p:
                            ready(dve, ("O", p - 1, 1))
                        for t in range(TT):
                            b = ready(dve, ("g", u, t))
                            release(dve.tensor_copy(va[:, t, :], b[:, 0:256]), ("g", u, t))
                elif u < U_GA:
                    for t in range(2):
                        h = 2 * (u - U_HG) + t
                        dve.wait_ge(sig_done, HEADS + h + 1)
                        b = ready(dve, ("g", u, t))
                        release(tt(sgt[:, h % 2, :], b[:, :], sgt[:, h % 2, :], ALU.mult), ("g", u, t))
                        evacuated(dve, ("g", u, t))
                        tt(yh[:, h, :], yh[:, h, :], sgt[:, h % 2, :], ALU.mult).then_inc(yfull_done, 1)
                    for t in range(2):
                        h = 2 * (u - U_HG) + t
                        dve.wait_ge(yahi_done, h + 1)
                        tt(ya_lo[:, h, :], yh[:, h, :], ya_hi[:, h, :].bitcast(F32), ALU.subtract).then_inc(yalo_done, 1)
                elif U_A <= u < U_B:
                    for t in range(4):
                        f = 4 * (u - U_A) + t
                        if t == 0 and u == U_A:
                            for v in range(U_GA, U_A):
                                for i in range(2):
                                    evacuated(dve, ("g", v, i))
                        b = ready(dve, ("g", u, t))
                        release(tt(sga[:, f, :], sga[:, f, :], b[:, :], ALU.mult), ("g", u, t))
                elif U_B <= u < U_OUT:
                    for t in range(4):
                        f = 4 * (u - U_B) + t
                        b = ready(dve, ("g", u, t))
                        release(tt(sgb[:, f, :], sgb[:, f, :], b[:, :], ALU.mult), ("g", u, t))
                        evacuated(dve, ("g", u, t))
                        tt(sgb[:, f, :], sgb[:, f, :], sga[:, f, :], ALU.add).then_inc(mfull_done, 1)
                        dve.wait_ge(mhi_done, f + 1)
                        tt(m_lo[:, f, :], sgb[:, f, :], m_hi[:, f, :].bitcast(F32), ALU.subtract).then_inc(mlo_done, 1)
                elif u >= U_OUT:
                    if u == U_OUT:
                        dve.wait_ge(x_again, 16)
                        for i in range(2):
                            evacuated(dve, ("row", 0, i))
                    c0 = 256 * (u - U_OUT)
                    cols = slice(c0, c0 + 256)
                    for t in range(TT):
                        b = ready(dve, ("g", u, t))
                        tmp = sgb[:, t, 0:256]
                        release(tt(tmp, b[:, 0:256], g1_row[:, cols], ALU.mult), ("g", u, t))
                        evacuated(dve, ("g", u, t))
                        tt(x1[:, t, cols], x1[:, t, cols], tmp, ALU.add).then_inc(x1_done, 1)
                        if u == U_UP - 1 and t:
                            sum_of_squares(t - 1)

            def sum_of_squares(t):
                dve.wait_ge(ssp_done, 3 * TT + t + 1)
                dve.tensor_reduce(ssq[:, TT + t:TT + t + 1], ssp[:, 4 * t:4 * t + 4], AX_X, ALU.add).then_inc(ssq_done, 1)

            for u in range(U_UP):
                small_results(u)
                for n in MOD_UNITS.get(u, ()):
                    dve.wait_ge(ada2_in[n % 2], 16 * ((n - MOD_FIRST) // 2 + 1))
                    if n >= MOD_FIRST + 4:
                        ready(dve, ("mod2", max(v for v in MOD_UNITS if MOD_UNITS[v][0] <= n - 4)))
                    partial_sums(ada2[n % 2], part2[n % 4][:, :])
                evacuate(u)
                if u == SLOT_SS + 1:
                    for h in range(HEADS):
                        dve.wait_ge(rs_done, h + 1)
                        stt(yh[:, h, :], o_sb[:, h, :], vec[:, G_HG + h:G_HG + h + 1], o_rs[:, h, :], ALU.mult, ALU.mult)

            def xn_again(t, cols):
                dve.wait_ge(rstd_done, 2 + t)
                ts(xn_ffn[:, t, cols], x1[:, t, cols], rstd[:, TT + t:TT + t + 1], None, ALU.mult).then_inc(xn_done[1], 1)

            sum_of_squares(TT - 1)
            xn_again(2, slice(0, D))
            xn_again(3, slice(0, 512))
            make_h()

            CW = convc[:, :]
            with dve.Fori(0, FT // 2) as i:
                for t in range(2):
                    dve.wait_ge(conv0_done, 2 * i + t + 1)
                    tt_ = conv[:, t, 1:S]
                    stt(tt_, bank[t][:, 0:S - 1], CW[:, bass.ds(2 * i + (FT + t), 1)], tt_, ALU.mult,
                        ALU.add).then_inc(tap_done, 1)
                    dve.wait_ge(tap_done, 2 * i + t + 1)
                    tt_ = conv[:, t, 2:S]
                    stt(tt_, bank[t][:, 0:S - 2], CW[:, bass.ds(2 * i + t, 1)], tt_, ALU.mult,
                        ALU.add).then_inc(free[t], 1)
                for t in range(2):
                    bk, n = BANKS[f"val{t}"]
                    dve.wait_ge(full[bk], i + (n + 1))
                    dve.wait_ge(gelu_done, 2 * i + t + 1)
                    tt(gelu[:, t, :], gelu[:, t, :], bank[bk][:, :], ALU.mult).then_inc(free[bk], 1)
                for t in range(2):
                    dve.wait_ge(ahi_done, 2 * i + t + 1)
                    hi = act_hi[:, bass.ds(2 * i + t, 1), :].rearrange("p a s -> p (a s)")
                    lo = act_lo[:, bass.ds(2 * i + t, 1), :].rearrange("p a s -> p (a s)")
                    tt(lo, gelu[:, t, :], hi.bitcast(F32), ALU.subtract).then_inc(alo_done, 1)

            dve.wait_ge(gf_in, 16)
            for i in range(2):
                evacuated(dve, ("row", 1, i))
            for t in range(TT):
                for half in range(2):
                    cols = slice(512 * half, 512 * half + 512)
                    b = ready(dve, ("y", t, half))
                    link(tt(gelu[:, half, :], b[:, :], g2_row[:, cols], ALU.mult))
                    tt(x1[:, t, cols], x1[:, t, cols], gelu[:, half, :], ALU.add).then_inc(x2_done, 1)
            dve.wait_ge(x2_done, 2 * TT)
            tt(xg[:, TT - 1, :], x1[:, TT - 1, :], gf_row[:, :], ALU.mult).then_inc(xg_last, 1)
            t = TT - 2
            dve.wait_ge(rstd_done, 2 + TT + t)
            stt(x1[:, t, :], x1[:, t, :], rstd[:, 2 * TT + t:2 * TT + t + 1], gf_row[:, :], ALU.mult,
                ALU.mult).then_inc(y_last[0], 1)


_INS = ["x", "c", "w_ada", "b_ada", "g_norm_mix", "w_in", "lb_logits", "g_hg_norm", "w_branch_a", "w_branch_b",
        "w_out", "g_norm_ffn", "w_up", "conv_w", "conv_b", "w_down", "g_final"]
_OUT = ((1, 512, 1024), "float32")


def kernel(**inputs):
    import concourse.bacc as _bacc
    from concourse.bass_utils import run_bass_kernel_spmd as _run

    nc = _bacc.Bacc("TRN2", target_bir_lowering=False, num_devices=1)
    arrays, args = {}, []
    for name in _INS:
        a = np.ascontiguousarray(inputs[name])
        arrays[f"in_{name}_dram"] = a
        args.append(nc.dram_tensor(f"in_{name}_dram", a.shape, mybir.dt.from_np(a.dtype), kind="ExternalInput").ap())
    shape, dtype = _OUT
    args.append(nc.dram_tensor("out_dram", shape, mybir.dt.from_np(np.dtype(dtype)), kind="ExternalOutput").ap())
    layer_kernel(nc, *args)
    r = _run(nc, [arrays], core_ids=[0])
    return r.results[0]["out_dram"]
```
